# Optimizing a Trainium2 kernel written in Bass

```python
import math
import jax, jax.numpy as jnp
from jax import lax
import numpy as np

D_MODEL = 1024
BATCH = 1
SEQ = 1024
DEPTH = 1
DEC_BATCH = 1
DEC_SEQ = 256
PAST_LEN = 128

ATTN_WIDTH = D_MODEL // 2
RWKV_WIDTH = D_MODEL - ATTN_WIDTH
ATTN_HEADS = 4
ATTN_QK_DIM = ATTN_WIDTH // (2 * ATTN_HEADS)
ATTN_V_DIM = 2 * ATTN_QK_DIM
RWKV_HEAD = 64
RWKV_HEADS = RWKV_WIDTH // RWKV_HEAD
DECAY_LORA = 32
AAA_LORA = 32
GATE_LORA = 96
ATTN_COLS = 3 * ATTN_WIDTH
RWKV_COLS = 3 * RWKV_WIDTH + 2 * DECAY_LORA + 2 * AAA_LORA + GATE_LORA
IN_COLS = ATTN_COLS + RWKV_COLS
RWKV_SPLITS = tuple(int(s) for s in np.cumsum([RWKV_WIDTH] * 3 + [DECAY_LORA] * 2 + [AAA_LORA] * 2 + [GATE_LORA])[:-1])
N_EXPERTS = 16
EXPERT_FF = 2 * D_MODEL
CAPACITY_FACTOR = 2
Q_BLOCK = 128
NORM_EPS = 1e-6
GN_EPS = 64e-5

kernel_name = 'hybrid_diffattn_rwkv7_ec_encoder'

def rmsnorm(x, g):
    xf = x.astype(jnp.float32)
    y = xf * lax.rsqrt(jnp.mean(xf * xf, axis=-1, keepdims=True) + NORM_EPS) * g.astype(jnp.float32)
    return y.astype(x.dtype)

def diff_attention(q, k, v, lam, subln_g, lambda_init):
    B, T = q.shape[0], q.shape[1]
    nb = T // Q_BLOCK
    slopes = 2.0 ** (-8.0 * jnp.arange(1, ATTN_HEADS + 1, dtype=jnp.float32) / ATTN_HEADS)
    kpos = jnp.arange(T, dtype=jnp.float32)
    scale = ATTN_QK_DIM ** -0.5
    qb = q.reshape(B, nb, Q_BLOCK, ATTN_HEADS, 2, ATTN_QK_DIM).transpose(1, 0, 2, 3, 4, 5)

    def block(args):
        q_blk, i = args
        s = jnp.einsum('bqhmd,bkhmd->bhmqk', q_blk, k).astype(jnp.float32) * scale
        qpos = (i * Q_BLOCK + jnp.arange(Q_BLOCK)).astype(jnp.float32)
        bias = -slopes[:, None, None] * jnp.abs(qpos[:, None] - kpos[None, :])
        p = jax.nn.softmax(s + bias[None, :, None], axis=-1)
        pd = (p[:, :, 0] - lam * p[:, :, 1]).astype(v.dtype)
        return jnp.einsum('bhqk,bkhe->bqhe', pd, v)

    o = lax.map(block, (qb, jnp.arange(nb)))
    o = o.transpose(1, 0, 2, 3, 4).reshape(B, T, ATTN_HEADS, ATTN_V_DIM)
    o = rmsnorm(o, subln_g) * (1.0 - lambda_init)
    return o.reshape(B, T, ATTN_WIDTH)

def wkv7_scan(r, w, k, v, a, b, reverse):
    B, T, H, N = r.shape
    tm = lambda z: jnp.swapaxes(z.astype(jnp.float32), 0, 1)

    def step(S, inp):
        r_t, w_t, k_t, v_t, a_t, b_t = inp
        Sa = jnp.einsum('bhij,bhj->bhi', S, a_t)
        S = S * w_t[:, :, None, :] + Sa[..., None] * b_t[:, :, None, :] + v_t[..., None] * k_t[:, :, None, :]
        y = jnp.einsum('bhij,bhj->bhi', S, r_t)
        return S, y

    S0 = jnp.zeros((B, H, N, N), jnp.float32)
    _, y = lax.scan(step, S0, (tm(r), tm(w), tm(k), tm(v), tm(a), tm(b)), reverse=reverse)
    return jnp.swapaxes(y, 0, 1)

def rwkv7_mix(z, mu, w0, w2, a0, a2, g2, k_k, k_a, r_k, lnx_w, lnx_b):
    B, T, _ = z.shape
    prev = jnp.pad(z, ((0, 0), (1, 0), (0, 0)))[:, :-1]
    nxt = jnp.pad(z, ((0, 0), (0, 1), (0, 0)))[:, 1:]
    z = z + mu[0] * (prev - z) + mu[1] * (nxt - z)
    r, k, v, xw_f, xw_b, xa_f, xa_b, xg = jnp.split(z, RWKV_SPLITS, axis=-1)
    hd = lambda t: t.reshape(B, T, RWKV_HEADS, RWKV_HEAD)
    kk = hd(k * k_k).astype(jnp.float32)
    kk = kk / jnp.maximum(jnp.sqrt(jnp.sum(kk * kk, axis=-1, keepdims=True)), 1e-12)
    ys = []
    for d, (xw, xa, rev) in enumerate(((xw_f, xa_f, False), (xw_b, xa_b, True))):
        wlog = -jax.nn.softplus(-(w0[d] + jnp.tanh(xw) @ w2[d])) - 0.5
        decay = jnp.exp(-jnp.exp(wlog.astype(jnp.float32)))
        iclr = jax.nn.sigmoid(a0[d] + xa @ a2[d])
        kd = k * (1.0 + (iclr - 1.0) * k_a)
        ys.append(wkv7_scan(hd(r), hd(decay), hd(kd), hd(v), -kk, kk * hd(iclr).astype(jnp.float32), rev))
    y = ys[0] + ys[1]
    mean = jnp.mean(y, axis=-1, keepdims=True)
    var = jnp.mean((y - mean) ** 2, axis=-1, keepdims=True)
    y = ((y - mean) * lax.rsqrt(var + GN_EPS)).reshape(B, T, RWKV_WIDTH) * lnx_w.astype(jnp.float32) + lnx_b.astype(jnp.float32)
    bonus = (jnp.sum(hd(r) * hd(k) * r_k, axis=-1, keepdims=True) * hd(v)).reshape(B, T, RWKV_WIDTH)
    g = jax.nn.sigmoid(xg) @ g2
    return ((y + bonus.astype(jnp.float32)) * g.astype(jnp.float32)).astype(z.dtype)

def expert_choice_ffn(h, w_router, w_gate, w_up, w_down):
    shp = h.shape
    x = h.reshape(-1, D_MODEL)
    n = x.shape[0]
    cap = CAPACITY_FACTOR * n // N_EXPERTS
    aff = jax.nn.softmax((x @ w_router).astype(jnp.float32), axis=-1)
    gates, idx = lax.top_k(aff.T, cap)
    xe = x[idx]

    def expert(args):
        xs, wg, wu, wd = args
        return (jax.nn.silu(xs @ wg) * (xs @ wu)) @ wd

    ye = lax.map(expert, (xe, w_gate, w_up, w_down))
    contrib = (gates[..., None].astype(ye.dtype) * ye).reshape(-1, D_MODEL)
    y = jnp.zeros_like(x).at[idx.reshape(-1)].add(contrib)
    return y.reshape(shp)

def trunk(x, norm1_g, w_in, lambda_qk, subln_g, shift_mu, w0, w2, a0, a2, g2, k_k, k_a, r_k,
          lnx_w, lnx_b, w_out, norm2_g, w_router, w_gate, w_up, w_down, final_g):
    B, T, _ = x.shape
    for l in range(DEPTH):
        lambda_init = 0.8 - 0.6 * math.exp(-0.3 * l)
        h = rmsnorm(x, norm1_g[l])
        zin = h @ w_in[l]
        za, zr = zin[..., :ATTN_COLS], zin[..., ATTN_COLS:]
        q, k, v = jnp.split(za, 3, axis=-1)
        q = q.reshape(B, T, ATTN_HEADS, 2, ATTN_QK_DIM)
        k = k.reshape(B, T, ATTN_HEADS, 2, ATTN_QK_DIM)
        v = v.reshape(B, T, ATTN_HEADS, ATTN_V_DIM)
        lq = lambda_qk[l].astype(jnp.float32)
        lam = jnp.exp(jnp.sum(lq[0] * lq[1])) - jnp.exp(jnp.sum(lq[2] * lq[3])) + lambda_init
        oa = diff_attention(q, k, v, lam, subln_g[l], lambda_init)
        orw = rwkv7_mix(zr, shift_mu[l], w0[l], w2[l], a0[l], a2[l], g2[l], k_k[l], k_a[l], r_k[l], lnx_w[l], lnx_b[l])
        x = x + jnp.concatenate([oa, orw], axis=-1) @ w_out[l]
        x = x + expert_choice_ffn(rmsnorm(x, norm2_g[l]), w_router[l], w_gate[l], w_up[l], w_down[l])
    return rmsnorm(x, final_g)

def setup_inputs(seed: int = 0) -> dict:
    key = jax.random.key(seed)
    ks = jax.random.split(key, 32)
    nrm = lambda i, shape, s: jax.random.normal(ks[i], shape, jnp.float32) * s
    L = DEPTH
    return {
        'x_prompt': nrm(0, (BATCH, SEQ, D_MODEL), 1.0),
        'x_sample': nrm(1, (DEC_BATCH, DEC_SEQ, D_MODEL), 1.0),
        'norm1_g': 1.0 + nrm(2, (L, D_MODEL), 0.02),
        'w_in': nrm(3, (L, D_MODEL, IN_COLS), D_MODEL ** -0.5),
        'lambda_qk': nrm(4, (L, 4, ATTN_QK_DIM), 0.1),
        'subln_g': 1.0 + nrm(5, (L, ATTN_V_DIM), 0.02),
        'shift_mu': jax.random.uniform(ks[6], (L, 2, RWKV_COLS), jnp.float32, 0.0, 0.5),
        'w0': jax.random.uniform(ks[7], (L, 2, RWKV_WIDTH), jnp.float32, -6.0, -0.5),
        'w2': nrm(8, (L, 2, DECAY_LORA, RWKV_WIDTH), 0.1 * DECAY_LORA ** -0.5),
        'a0': nrm(9, (L, 2, RWKV_WIDTH), 0.1),
        'a2': nrm(10, (L, 2, AAA_LORA, RWKV_WIDTH), 0.1 * AAA_LORA ** -0.5),
        'g2': nrm(11, (L, GATE_LORA, RWKV_WIDTH), GATE_LORA ** -0.5),
        'k_k': 0.85 + nrm(12, (L, RWKV_WIDTH), 0.02),
        'k_a': 1.0 + nrm(13, (L, RWKV_WIDTH), 0.02),
        'r_k': nrm(14, (L, RWKV_HEADS, RWKV_HEAD), 0.1),
        'lnx_w': 1.0 + nrm(15, (L, RWKV_WIDTH), 0.02),
        'lnx_b': nrm(16, (L, RWKV_WIDTH), 0.02),
        'w_out': nrm(17, (L, D_MODEL, D_MODEL), D_MODEL ** -0.5),
        'norm2_g': 1.0 + nrm(18, (L, D_MODEL), 0.02),
        'w_router': nrm(19, (L, D_MODEL, N_EXPERTS), D_MODEL ** -0.5),
        'w_gate': nrm(20, (L, N_EXPERTS, D_MODEL, EXPERT_FF), D_MODEL ** -0.5),
        'w_up': nrm(21, (L, N_EXPERTS, D_MODEL, EXPERT_FF), D_MODEL ** -0.5),
        'w_down': nrm(22, (L, N_EXPERTS, EXPERT_FF, D_MODEL), EXPERT_FF ** -0.5),
        'final_g': 1.0 + nrm(23, (D_MODEL,), 0.02),
    }

def reference(x_prompt, x_sample, norm1_g, w_in, lambda_qk, subln_g, shift_mu, w0, w2, a0, a2, g2, k_k, k_a, r_k,
              lnx_w, lnx_b, w_out, norm2_g, w_router, w_gate, w_up, w_down, final_g):
    weights = (norm1_g, w_in, lambda_qk, subln_g, shift_mu, w0, w2, a0, a2, g2, k_k, k_a, r_k,
               lnx_w, lnx_b, w_out, norm2_g, w_router, w_gate, w_up, w_down, final_g)
    y_prompt = trunk(x_prompt, *weights)
    y_sample = trunk(x_sample, *weights)
    return (y_prompt, y_sample)


_drawn_inputs = setup_inputs


def setup_inputs(seed=0):
    import zlib

    import numpy as np

    out = dict(_drawn_inputs(seed))
    spreads = {}
    factors = {'lambda_qk': 5.417,
     'subln_g': 3.793,
     'w2': 8.0,
     'a0': 3.12,
     'a2': 3.612,
     'k_k': 5.205,
     'k_a': 4.886,
     'lnx_w': 4.621,
     'lnx_b': 7.245,
     'norm2_g': 4.31,
     'final_g': 2.903}
    for name, (base, spread) in spreads.items():
        noise = np.random.default_rng([zlib.crc32(name.encode()), seed]).standard_normal(out[name].shape)
        drawn = base * np.exp(spread * noise) if base else spread * noise
        out[name] = __import__('jax').numpy.asarray(drawn.astype(out[name].dtype))
    for name, factor in factors.items():
        out[name] = (out[name] * factor).astype(out[name].dtype)
    return out
```

```python
import math
from contextlib import ExitStack

import concourse.bass as bass
from concourse import mybir
import numpy as np

P = 128
D = 1024
KD = D // P
T0, T1 = 1024, 256
NT = T0 + T1
NTT = NT // P
HEADS_A = 4
AW = 512
RW = 512
RT = RW // P
LORA = 128
GATE = 96
IN_COLS = 3 * AW + 3 * RW + LORA + GATE
ZT = 3 * RT + 2
C = 64
NE = 16
FF = 2048
CAP0, CAP1 = 2 * T0 // NE, 2 * T1 // NE
SLOTS = CAP0 + CAP1
LAMBDA_INIT = 0.8 - 0.6 * math.exp(-0.3 * 0)
NORM_EPS, GN_EPS = 1e-6, 64e-5
DECAY = -math.exp(-0.5)
LEVELS = (1, 2, 4, 8, 16, 32)

CHUNKS = ((0, 512), (512, 512), (1024, 256))

F_R, F_K, F_V, F_KK, F_SIG, F_IC, F_BONUS, F_GATE = 0, 4, 8, 12, 16, 24, 32, 36
N_FEAT = 40

P_MU = 0
P_W0 = P_MU + 2 * ZT
P_A0 = P_W0 + 2 * RT
P_KK = P_A0 + 2 * RT
P_KA = P_KK + RT
P_RK = P_KA + RT
P_LW = P_RK + RT
P_LB = P_LW + RT
N_PAR = P_LB + RT

BIAS_W = T0 + T0 - P


def build(nc, tokens, gains, sub_g, w_in, lam_qk, par, w2, a2, g2, w_out, w_router,
          w_gate, w_up, w_down, c_bias, c_mask, out):
    F32 = mybir.dt.float32
    U32 = mybir.dt.uint32
    ALU = mybir.AluOpType
    ACT = mybir.ActivationFunctionType
    AX = mybir.AxisListType.X
    ds = bass.ds

    feat = nc.dram_tensor("feat", (N_FEAT, P, NT), F32).ap()
    resid = nc.dram_tensor("resid", (NT, D), F32).ap()
    h2 = nc.dram_tensor("h2", (NT, D), F32).ap()

    with ExitStack() as ctx:
        def sb(name, shape, dt=F32):
            return ctx.enter_context(nc.sbuf_tensor(name, shape, dt))

        ident = sb("ident", [P, P])
        onesbd = sb("onesbd", [P, P])
        causal = sb("causal", [P, 2, 2 * P])
        lvl = sb("lvl", [P, 2, len(LEVELS), P])
        pars = sb("pars", [P, N_PAR])
        muc = sb("muc", [P, ZT])
        cst = sb("cst", [P, 4])
        small = sb("small", [P, 64])
        subg = sb("subg", [P, P])
        restart = sb("restart", [P, RT * C])
        g2s = sb("g2s", [GATE, RW])
        lamr = sb("lamr", [P, 384])
        arena = sb("arena", [P, 48140])

        def at(off, *dims):
            n = int(np.prod(dims))
            v = arena[:, off:off + n]
            if len(dims) == 1:
                return v
            if len(dims) == 2:
                return v.rearrange("p (a b) -> p a b", b=dims[1])
            if len(dims) == 3:
                return v.rearrange("p (a b c) -> p a b c", b=dims[1], c=dims[2])
            return v.rearrange("p (a b c d) -> p a b c d", b=dims[1], c=dims[2], d=dims[3])

        A_, B_, C_, D_ = 0, 10240, 20480, 25600
        E_ = D_ + ZT * NT
        hT = at(A_, KD, NT)
        qk = at(B_, KD, NT)
        vt = at(C_, NTT, AW)
        zt = at(D_, ZT, NT)
        wb = at(E_, 2, KD, P)
        zpad = at(E_ + 2 * KD * P, 2, NT + 3)
        loraw = at(E_, 4 * RW)
        xt = at(D_, 2, D)
        hb = at(D_ + 2 * D, 2, D)
        junk = at(D_ + 4 * D, D)
        g1 = at(D_ + 5 * D, D)
        wv = at(D_ + 8 * D, KD, AW)

        ps = ctx.enter_context(nc.psum_tensor("ps", [P, 8 * 512], F32))

        carry = sb("carry", [P, 4])

        def bank(b, n=512):
            return ps[:, b * 512:b * 512 + n]


        sems = {}

        def sem(name):
            sems[name] = ctx.enter_context(nc.semaphore(name))
            return sems[name]

        consts_in = sem("consts_in")
        tables_in = sem("tables_in")
        eps_ready = sem("eps_ready")
        x_in = [sem(f"x_in{b}") for b in range(2)]
        x_free = [sem(f"x_free{b}") for b in range(2)]
        rms_ready = sem("rms_ready")
        h_ready = sem("h_ready")
        hT_psum = sem("hT_psum")
        hT_ready = sem("hT_ready")
        wv_in = sem("wv_in")
        v_psum = sem("v_psum")
        v_ready = sem("v_ready")
        w_in_in = [sem(f"w_in_in{b}") for b in range(2)]
        proj_psum = sem("proj_psum")
        proj_out = sem("proj_out")
        mix_done = sem("mix_done")
        n_consts = 3 * 16

        with nc.Block() as block:
            @block.sync
            def _(sp):
                sp.dma_start(ident[:, :], c_mask[:, 0:P]).then_inc(consts_in, 16)
                sp.dma_start(g1, gains[0:1, :].partition_broadcast(P)).then_inc(consts_in, 16)
                for b in range(2):
                    sp.dma_start(xt[:, b], tokens[b * P:(b + 1) * P, :]).then_inc(x_in[b], 16)
                sp.dma_start(wv, w_in[:, 2 * AW:3 * AW].rearrange("(k p) n -> p k n", p=P)).then_inc(wv_in, 16)
                sp.dma_start(pars[:, :], par).then_inc(consts_in, 16)
                with sp.Fori(1, NTT // 2) as j:
                    for b in range(2):
                        sp.wait_ge(x_free[b], j)
                        sp.dma_start(xt[:, b], tokens[ds((2 * j + b) * P, P), :]).then_inc(x_in[b], 16)
                for b in range(2):
                    sp.dma_start(wb[:, b], w_in[:, 3 * AW + b * P:3 * AW + (b + 1) * P]
                                 .rearrange("(k p) n -> p k n", p=P)).then_inc(w_in_in[b], 16)
                sp.dma_start(onesbd[:, :], c_mask[:, P:2 * P]).then_inc(tables_in, 16)
                sp.dma_start(subg[:, :], sub_g.partition_broadcast(P)).then_inc(tables_in, 16)
                sp.dma_start(causal[:, :, :].rearrange("p a b -> p (a b)"),
                             c_mask[:, 2 * P:6 * P]).then_inc(tables_in, 16)
                sp.dma_start(lvl[:, :, :, :].rearrange("p a b c -> p (a b c)"),
                             c_mask[:, 6 * P:(6 + 2 * len(LEVELS)) * P]).then_inc(tables_in, 16)
                sp.dma_start(lamr[:, 0:256], lam_qk.partition_broadcast(P)).then_inc(tables_in, 16)
                with sp.Fori(1, (ZT - 2) // 2) as j:
                    for b in range(2):
                        sp.wait_ge(proj_psum, 2 * j + b - 1)
                        sp.dma_start(wb[:, b], w_in[:, ds((2 * j + b) * P + 3 * AW, P)]
                                     .rearrange("(k p) n -> p k n", p=P)).then_inc(w_in_in[b], 16)
                sp.wait_ge(proj_psum, ZT - 3)
                sp.dma_start(wb[:, 0], w_in[:, 3 * AW + 12 * P:3 * AW + 13 * P]
                             .rearrange("(k p) n -> p k n", p=P)).then_inc(w_in_in[0], 16)
                sp.wait_ge(proj_psum, ZT - 2)
                sp.dma_start(wb[:, 1, :, 0:GATE], w_in[:, 3 * AW + 13 * P:IN_COLS]
                             .rearrange("(k p) n -> p k n", p=P)).then_inc(w_in_in[1], 16)
                with sp.Fori(0, 4) as j:
                    for b in range(2):
                        sp.wait_ge(proj_psum, 2 * j + (ZT + b - 1))
                        sp.dma_start(wb[:, b], w_in[:, ds((2 * j + b) * P, P)]
                                     .rearrange("(k p) n -> p k n", p=P)).then_inc(w_in_in[b], 16)

            @block.scalar
            def _(act):
                act.drain().then_inc(hT_ready, 2)
                act.wait_ge(eps_ready, 1)
                with act.Fori(0, NTT // 2) as j:
                    for b in range(2):
                        act.wait_ge(x_in[b], 16 * j + 16)
                        act.activation(junk, xt[:, b], ACT.Square, accum_out=small[:, b:b + 1])
                        act.drain()
                        act.activation(small[:, 2 + b:3 + b], small[:, b:b + 1], ACT.Sqrt,
                                       bias=cst[:, 0:1], scale=1.0 / D).then_inc(rms_ready, 1)
                    for b in range(2):
                        act.wait_ge(hT_psum, 2 * j + b + 3)
                        for half in range(2):
                            ins = act.copy(hT[:, 4 * half:4 * half + 4, ds((2 * j + b) * P, P)],
                                           ps[:, (2 * b + half) * 512:(2 * b + half + 1) * 512]
                                           .rearrange("p (a b) -> p a b", b=P))
                        ins.then_inc(hT_ready, 1)
                with act.Fori(0, NTT // 2) as j:
                    for b in range(2):
                        act.wait_ge(v_psum, 2 * j + b + 1)
                        act.copy(vt[:, ds(2 * j + b, 1), :].rearrange("p a b -> p (a b)"),
                                 bank(4 + b)).then_inc(v_ready, 1)
                with act.Fori(0, ZT // 2) as j:
                    for b in range(2):
                        act.wait_ge(proj_psum, 2 * j + b + 1)
                        act.wait_ge(mix_done, 2 * j + b + 1)
                        act.copy(zpad[:, b, 1:1 + T0], ps[:, b * 2048:b * 2048 + T0])
                        act.copy(zpad[:, b, 2 + T0:2 + NT],
                                 ps[:, b * 2048 + T0:b * 2048 + NT]).then_inc(proj_out, 1)
                with act.Fori(0, 4) as j:
                    for b in range(2):
                        act.wait_ge(proj_psum, 2 * j + (ZT + b + 1))
                        act.copy(qk[:, ds(2 * j + b, 1), :].rearrange("p a b -> p (a b)"),
                                 ps[:, b * 2048:b * 2048 + NT]).then_inc(proj_out, 1)

            @block.vector
            def _(v):
                v.memset(cst[:, 0:1], NORM_EPS)
                v.memset(carry[:, :], 0.0)
                v.memset(cst[:, 1:2], GN_EPS).then_inc(eps_ready, 1)
                v.memset(restart[:, :], 1.0)
                v.memset(zpad.rearrange("p a b -> p (a b)"), 0.0)
                v.drain()
                v.memset(restart[:, :].rearrange("p (a b) -> p a b", b=C)[:, :, 0:1], 0.0)
                v.drain().then_inc(mix_done, 2)
                v.wait_ge(consts_in, n_consts)
                with v.Fori(0, NTT // 2) as j:
                    for b in range(2):
                        v.wait_ge(rms_ready, 2 * j + b + 1)
                        v.reciprocal(small[:, 4 + b:5 + b], small[:, 2 + b:3 + b])
                        v.drain()
                        v.wait_ge(hT_psum, 2 * j + b + 1)
                        v.scalar_tensor_tensor(hb[:, b], xt[:, b], small[:, 4 + b:5 + b], g1,
                                               ALU.mult, ALU.mult).then_inc(h_ready, 1)
                        v.drain().then_inc(x_free[b], 1)
                v.tensor_tensor(muc[:, :], pars[:, P_MU:P_MU + ZT], pars[:, P_MU + ZT:P_MU + 2 * ZT], ALU.add)
                v.drain()
                v.tensor_scalar(muc[:, :], muc[:, :], -1.0, 1.0, ALU.mult, ALU.add)
                v.drain()
                v.wait_ge(v_psum, NTT)
                with v.Fori(0, ZT // 2) as j:
                    for b in range(2):
                        v.wait_ge(proj_out, 2 * j + b + 1)
                        v.tensor_copy(small[:, 8:9], muc[:, ds(2 * j + b, 1)])
                        v.tensor_copy(small[:, 9:10], pars[:, ds(2 * j + b + P_MU, 1)])
                        v.tensor_copy(small[:, 10:11], pars[:, ds(2 * j + b + P_MU + ZT, 1)])
                        v.drain()
                        for step in range(3):
                            for o, c, n in ((1, 0, T0), (T0 + 2, T0, T1)):
                                dst = zt[:, ds(2 * j + b, 1), c:c + n].rearrange("p a b -> p (a b)")
                                if step == 0:
                                    v.tensor_scalar(dst, zpad[:, b, o:o + n], small[:, 8:9], None, ALU.mult)
                                else:
                                    src = zpad[:, b, o - 1:o - 1 + n] if step == 1 else zpad[:, b, o + 1:o + 1 + n]
                                    v.scalar_tensor_tensor(dst, src, small[:, 8 + step:9 + step], dst,
                                                           ALU.mult, ALU.add)
                            if step < 2:
                                v.drain()
                        v.drain().then_inc(mix_done, 1)

            @block.tensor
            def _(pe):
                pe.drain().then_inc(hT_psum, 2)
                pe.wait_ge(consts_in, n_consts)
                with pe.Fori(0, NTT // 2) as j:
                    for b in range(2):
                        pe.wait_ge(h_ready, 2 * j + b + 1)
                        pe.wait_ge(hT_ready, 2 * j + b + 1)
                        for k in range(KD):
                            o = 2 * b * 512 + k * P
                            ins = pe.transpose(ps[:, o:o + P], hb[:, b, k * P:(k + 1) * P], ident[:, :])
                        ins.then_inc(hT_psum, 1)
                pe.wait_ge(wv_in, 16)
                pe.wait_ge(hT_ready, NTT + 2)
                for t in range(NTT):
                    if t >= 2:
                        pe.wait_ge(v_ready, t - 1)
                    for k in range(KD):
                        ins = pe.matmul(bank(4 + t % 2), hT[:, k, t * P:(t + 1) * P], wv[:, k, :],
                                        start=(k == 0), stop=(k == KD - 1))
                    ins.then_inc(v_psum, 1)
                pe.wait_ge(v_ready, NTT)

                def project(b):
                    for o, n in CHUNKS:
                        for k in range(KD):
                            ins = pe.matmul(ps[:, b * 2048 + o:b * 2048 + o + n], wb[:, b, k, :],
                                            hT[:, k, o:o + n], start=(k == 0), stop=(k == KD - 1))
                    ins.then_inc(proj_psum, 1)

                for b in range(2):
                    pe.wait_ge(w_in_in[b], 16)
                    project(b)
                with pe.Fori(1, ZT // 2 + 4) as j:
                    for b in range(2):
                        pe.wait_ge(w_in_in[b], 16 * j + 16)
                        pe.wait_ge(proj_out, 2 * j + b - 1)
                        project(b)

        sq = at(A_, 2, NT)
        ob = at(A_ + 2 * NT, 4, NT)
        tmp = at(A_ + 6 * NT, NT)
        lora_in = sem("lora_in")
        loraw_zero = sem("loraw_zero")
        tanh_done = sem("tanh_done")
        sq_ready = sem("sq_ready")
        pre_psum = sem("pre_psum")
        root_ready = sem("root_ready")
        pset_free = [sem(f"pset_free{b}") for b in range(2)]
        ob_full = [sem(f"ob_full{b}") for b in range(4)]
        ob_stored = [sem(f"ob_stored{b}") for b in range(4)]
        z_stored = sem("z_stored")
        items = [("kk", f, 0, F_KK + f) for f in range(RT)]
        for f in range(RT):
            items.append(("bonus", f, 0, F_BONUS + f))
            for d in range(2):
                items.append(("sig", f, d, F_SIG + RT * d + f))
                items.append(("ic", f, d, F_IC + RT * d + f))
            items.append(("gate", f, 0, F_GATE + f))
        n_sums = [sum(1 for x in items[:n] if x[0] in ("kk", "bonus")) for n in range(len(items) + 1)]
        Z_LORA, Z_GATE = 3 * RT, 3 * RT + 1

        with nc.Block() as block:
            @block.sync
            def _(sp):
                sp.wait_ge(loraw_zero, 1)
                for n, w in enumerate((w2[0], w2[1], a2[0], a2[1])):
                    sp.dma_start(loraw[32 * n:32 * n + 32, RW * n:RW * (n + 1)], w).then_inc(lora_in, 16)
                sp.dma_start(g2s[:, :], g2).then_inc(lora_in, 16)
                sp.dma_start(feat[0:3 * RT].rearrange("t p n -> p t n"), zt[:, 0:3 * RT, :]).then_inc(z_stored, 16)
                for n, (_, _, _, where) in enumerate(items):
                    sp.wait_ge(ob_full[n % 4], n // 4 + 1)
                    sp.dma_start(feat[where], ob[:, n % 4]).then_inc(ob_stored[n % 4], 16)
                for b in range(4):
                    sp.wait_ge(ob_stored[b], 16 * len(items[b::4]))
                sp.wait_ge(z_stored, 16)

            @block.tensor
            def _(pe):
                pe.wait_ge(tables_in, 5 * 16)
                pe.wait_ge(lora_in, 5 * 16)
                for n, (what, f, d, _) in enumerate(items):
                    if what in ("kk", "bonus"):
                        pe.wait_ge(sq_ready, n_sums[n + 1])
                    if n >= 2:
                        pe.wait_ge(pset_free[n % 2], n // 2)
                    if what in ("sig", "ic", "gate"):
                        pe.wait_ge(tanh_done, 1)
                    for o, c in CHUNKS:
                        dst = ps[:, (n % 2) * 2048 + o:(n % 2) * 2048 + o + c]
                        if what in ("kk", "bonus"):
                            ins = pe.matmul(dst, onesbd[:, :], sq[:, n_sums[n] % 2, o:o + c], start=True, stop=True)
                        elif what == "gate":
                            ins = pe.matmul(dst, g2s[:, f * P:(f + 1) * P], zt[0:GATE, Z_GATE, o:o + c],
                                            start=True, stop=True)
                        else:
                            w = (d if what == "sig" else 2 + d) * RW + f * P
                            ins = pe.matmul(dst, loraw[:, w:w + P], zt[:, Z_LORA, o:o + c], start=True, stop=True)
                    ins.then_inc(pre_psum, 1)

            @block.scalar
            def _(act):
                act.activation(zt[0:64, Z_LORA, :], zt[0:64, Z_LORA, :], ACT.Tanh)
                act.activation(zt[0:GATE, Z_GATE, :], zt[0:GATE, Z_GATE, :], ACT.Sigmoid).then_inc(tanh_done, 1)
                for n, (what, f, d, _) in enumerate(items):
                    src = ps[:, (n % 2) * 2048:(n % 2) * 2048 + NT]
                    if what == "bonus":
                        continue
                    act.wait_ge(pre_psum, n + 1)
                    if what == "kk":
                        act.activation(src, src, ACT.Sqrt).then_inc(root_ready, 1)
                        continue
                    if n >= 4:
                        act.wait_ge(ob_stored[n % 4], 16 * (n // 4))
                    if what == "gate":
                        act.copy(ob[:, n % 4], src)
                    else:
                        first = P_W0 if what == "sig" else P_A0
                        act.activation(ob[:, n % 4], src, ACT.Sigmoid,
                                       bias=pars[:, first + RT * d + f:first + RT * d + f + 1])
                    act.drain().then_inc(ob_full[n % 4], 1)
                    act.drain().then_inc(pset_free[n % 2], 1)

            @block.vector
            def _(v):
                v.memset(loraw, 0.0).then_inc(loraw_zero, 1)

                def operand(n):
                    what, f, _, _ = items[n]
                    if n_sums[n] >= 2:
                        last = [m for m in range(n) if items[m][0] in ("kk", "bonus")][-2]
                        v.wait_ge(pre_psum, last + 1)
                    dst = sq[:, n_sums[n] % 2]
                    if what == "kk":
                        v.tensor_scalar(dst, zt[:, RT + f], pars[:, P_KK + f:P_KK + f + 1], None, ALU.mult)
                        v.drain()
                        v.tensor_tensor(dst, dst, dst, ALU.mult).then_inc(sq_ready, 1)
                    else:
                        v.scalar_tensor_tensor(dst, zt[:, f], pars[:, P_RK + f:P_RK + f + 1], zt[:, RT + f],
                                               ALU.mult, ALU.mult).then_inc(sq_ready, 1)

                sums = [n for n in range(len(items)) if items[n][0] in ("kk", "bonus")]
                operand(sums[0])
                for s, n in enumerate(sums):
                    if s + 1 < len(sums):
                        operand(sums[s + 1])
                    what, f, _, _ = items[n]
                    src = ps[:, (n % 2) * 2048:(n % 2) * 2048 + NT]
                    if n >= 4:
                        v.wait_ge(ob_stored[n % 4], 16 * (n // 4))
                    if what == "kk":
                        v.wait_ge(root_ready, s + 1)
                        v.tensor_scalar(tmp, src, 1e-12, None, ALU.max)
                        v.drain()
                        v.reciprocal(tmp, tmp)
                        v.drain()
                        v.scalar_tensor_tensor(ob[:, n % 4], zt[:, RT + f], pars[:, P_KK + f:P_KK + f + 1], tmp,
                                               ALU.mult, ALU.mult)
                    else:
                        v.wait_ge(pre_psum, n + 1)
                        v.tensor_tensor(ob[:, n % 4], src, zt[:, 2 * RT + f], ALU.mult)
                    v.drain().then_inc(ob_full[n % 4], 1)
                    v.drain().then_inc(pset_free[n % 2], 1)

        qz = at(D_, 2, NT)
        sc = at(D_ + 2 * NT, 2, 2, T0)
        pd = at(D_ + 2 * NT + 4 * T0, T0)
        pdT = at(D_ + 2 * NT + 5 * T0, KD, P)
        oraw = at(D_ + 2 * NT + 6 * T0, HEADS_A, NTT, P)
        bias = at(A_, BIAS_W)
        ojunk = at(A_ + 2048, P)
        ostat = at(A_ + 2048 + P, 3, HEADS_A * NTT)
        srow = at(A_ + 2048 + 4 * P, 2, 8)
        bias_in = sem("bias_in")
        lam_exp = sem("lam_exp")
        lam_dot = sem("lam_dot")
        q_ready = sem("q_ready")
        scores_psum = sem("scores_psum")
        scores_read = sem("scores_read")
        probs_ready = sem("probs_ready")
        pd_ready = sem("pd_ready")
        pdT_psum = sem("pdT_psum")
        pdT_ready = sem("pdT_ready")
        o_psum = sem("o_psum")
        o_read = sem("o_read")
        ostat_root = sem("ostat_root")
        on_ready = sem("on_ready")
        oT_psum = sem("oT_psum")
        oT_read = sem("oT_read")
        NU = NTT
        units = [(0, T0, i) for i in range(T0 // P)] + [(T0, T1, i) for i in range(T1 // P)]

        with nc.Block() as block:
            @block.sync
            def _(sp):
                sp.dma_start(bias, c_bias).then_inc(bias_in, 16)

            @block.tensor
            def _(pe):
                with pe.Fori(0, HEADS_A) as h:
                    pe.wait_ge(q_ready, h + 1)

                    def scores(u):
                        t0, n, i = units[u]
                        for m in range(2):
                            pe.wait_ge(scores_read, 2 * NU * h + (2 * u + m + 1))
                            for o in range(0, n, 512):
                                w = min(512, n)
                                ins = pe.matmul(ps[:, m * T0 + o:m * T0 + o + w],
                                                qz[:, m, t0 + i * P:t0 + (i + 1) * P],
                                                qk[:, ds(h + HEADS_A, 1), t0 + o:t0 + o + w]
                                                .rearrange("p a b -> p (a b)"), start=True, stop=True)
                            ins.then_inc(scores_psum, 1)

                    scores(0)
                    for u, (t0, n, i) in enumerate(units):
                        if u + 1 < NU:
                            scores(u + 1)
                        pe.wait_ge(pd_ready, NU * h + (u + 1))
                        pe.wait_ge(pdT_ready, NU * h + (u + 1))
                        for k in range(n // P):
                            ins = pe.transpose(ps[:, 4 * 512 + k * P:4 * 512 + (k + 1) * P],
                                               pd[:, k * P:(k + 1) * P], ident[:, :])
                        ins.then_inc(pdT_psum, 1)
                        pe.wait_ge(pdT_ready, NU * h + (u + 2))
                        pe.wait_ge(o_read, NU * h + (u + 1))
                        for k in range(n // P):
                            ins = pe.matmul(bank(6, P), pdT[:, k, :],
                                            vt[:, t0 // P + k, ds(h * P, P)],
                                            start=(k == 0), stop=(k == n // P - 1))
                        ins.then_inc(o_psum, 1)
                for n in range(HEADS_A):
                    for u in range(NU):
                        m = n * NU + u
                        pe.wait_ge(on_ready, m + 1)
                        if m >= 2:
                            pe.wait_ge(oT_read, m - 1)
                        pe.transpose(bank(m % 2, P), oraw[:, n, u], ident[:, :]).then_inc(oT_psum, 1)

            @block.scalar
            def _(act):
                act.drain().then_inc(pdT_ready, 1)
                act.drain().then_inc(o_read, 1)
                act.wait_ge(lam_dot, 1)
                act.activation(small[:, 18:20], small[:, 16:18], ACT.Exp).then_inc(lam_exp, 1)
                with act.Fori(0, HEADS_A) as h:
                    def probs(u):
                        t0, n, i = units[u]
                        for m in range(2):
                            act.wait_ge(scores_read, 2 * NU * h + (2 * u + m + 3))
                            act.activation(sc[:, u % 2, m, 0:n], sc[:, u % 2, m, 0:n], ACT.Exp,
                                           bias=srow[:, u % 2, m:m + 1],
                                           accum_out=srow[:, u % 2, 2 + m:3 + m]).then_inc(probs_ready, 1)

                    probs(0)
                    for u, (t0, n, i) in enumerate(units):
                        if u + 1 < NU:
                            probs(u + 1)
                        act.wait_ge(pdT_psum, NU * h + (u + 1))
                        act.copy(pdT[:, 0:n // P, :].rearrange("p a b -> p (a b)"),
                                 ps[:, 4 * 512:4 * 512 + n]).then_inc(pdT_ready, 1)
                        act.wait_ge(o_psum, NU * h + (u + 1))
                        act.copy(oraw[:, ds(h, 1), u].rearrange("p a b -> p (a b)"), bank(6, P))
                        act.activation(ojunk, bank(6, P), ACT.Square,
                                       accum_out=ostat[:, 0, ds(h * NU + u, 1)])
                        act.drain().then_inc(o_read, 1)
                act.activation(ostat[:, 1], ostat[:, 0], ACT.Sqrt, bias=cst[:, 0:1],
                               scale=1.0 / P).then_inc(ostat_root, 1)
                for n in range(HEADS_A):
                    for u in range(NU):
                        m = n * NU + u
                        act.wait_ge(oT_psum, m + 1)
                        act.copy(qk[:, n, u * P:(u + 1) * P], bank(m % 2, P)).then_inc(oT_read, 1)

            @block.vector
            def _(v):
                v.wait_ge(tables_in, 5 * 16)
                for n in range(2):
                    v.tensor_tensor(lamr[:, 256 + 64 * n:320 + 64 * n], lamr[:, 128 * n:128 * n + 64],
                                    lamr[:, 128 * n + 64:128 * n + 128], ALU.mult)
                v.drain()
                v.tensor_reduce(small[:, 16:18], lamr[:, 256:384].rearrange("p (a b) -> p a b", b=64),
                                AX, ALU.add).then_inc(lam_dot, 1)
                v.memset(qz.rearrange("p a b -> p (a b)"), 0.0)
                v.wait_ge(lam_exp, 1)
                v.tensor_tensor(small[:, 20:21], small[:, 19:20], small[:, 18:19], ALU.subtract)
                v.drain()
                v.tensor_scalar(cst[:, 2:3], small[:, 20:21], -LAMBDA_INIT, None, ALU.add)
                v.drain().then_inc(scores_read, 2)
                v.wait_ge(bias_in, 16)
                with v.Fori(0, HEADS_A) as h:
                    v.tensor_scalar(bias, bias, 0.25, None, ALU.mult)
                    for m in range(2):
                        v.tensor_scalar(qz[64 * m:64 * m + 64, m, :],
                                        qk[64 * m:64 * m + 64, ds(h, 1), :].rearrange("p a b -> p (a b)"),
                                        0.125, None, ALU.mult)
                    v.drain().then_inc(q_ready, 1)

                    def biased(u):
                        t0, n, i = units[u]
                        for m in range(2):
                            v.wait_ge(scores_psum, 2 * NU * h + (2 * u + m + 1))
                            v.tensor_copy(carry[0:1, 0:1], carry[0:1, 1:2])
                            w = T0 - P - i * P
                            v.tensor_tensor_reduce(sc[:, u % 2, m, 0:n], ps[:, m * T0:m * T0 + n],
                                                   bias[:, w:w + n], 1.0, -3.0e38, ALU.add, ALU.max,
                                                   small[:, 24 + m:25 + m])
                            v.drain()
                            v.tensor_scalar(srow[:, u % 2, m:m + 1], small[:, 24 + m:25 + m], -1.0, None,
                                            ALU.mult).then_inc(scores_read, 1)

                    biased(0)
                    for u, (t0, n, i) in enumerate(units):
                        if u + 1 < NU:
                            biased(u + 1)
                        v.wait_ge(probs_ready, 2 * NU * h + (2 * u + 2))
                        r = srow[:, u % 2]
                        v.reciprocal(r[:, 4:6], r[:, 2:4])
                        v.drain()
                        v.tensor_scalar(r[:, 5:6], r[:, 5:6], cst[:, 2:3], None, ALU.mult)
                        if u:
                            v.wait_ge(pdT_psum, NU * h + u)
                        v.tensor_scalar(pd[:, 0:n], sc[:, u % 2, 0, 0:n], r[:, 4:5], None, ALU.mult)
                        v.drain()
                        v.scalar_tensor_tensor(pd[:, 0:n], sc[:, u % 2, 1, 0:n], r[:, 5:6], pd[:, 0:n],
                                               ALU.mult, ALU.add).then_inc(pd_ready, 1)
                        v.drain()
                v.wait_ge(ostat_root, 1)
                v.reciprocal(ostat[:, 2], ostat[:, 1])
                v.drain()
                v.tensor_scalar(ostat[:, 2], ostat[:, 2], 1.0 - LAMBDA_INIT, None, ALU.mult)
                v.drain()
                for n in range(HEADS_A):
                    for u in range(NU):
                        m = n * NU + u
                        v.scalar_tensor_tensor(oraw[:, n, u], oraw[:, n, u], ostat[:, 2, m:m + 1], subg[:, :],
                                               ALU.mult, ALU.mult).then_inc(on_ready, 1)

        yacc = at(B_ + RT * NT, RT, NT)
        R1, R2 = A_, C_
        cin = [at(R2 + d * 6 * RT * C, 6, RT * C) for d in range(2)]
        o2 = R2 + 12 * RT * C
        ext = [at(o2 + d * 7 * RT * C, 7, RT * C) for d in range(2)]
        o3 = o2 + 14 * RT * C
        ar_bd = [at(o3 + d * RT * 5 * P, RT, 2, P) for d in range(2)]
        b_bd = [at(o3 + d * RT * 5 * P + RT * 2 * P, RT, P) for d in range(2)]
        k_bd = [at(o3 + d * RT * 5 * P + RT * 3 * P, RT, P) for d in range(2)]
        v_bd = [at(o3 + d * RT * 5 * P + RT * 4 * P, RT, P) for d in range(2)]
        o4 = o3 + RT * 10 * P
        bm = [at(o4 + d * RT * 4 * P, RT, 2, P) for d in range(2)]
        km = [at(o4 + d * RT * 4 * P + RT * 2 * P, RT, 2, P) for d in range(2)]
        o5 = o4 + RT * 8 * P
        inv = [at(o5 + d * RT * 2 * P, RT, P) for d in range(2)]
        invT = [at(o5 + d * RT * 2 * P + RT * P, RT, P) for d in range(2)]
        assert o5 + RT * 4 * P <= E_ + 2 * KD * P + 2 * (NT + 3)
        alv = [at(R1 + d * 6 * RT * P, len(LEVELS), RT, P) for d in range(2)]
        o6 = R1 + 12 * RT * P
        tokb = [at(o6 + d * 4 * RT * P, RT, P) for d in range(2)]
        tokk = [at(o6 + d * 4 * RT * P + RT * P, RT, P) for d in range(2)]
        tokv = [at(o6 + d * 4 * RT * P + 2 * RT * P, RT, P) for d in range(2)]
        prod = [at(o6 + d * 4 * RT * P + 3 * RT * P, RT, P) for d in range(2)]
        assert o6 + 8 * RT * P <= B_
        state = [sb(f"state{d}", [P, RT, P]) for d in range(2)]
        eb = sb("eb", [P, 2, RT])

        cin_in = [sem(f"cin_in{d}") for d in range(2)]
        cin_free = [sem(f"cin_free{d}") for d in range(2)]
        cum_ready = [sem(f"cum_ready{d}") for d in range(2)]
        exp_ready = [sem(f"exp_ready{d}") for d in range(2)]
        vbd_ready = [sem(f"vbd_ready{d}") for d in range(2)]
        bd_ready = [sem(f"bd_ready{d}") for d in range(2)]
        pairs_psum = [sem(f"pairs_psum{d}") for d in range(2)]
        pairs_read = [sem(f"pairs_read{d}") for d in range(2)]
        lvl_ready = [sem(f"lvl_ready{d}") for d in range(2)]
        lvl_rest = [sem(f"lvl_rest{d}") for d in range(2)]
        tok_psum = [sem(f"tok_psum{d}") for d in range(2)]
        tok_read = [sem(f"tok_read{d}") for d in range(2)]
        inv_ready = [sem(f"inv_ready{d}") for d in range(2)]
        ax_psum = [sem(f"ax_psum{d}") for d in range(2)]
        prod_ready = [sem(f"prod_ready{d}") for d in range(2)]
        xax_psum = [sem(f"xax_psum{d}") for d in range(2)]
        state_ready = [sem(f"state_ready{d}") for d in range(2)]
        invT_final = [sem(f"invT_final{d}") for d in range(2)]
        g_psum = [sem(f"g_psum{d}") for d in range(2)]
        u_psum = [sem(f"u_psum{d}") for d in range(2)]
        y_psum = [sem(f"y_psum{d}") for d in range(2)]
        y_read = [sem(f"y_read{d}") for d in range(2)]
        NL = len(LEVELS) - 1
        SEGS = ((0, T0 // C, 0), (T0, T1 // C, T0 // C))

        with nc.Block() as block:
            @block.sync
            def _(sp):
                for t0, nch, c0 in SEGS:
                    with sp.Fori(0, nch) as n:
                        for d in range(2):
                            first = n * C + t0 if d == 0 else (nch - 1) * C + t0 - n * C
                            sp.wait_ge(cin_free[d], 1)
                            sp.wait_ge(cin_free[d], n + (c0 + 1))
                            for q, t in ((0, F_R), (1, F_K), (2, F_V), (3, F_KK),
                                         (4, F_SIG + RT * d), (5, F_IC + RT * d)):
                                sp.dma_start(cin[d][:, q].rearrange("p (a b) -> p a b", b=C),
                                             feat[t:t + RT, :, ds(first, C)].rearrange("t p n -> p t n")
                                             ).then_inc(cin_in[d], 16)

            @block.gpsimd
            def _(pool):
                for t0, nch, c0 in SEGS:
                    with pool.Fori(0, nch) as n:
                        for d in range(2):
                            pool.wait_ge(pairs_read[d], n + (c0 + 1))
                            for l in range(2, NL + 1):
                                pool.tensor_tensor(alv[d][:, l], bm[d][:, :, 0],
                                                   lvl[:, d, l:l + 1, :].broadcast_to([P, RT, P]),
                                                   ALU.mult).then_inc(lvl_rest[d], 1)

            @block.tensor
            def _(pe):
                def pb(d, b, p):
                    return ps[:, (4 * d + b) * 512 + p * P:(4 * d + b) * 512 + (p + 1) * P]

                for t0, nch, c0 in SEGS:
                    with pe.Fori(0, nch) as n:
                        for d in range(2):
                            pe.wait_ge(bd_ready[d], n + (c0 + 1))
                            pe.wait_ge(vbd_ready[d], n + (c0 + 1))
                            pe.wait_ge(y_read[d], n + (c0 + 1))
                            for p in range(RT):
                                for b, m in ((0, b_bd), (2, k_bd)):
                                    o = (4 * d + b + p // 2) * 512 + (p % 2) * 2 * P
                                    ins = pe.matmul(ps[:, o:o + 2 * P], m[d][:, p],
                                                    ar_bd[d][:, p].rearrange("p a b -> p (a b)"),
                                                    start=True, stop=True)
                            ins.then_inc(pairs_psum[d], 1)
                        for d in range(2):
                            pe.wait_ge(pairs_read[d], n + (c0 + 1))
                            pe.wait_ge(lvl_ready[d], n + (c0 + 1))
                            for p in range(RT):
                                pe.transpose(pb(d, 3, p), alv[d][:, 0, p], ident[:, :])
                            for p in range(RT):
                                for b, m in ((0, b_bd), (1, k_bd), (2, v_bd)):
                                    ins = pe.transpose(pb(d, b, p), m[d][:, p], ident[:, :])
                            ins.then_inc(tok_psum[d], 1)
                        for l in range(1, NL + 1):
                            for d in range(2):
                                pe.wait_ge(inv_ready[d], NL * n + (NL * c0 + l))
                                if l == 1:
                                    pe.wait_ge(tok_read[d], n + (c0 + 1))
                                if l >= 2:
                                    pe.wait_ge(lvl_rest[d], (NL - 1) * n + ((NL - 1) * c0 + l - 1))
                                for p in range(RT):
                                    ins = pe.matmul(pb(d, 0, p), alv[d][:, l, p], inv[d][:, p],
                                                    start=True, stop=True)
                                ins.then_inc(ax_psum[d], 1)
                            for d in range(2):
                                pe.wait_ge(prod_ready[d], (NL + 2) * n + ((NL + 2) * c0 + l))
                                for p in range(RT):
                                    if l < NL:
                                        pe.matmul(pb(d, 1, p), invT[d][:, p], prod[d][:, p],
                                                  start=True, stop=True)
                                    ins = pe.matmul(pb(d, 2, p), prod[d][:, p], invT[d][:, p],
                                                    start=True, stop=True)
                                ins.then_inc(xax_psum[d], 1)
                        for d in range(2):
                            pe.wait_ge(state_ready[d], n + (c0 + 1))
                            for p in range(RT):
                                pe.matmul(pb(d, 3, p), ar_bd[d][:, p, 0], state[d][:, p], start=True, stop=False)
                                ins = pe.matmul(pb(d, 3, p), km[d][:, p, 0], tokv[d][:, p], start=False, stop=True)
                            ins.then_inc(g_psum[d], 1)
                        for d in range(2):
                            pe.wait_ge(prod_ready[d], (NL + 2) * n + ((NL + 2) * c0 + NL + 1))
                            pe.wait_ge(invT_final[d], n + (c0 + 1))
                            for p in range(RT):
                                ins = pe.matmul(pb(d, 0, p), invT[d][:, p], prod[d][:, p], start=True, stop=True)
                            ins.then_inc(u_psum[d], 1)
                        for d in range(2):
                            for p in range(RT):
                                pe.matmul(pb(d, 1, p), state[d][:, p], ar_bd[d][:, p, 1], start=True, stop=False)
                                pe.matmul(pb(d, 1, p), tokv[d][:, p], km[d][:, p, 1], start=False, stop=False)
                                if p == 0:
                                    pe.wait_ge(prod_ready[d], (NL + 2) * n + ((NL + 2) * c0 + NL + 2))
                                pe.matmul(pb(d, 1, p), prod[d][:, p], bm[d][:, p, 1], start=False, stop=True)
                                pe.matmul(pb(d, 2, p), tokb[d][:, p], prod[d][:, p], start=True, stop=False)
                                ins = pe.matmul(pb(d, 2, p), tokk[d][:, p], tokv[d][:, p], start=False, stop=True)
                            ins.then_inc(y_psum[d], 1)

            @block.scalar
            def _(act):
                for t0, nch, c0 in SEGS:
                    with act.Fori(0, nch) as n:
                        for d in range(2):
                            s = -1.0 if d else 1.0
                            cum, exc = ext[d][:, 0], ext[d][:, 1]
                            act.wait_ge(cum_ready[d], n + (c0 + 1))
                            for slot, src, sign in (((2, exc, 1), (3, cum, 1), (4, cum, -1)) if d == 0 else
                                                    ((2, cum, -1), (3, exc, -1), (4, exc, 1))):
                                act.activation(ext[d][:, slot], src, ACT.Exp, scale=sign * DECAY)
                            act.activation(eb[:, d, :].unsqueeze(2),
                                           cum.rearrange("p (a b) -> p a b", b=C)[:, :, C - 1:C],
                                           ACT.Exp, scale=DECAY).then_inc(exp_ready[d], 1)
                            for hh in range(2):
                                r = slice(64 * hh, 64 * hh + 64)
                                ins = act.copy(v_bd[d][r, :, 64 * hh:64 * hh + 64],
                                               cin[d][r, 2].rearrange("p (a b) -> p a b", b=C))
                            ins.then_inc(vbd_ready[d], 1)
                        for d in range(2):
                            act.wait_ge(tok_psum[d], n + (c0 + 1))
                            for b, m in ((0, tokb), (1, tokk), (2, tokv)):
                                ins = act.copy(m[d].rearrange("p a b -> p (a b)"), bank(4 * d + b))
                            ins.then_inc(tok_read[d], 1)
                        for l in range(1, NL + 1):
                            for d in range(2):
                                act.wait_ge(ax_psum[d], NL * n + (NL * c0 + l))
                                act.copy(prod[d].rearrange("p a b -> p (a b)"),
                                         bank(4 * d)).then_inc(prod_ready[d], 1)
                        for d in range(2):
                            act.wait_ge(g_psum[d], n + (c0 + 1))
                            act.copy(prod[d].rearrange("p a b -> p (a b)"),
                                     bank(4 * d + 3)).then_inc(prod_ready[d], 1)
                        for d in range(2):
                            act.wait_ge(u_psum[d], n + (c0 + 1))
                            act.copy(prod[d].rearrange("p a b -> p (a b)"),
                                     bank(4 * d)).then_inc(prod_ready[d], 1)

            @block.vector
            def _(v):
                def tiles(x):
                    return x.rearrange("p (a b) -> p a b", b=C)

                v.memset(at(o3, RT * 10 * P), 0.0)
                v.memset(yacc.rearrange("p a b -> p (a b)"), 0.0)
                v.drain()
                for d in range(2):
                    v.drain().then_inc(cin_free[d], 1)
                    v.drain().then_inc(y_read[d], 1)
                for t0, nch, c0 in SEGS:
                    for d in range(2):
                        v.memset(state[d][:, :, :].rearrange("p a b -> p (a b)"), 0.0)
                    v.drain()
                    with v.Fori(0, nch) as n:
                        for d in range(2):
                            r_, k_, v_, kk_, sig_, ic_ = (cin[d][:, q] for q in range(6))
                            cum, exc, ea, er, ebk, t1, t2 = (ext[d][:, q] for q in range(7))
                            v.wait_ge(cin_in[d], 96 * n + (96 * c0 + 96))
                            v.tensor_tensor_scan(cum, restart[:, :], sig_, 0.0, ALU.mult, ALU.add)
                            v.tensor_tensor(t1, kk_, ic_, ALU.mult)
                            v.scalar_tensor_tensor(
                                tiles(t2), tiles(ic_), -1.0,
                                pars[:, P_KA:P_KA + RT].unsqueeze(2).broadcast_to([P, RT, C]), ALU.add, ALU.mult)
                            v.drain()
                            v.tensor_tensor(exc, cum, sig_, ALU.subtract).then_inc(cum_ready[d], 1)
                            v.scalar_tensor_tensor(t2, t2, 1.0, k_, ALU.add, ALU.mult)
                            v.drain()
                            v.wait_ge(exp_ready[d], n + (c0 + 1))
                            if d == 1:
                                v.tensor_tensor(state[d][:, :, :], state[d][:, :, :],
                                                eb[:, d, :].unsqueeze(2).broadcast_to([P, RT, P]), ALU.mult)
                            for hh in range(2):
                                r = slice(64 * hh, 64 * hh + 64)
                                c = slice(64 * hh, 64 * hh + 64)
                                v.scalar_tensor_tensor(ar_bd[d][r, :, 0, c], tiles(kk_)[r], -1.0, tiles(ea)[r],
                                                       ALU.mult, ALU.mult)
                                v.tensor_tensor(ar_bd[d][r, :, 1, c], tiles(r_)[r], tiles(er)[r], ALU.mult)
                                v.tensor_tensor(b_bd[d][r, :, c], tiles(t1)[r], tiles(ebk)[r], ALU.mult)
                                v.tensor_tensor(k_bd[d][r, :, c], tiles(t2)[r], tiles(ebk)[r], ALU.mult)
                            v.drain().then_inc(bd_ready[d], 1)
                            v.drain().then_inc(state_ready[d], 1)
                            v.wait_ge(vbd_ready[d], n + (c0 + 1))
                            v.tensor_copy(carry[0:1, 0:1], carry[0:1, 1:2])
                            v.drain().then_inc(cin_free[d], 1)
                        for d in range(2):
                            v.wait_ge(pairs_psum[d], n + (c0 + 1))
                            for b, m in ((0, bm), (2, km)):
                                for half in range(2):
                                    v.tensor_tensor(
                                        m[d][:, 2 * half:2 * half + 2].rearrange("p a b c -> p a (b c)"),
                                        bank(4 * d + b + half).rearrange("p (a b) -> p a b", b=2 * P),
                                        causal[:, d:d + 1, :].broadcast_to([P, 2, 2 * P]), ALU.mult)
                            v.drain().then_inc(pairs_read[d], 1)
                            for l in range(2):
                                v.tensor_tensor(alv[d][:, l], bm[d][:, :, 0],
                                                lvl[:, d, l:l + 1, :].broadcast_to([P, RT, P]), ALU.mult)
                            v.drain().then_inc(lvl_ready[d], 1)
                            v.tensor_tensor(invT[d], alv[d][:, 0],
                                            ident[:, :].unsqueeze(1).broadcast_to([P, RT, P]), ALU.add)
                        for d in range(2):
                            v.wait_ge(tok_psum[d], n + (c0 + 1))
                            v.tensor_tensor(inv[d], bank(4 * d + 3).rearrange("p (a b) -> p a b", b=P),
                                            ident[:, :].unsqueeze(1).broadcast_to([P, RT, P]), ALU.add)
                            v.drain().then_inc(inv_ready[d], 1)
                        for l in range(1, NL + 1):
                            for d in range(2):
                                v.wait_ge(xax_psum[d], NL * n + (NL * c0 + l))
                                if l < NL:
                                    v.tensor_tensor(inv[d].rearrange("p a b -> p (a b)"),
                                                    inv[d].rearrange("p a b -> p (a b)"), bank(4 * d + 1), ALU.add)
                                ins = v.tensor_tensor(invT[d].rearrange("p a b -> p (a b)"),
                                                      invT[d].rearrange("p a b -> p (a b)"), bank(4 * d + 2), ALU.add)
                                if l < NL:
                                    v.drain().then_inc(inv_ready[d], 1)
                                else:
                                    v.drain().then_inc(invT_final[d], 1)
                        for d in range(2):
                            v.wait_ge(y_psum[d], n + (c0 + 1))
                            v.tensor_copy(carry[0:1, 0:1], carry[0:1, 1:2])
                            for hh in range(2):
                                r = slice(64 * hh, 64 * hh + 64)
                                first = n * C + t0 if d == 0 else (nch - 1) * C + t0 - n * C
                                y = yacc[r, :, ds(first, C)]
                                v.tensor_tensor(y, y, bank(4 * d + 1).rearrange("p (a b) -> p a b", b=P)
                                                [r, :, 64 * hh:64 * hh + 64], ALU.add)
                            v.tensor_tensor(state[d][:, :, :].rearrange("p a b -> p (a b)"),
                                            state[d][:, :, :].rearrange("p a b -> p (a b)"),
                                            bank(4 * d + 2), ALU.add)
                            v.drain().then_inc(y_read[d], 1)
                            if d == 0:
                                v.tensor_tensor(state[d][:, :, :], state[d][:, :, :],
                                                eb[:, d, :].unsqueeze(2).broadcast_to([P, RT, P]), ALU.mult)
                                v.drain()

        bonus = at(A_, RT, NT)
        gate = at(R2, RT, NT)
        cen = at(R2 + RT * NT, 2, NT)
        csq = at(R2 + (RT + 2) * NT, 2, NT)
        inv_s = at(R2 + (RT + 4) * NT, 2, NT)
        post_in = sem("post_in")
        sum_psum = sem("sum_psum")
        csq_ready = sem("csq_ready")
        var_psum = sem("var_psum")
        std_ready = sem("std_ready")
        post_done = sem("post_done")

        with nc.Block() as block:
            @block.sync
            def _(sp):
                sp.dma_start(bonus, feat[F_BONUS:F_BONUS + RT].rearrange("t p n -> p t n")).then_inc(post_in, 16)
                sp.dma_start(gate, feat[F_GATE:F_GATE + RT].rearrange("t p n -> p t n")).then_inc(post_in, 16)

            @block.tensor
            def _(pe):
                def head_sum(b, src):
                    for o, c in CHUNKS:
                        ins = pe.matmul(ps[:, b * 2048 + o:b * 2048 + o + c], onesbd[:, :], src[:, o:o + c],
                                        start=True, stop=True)
                    return ins

                for f in range(RT):
                    if f:
                        pe.wait_ge(csq_ready, f)
                    head_sum(0, yacc[:, f]).then_inc(sum_psum, 1)
                    pe.wait_ge(csq_ready, f + 1)
                    if f:
                        pe.wait_ge(std_ready, f)
                    head_sum(1, csq[:, f % 2]).then_inc(var_psum, 1)

            @block.scalar
            def _(act):
                for f in range(RT):
                    act.wait_ge(var_psum, f + 1)
                    if f >= 2:
                        act.wait_ge(post_done, f - 1)
                    act.activation(inv_s[:, f % 2], ps[:, 2048:2048 + NT], ACT.Sqrt, bias=cst[:, 1:2],
                                   scale=1.0 / 64).then_inc(std_ready, 1)

            @block.vector
            def _(v):
                def centre(f):
                    v.wait_ge(sum_psum, f + 1)
                    if f >= 2:
                        v.wait_ge(var_psum, f - 1)
                    v.scalar_tensor_tensor(cen[:, f % 2], ps[:, 0:NT], -1.0 / 64, yacc[:, f], ALU.mult, ALU.add)
                    v.drain()
                    v.tensor_tensor(csq[:, f % 2], cen[:, f % 2], cen[:, f % 2], ALU.mult).then_inc(csq_ready, 1)

                centre(0)
                v.wait_ge(post_in, 32)
                for f in range(RT):
                    if f + 1 < RT:
                        centre(f + 1)
                    v.wait_ge(std_ready, f + 1)
                    v.reciprocal(inv_s[:, f % 2], inv_s[:, f % 2])
                    v.drain()
                    v.tensor_tensor(cen[:, f % 2], cen[:, f % 2], inv_s[:, f % 2], ALU.mult)
                    v.drain()
                    v.tensor_scalar(cen[:, f % 2], cen[:, f % 2], pars[:, P_LW + f:P_LW + f + 1],
                                    pars[:, P_LB + f:P_LB + f + 1], ALU.mult, ALU.add)
                    v.drain()
                    v.tensor_tensor(cen[:, f % 2], cen[:, f % 2], bonus[:, f], ALU.add)
                    v.drain()
                    v.tensor_tensor(yacc[:, f], cen[:, f % 2], gate[:, f], ALU.mult)
                    v.drain().then_inc(post_done, 1)

        wo = at(D_, KD, D)
        o8 = D_ + KD * D
        x6 = at(o8, 2, D)
        ot = at(o8 + 2 * D, 2, KD, P)
        h6 = at(o8 + 4 * D, 2, D)
        hT6 = at(o8 + 6 * D, 2, KD, P)
        o9 = o8 + 8 * D
        wr = at(o9, KD, NE)
        g2n = at(o9 + KD * NE, D)
        junk6 = at(o9 + KD * NE + D, D)
        logit = at(o9 + KD * NE + 2 * D, NTT, NE)
        lstat = at(o9 + KD * NE + 2 * D + NTT * NE, 2, NTT)
        aff = at(o9 + KD * NE + 2 * D + NTT * NE + 2 * NTT, NT)[0:NE]
        assert o9 + KD * NE + 2 * D + NTT * NE + 2 * NTT + NT <= E_ + 2 * KD * P + 2 * (NT + 3)
        RING = 6
        ring = [at(A_ + n * 4096, 4096) for n in range(RING)]
        wo_in = sem("wo_in")
        x6_in = [sem(f"x6_in{b}") for b in range(2)]
        ot_ready = sem("ot_ready")
        out_psum = sem("out_psum")
        x2_ready = sem("x2_ready")
        x2_stored = [sem(f"x2_stored{b}") for b in range(2)]
        h6_stored = [sem(f"h6_stored{b}") for b in range(2)]
        rms6_ready = sem("rms6_ready")
        h6_ready = sem("h6_ready")
        h6T_psum = sem("h6T_psum")
        h6T_ready = sem("h6T_ready")
        logit_psum = sem("logit_psum")
        logit_read = sem("logit_read")
        shift_ready = sem("shift_ready")
        exp_done = sem("exp_done")
        aff_ready = sem("aff_ready")
        affT_psum = sem("affT_psum")
        affT_read = sem("affT_read")
        w_in_ring = [sem(f"w_in_ring{n}") for n in range(RING)]

        def weight_chunk(k, e):
            if k < 8:
                w = (w_gate, w_up)[k % 2]
                return w[ds(e, 1), :, (k // 2) * 512:(k // 2 + 1) * 512].rearrange("o (k p) n -> p (o k) n", p=P)
            return w_down[ds(e, 1), (k - 8) * 512:(k - 7) * 512, :].rearrange("o (k p) n -> p (o k) n", p=P)

        def slot(k):
            return ring[k % RING].rearrange("p (a b) -> p a b", b=512 if k < 8 else D)

        with nc.Block() as block:
            @block.sync
            def _(sp):
                sp.dma_start(wo, w_out.rearrange("(k p) n -> p k n", p=P)).then_inc(wo_in, 16)
                sp.dma_start(wr, w_router.rearrange("(k p) n -> p k n", p=P)).then_inc(wo_in, 16)
                sp.dma_start(g2n, gains[1:2, :].partition_broadcast(P)).then_inc(wo_in, 16)
                for b in range(2):
                    sp.dma_start(x6[:, b], tokens[b * P:(b + 1) * P, :]).then_inc(x6_in[b], 16)
                for k in range(2):
                    sp.dma_start(slot(k), weight_chunk(k, 0)).then_inc(w_in_ring[k], 16)

                def store(j, b):
                    rows = ds((2 * j + b) * P, P)
                    sp.wait_ge(x2_ready, 2 * j + b + 1)
                    sp.dma_start(resid[rows, :], x6[:, b]).then_inc(x2_stored[b], 16)
                    sp.wait_ge(h6_ready, 2 * j + b + 1)
                    sp.dma_start(h2[rows, :], h6[:, b]).then_inc(h6_stored[b], 16)

                with sp.Fori(0, NTT // 2 - 1) as j:
                    for b in range(2):
                        store(j, b)
                        sp.wait_ge(x2_stored[b], 16 * j + 16)
                        sp.dma_start(x6[:, b], tokens[ds((2 * j + b + 2) * P, P), :]).then_inc(x6_in[b], 16)
                for b in range(2):
                    store(NTT // 2 - 1, b)
                for b in range(2):
                    sp.wait_ge(x2_stored[b], 16 * (NTT // 2))
                    sp.wait_ge(h6_stored[b], 16 * (NTT // 2) + 16)

            @block.gpsimd
            def _(pool):
                with pool.Fori(0, NTT // 2) as j:
                    for b in range(2):
                        pool.wait_ge(out_psum, 2 * j + b + 1)
                        pool.tensor_copy(ot[:, b], qk[:, :, ds((2 * j + b) * P, P)]).then_inc(ot_ready, 1)

            @block.tensor
            def _(pe):
                pe.drain().then_inc(out_psum, 2)
                pe.wait_ge(wo_in, 48)

                with pe.Fori(0, NTT // 2) as j:
                    for b in range(2):
                        pe.wait_ge(ot_ready, 2 * j + b + 1)
                        for half in range(2):
                            for k in range(KD):
                                ins = pe.matmul(bank(2 * b + half), ot[:, b, k],
                                                wo[:, k, half * 512:(half + 1) * 512],
                                                start=(k == 0), stop=(k == KD - 1))
                        ins.then_inc(out_psum, 1)
                    for b in range(2):
                        pe.wait_ge(h6_ready, 2 * j + b + 1)
                        for k in range(KD):
                            o = (4 + k // 4) * 512 + (k % 4) * P
                            ins = pe.transpose(ps[:, o:o + P], h6[:, b, k * P:(k + 1) * P], ident[:, :])
                        ins.then_inc(h6T_psum, 1)
                        pe.wait_ge(h6T_ready, 2 * j + b + 1)
                        pe.wait_ge(logit_read, 2 * j + b + 1)
                        for k in range(KD):
                            ins = pe.matmul(bank(6, NE), hT6[:, b, k], wr[:, k], start=(k == 0), stop=(k == KD - 1))
                        ins.then_inc(logit_psum, 1)
                pe.wait_ge(aff_ready, 1)
                for t in range(NTT):
                    if t >= 2:
                        pe.wait_ge(affT_read, t - 1)
                    pe.transpose(ps[0:NE, (t % 2) * 512:(t % 2) * 512 + P], logit[:, t], ident[:, :]).then_inc(affT_psum, 1)

            @block.scalar
            def _(act):
                act.drain().then_inc(logit_read, 1)
                with act.Fori(0, NTT // 2) as j:
                    for b in range(2):
                        act.wait_ge(x2_ready, 2 * j + b + 1)
                        act.activation(junk6, x6[:, b], ACT.Square, accum_out=small[:, b:b + 1])
                        act.drain()
                        act.activation(small[:, 2 + b:3 + b], small[:, b:b + 1], ACT.Sqrt,
                                       bias=cst[:, 0:1], scale=1.0 / D).then_inc(rms6_ready, 1)
                    for b in range(2):
                        act.wait_ge(h6T_psum, 2 * j + b + 1)
                        act.copy(hT6[:, b].rearrange("p a b -> p (a b)"),
                                 ps[:, 2048:2048 + D]).then_inc(h6T_ready, 1)
                        act.wait_ge(logit_psum, 2 * j + b + 1)
                        act.copy(logit[:, ds(2 * j + b, 1)].rearrange("p a b -> p (a b)"),
                                 bank(6, NE)).then_inc(logit_read, 1)
                act.wait_ge(shift_ready, 1)
                act.activation(logit.rearrange("p a b -> p (a b)"), logit.rearrange("p a b -> p (a b)"),
                               ACT.Exp).then_inc(exp_done, 1)
                for t in range(NTT):
                    act.wait_ge(affT_psum, t + 1)
                    act.copy(aff[:, t * P:(t + 1) * P],
                             ps[0:NE, (t % 2) * 512:(t % 2) * 512 + P]).then_inc(affT_read, 1)

            @block.vector
            def _(v):
                for b in range(2):
                    v.drain().then_inc(h6_stored[b], 16)
                v.wait_ge(wo_in, 48)
                with v.Fori(0, NTT // 2) as j:
                    for b in range(2):
                        v.wait_ge(out_psum, 2 * j + b + 3)
                        v.wait_ge(x6_in[b], 16 * j + 16)
                        v.tensor_tensor(x6[:, b], x6[:, b], ps[:, b * 1024:(b + 1) * 1024],
                                        ALU.add).then_inc(x2_ready, 1)
                    for b in range(2):
                        v.wait_ge(rms6_ready, 2 * j + b + 1)
                        v.reciprocal(small[:, 4 + b:5 + b], small[:, 2 + b:3 + b])
                        v.drain()
                        v.wait_ge(h6_stored[b], 16 * j + 16)
                        v.scalar_tensor_tensor(h6[:, b], x6[:, b], small[:, 4 + b:5 + b], g2n,
                                               ALU.mult, ALU.mult).then_inc(h6_ready, 1)
                        v.drain()
                v.wait_ge(logit_read, NTT + 1)
                v.tensor_reduce(lstat[:, 0], logit, AX, ALU.max)
                v.drain()
                v.tensor_tensor(logit, logit, lstat[:, 0].unsqueeze(2).broadcast_to([P, NTT, NE]), ALU.subtract)
                v.drain().then_inc(shift_ready, 1)
                v.wait_ge(exp_done, 1)
                v.tensor_reduce(lstat[:, 1], logit, AX, ALU.add)
                v.drain()
                v.reciprocal(lstat[:, 1], lstat[:, 1])
                v.drain()
                v.tensor_tensor(logit, logit, lstat[:, 1].unsqueeze(2).broadcast_to([P, NTT, NE]), ALU.mult)
                v.drain().then_inc(aff_ready, 1)

        o10 = D_
        val = at(o10, SLOTS)[0:NE]
        idx = sb("idx", [NE, SLOTS], U32)
        idxf = at(o10 + SLOTS, SLOTS)[0:NE]
        gsel = sb("gsel", [P, 2, NE])
        isel = sb("isel", [P, 2, NE + 1])
        icol = sb("icol", [P, 2, 2], U32)
        xe = at(o10 + 2 * SLOTS, D)
        xs = at(o10 + 2 * SLOTS + D, D)
        xT = at(o10 + 2 * SLOTS + 2 * D, KD, SLOTS)
        o11 = o10 + 2 * SLOTS + 2 * D + KD * SLOTS
        hid = at(o11, FF // P, SLOTS)
        sil = at(o11 + FF // P * SLOTS, 2, SLOTS)
        ye = at(o11 + (FF // P + 2) * SLOTS, D)
        ys = at(o11 + (FF // P + 2) * SLOTS + D, D)
        assert o11 + (FF // P + 2) * SLOTS + 2 * D <= o9
        NK = 12
        vi_ready = sem("vi_ready")
        vi_psum = sem("vi_psum")
        sel_ready = sem("sel_ready")
        icol_ready = sem("icol_ready")
        rows_in = sem("rows_in")
        xT_psum = sem("xT_psum")
        xT_ready = sem("xT_ready")
        gu_psum = sem("gu_psum")
        silu_ready = sem("silu_ready")
        hid_ready = sem("hid_ready")
        down_psum = sem("down_psum")
        y_gated = sem("y_gated")
        added = sem("added")
        rows_free = sem("rows_free")
        NFT = FF // P

        with nc.Block() as block:
            @block.sync
            def _(sp):
                for k in range(2, RING):
                    sp.dma_start(slot(k), weight_chunk(k, 0)).then_inc(w_in_ring[k], 16)

                def load(k, e):
                    if k >= RING:
                        sp.wait_ge(gu_psum, NFT * e + 4 * ((k - RING) // 2 + 1))
                    elif k < 2:
                        sp.wait_ge(gu_psum, NFT * e)
                    else:
                        sp.wait_ge(down_psum, 4 * e + (k - 5))
                    sp.dma_start(slot(k), weight_chunk(k, e)).then_inc(w_in_ring[k % RING], 16)

                for k in range(RING, NK):
                    load(k, 0)
                with sp.Fori(1, NE) as e:
                    for k in range(NK):
                        load(k, e)

            @block.gpsimd
            def _(pool):
                def gather(e):
                    pool.wait_ge(icol_ready, e + 1)
                    pool.wait_ge(xT_psum, e + 1)
                    pool.tensor_tensor(carry[0:1, 2:3], carry[0:1, 1:2], carry[0:1, 1:2], ALU.add)
                    pool.drain()
                    for g, (dst, n) in enumerate(((xe, CAP0), (xs, CAP1))):
                        pool.indirect_dma_start(dst[0:n], None, h2[:, :],
                                                bass.IndirectOffsetOnAxis(ap=icol[0:n, 0, g:g + 1], axis=0)
                                                ).then_inc(rows_in, 16)

                def add_rows(e):
                    pool.wait_ge(y_gated, e + 2)
                    pool.tensor_tensor(carry[0:1, 2:3], carry[0:1, 1:2], carry[0:1, 1:2], ALU.add)
                    pool.drain()
                    for g, (src, n) in enumerate(((ye, CAP0), (ys, CAP1))):
                        pool.indirect_dma_start(resid[:, :],
                                                bass.IndirectOffsetOnAxis(ap=icol[0:n, 1, g:g + 1], axis=0),
                                                src[0:n], None, compute_op=ALU.add).then_inc(added, 16)
                    pool.wait_ge(added, 32 * e + 32)
                    pool.tensor_tensor(carry[0:1, 2:3], carry[0:1, 1:2], carry[0:1, 1:2], ALU.add)
                    pool.drain()
                    pool.drain().then_inc(rows_free, 1)

                pool.drain().then_inc(rows_free, 1)
                gather(0)
                with pool.Fori(0, NE - 1) as e:
                    gather(e + 1)
                    add_rows(e)
                add_rows(NE - 1)

            @block.tensor
            def _(pe):
                pe.drain().then_inc(xT_psum, 1)
                pe.wait_ge(vi_ready, 1)
                for n, src in enumerate((val, idxf)):
                    pe.transpose(ps[:, n * 512:n * 512 + NE], src[:, 0:CAP0], ident[0:NE, 0:NE])
                    ins = pe.transpose(ps[0:CAP1, n * 512 + NE:n * 512 + 2 * NE], src[:, CAP0:SLOTS],
                                       ident[0:NE, 0:NE])
                ins.then_inc(vi_psum, 1)

                def turn(e):
                    pe.wait_ge(rows_in, 32 * e + 32)
                    for k in range(KD):
                        o = (5 + k // 3) * 512 + (k % 3) * SLOTS
                        pe.transpose(ps[:, o:o + CAP0], xe[:, k * P:(k + 1) * P], ident[:, :])
                        ins = pe.transpose(ps[:, o + CAP0:o + SLOTS], xs[0:CAP1, k * P:(k + 1) * P],
                                           ident[0:CAP1, 0:CAP1])
                    ins.then_inc(xT_psum, 1)

                def gate_up(e):
                    pe.wait_ge(xT_ready, e + 1)
                    for c in range(4):
                        for w in range(2):
                            k = 2 * c + w
                            pe.wait_ge(w_in_ring[k % RING], 32 * e + 16 * (k // RING + 1))
                        for f in range(4):
                            n = 4 * c + f
                            pe.wait_ge(hid_ready, NFT * e + (n + 1))
                            for w in range(2):
                                o = (n % 2) * 512 + w * SLOTS
                                for k in range(KD):
                                    ins = pe.matmul(ps[:, o:o + SLOTS], slot(2 * c + w)[:, k, f * P:(f + 1) * P],
                                                    xT[:, k], start=(k == 0), stop=(k == KD - 1))
                            ins.then_inc(gu_psum, 1)

                def down(e):
                    pe.wait_ge(y_gated, e + 1)
                    for c in range(4):
                        k = 8 + c
                        pe.wait_ge(w_in_ring[k % RING], 32 * e + 16 * (k // RING + 1))
                        for f in range(4):
                            n = 4 * c + f
                            pe.wait_ge(hid_ready, NFT * e + (n + 3))
                            for half in range(2):
                                pe.matmul(bank(2 + half), hid[:, n, 0:CAP0],
                                          slot(k)[:, f, half * 512:(half + 1) * 512],
                                          start=(n == 0), stop=(n == NFT - 1))
                            for q in range(4):
                                ins = pe.matmul(ps[32 * q:32 * q + 32, 4 * 512:4 * 512 + D // 4],
                                                hid[:, n, CAP0:SLOTS], slot(k)[:, f, q * 256:(q + 1) * 256],
                                                start=(n == 0), stop=(n == NFT - 1))
                        ins.then_inc(down_psum, 1)

                turn(0)
                with pe.Fori(0, NE - 1) as e:
                    gate_up(e)
                    turn(e + 1)
                    down(e)
                gate_up(NE - 1)
                down(NE - 1)

            @block.scalar
            def _(act):
                with act.Fori(0, NE) as e:
                    act.wait_ge(xT_psum, e + 2)
                    for k in range(0, KD, 3):
                        w = min(3, KD - k)
                        ins = act.copy(xT[:, k:k + w].rearrange("p a b -> p (a b)"),
                                       ps[:, (5 + k // 3) * 512:(5 + k // 3) * 512 + w * SLOTS])
                    ins.then_inc(xT_ready, 1)
                    for n in range(NFT):
                        act.wait_ge(gu_psum, NFT * e + (n + 1))
                        act.wait_ge(hid_ready, NFT * e + (n + 1))
                        act.activation(sil[:, n % 2], ps[:, (n % 2) * 512:(n % 2) * 512 + SLOTS],
                                       ACT.Silu).then_inc(silu_ready, 1)

            @block.vector
            def _(v):
                v.memset(isel[:, :, :].rearrange("p a b -> p (a b)"), 0.0)
                for first, n, o, cap in ((0, T0, 0, CAP0), (T0, T1, CAP0, CAP1)):
                    row = aff[:, first:first + n]
                    for r in range(cap // 8):
                        top = val[:, o + 8 * r:o + 8 * r + 8]
                        v.max(top, row)
                        v.drain()
                        v.max_index(idx[:, o + 8 * r:o + 8 * r + 8], top, row)
                        if r < cap // 8 - 1:
                            v.drain()
                            v.match_replace(row, top, row, -1.0)
                            v.drain()
                v.drain()
                v.tensor_copy(idxf, idx[:, :])
                v.drain()
                v.tensor_scalar(idxf[:, CAP0:SLOTS], idxf[:, CAP0:SLOTS], float(T0), None, ALU.add)
                v.drain().then_inc(vi_ready, 1)
                v.wait_ge(vi_psum, 1)
                for n, dst in enumerate((gsel, isel)):
                    v.tensor_copy(dst[:, 0, 0:NE], ps[:, n * 512:n * 512 + NE])
                    v.tensor_copy(dst[0:CAP1, 1, 0:NE], ps[0:CAP1, n * 512 + NE:n * 512 + 2 * NE])
                v.drain()
                v.tensor_copy(icol[:, 0, 0:1], isel[:, 0, 0:1])
                v.tensor_copy(icol[0:CAP1, 0, 1:2], isel[0:CAP1, 1, 0:1])
                v.drain().then_inc(icol_ready, 1)
                v.drain().then_inc(hid_ready, 2)
                v.drain().then_inc(y_gated, 1)
                with v.Fori(0, NE) as e:
                    v.wait_ge(rows_in, 32 * e + 32)
                    v.tensor_copy(icol[:, 0, 0:1], isel[:, 0, ds(e + 1, 1)])
                    v.tensor_copy(icol[0:CAP1, 0, 1:2], isel[0:CAP1, 1, ds(e + 1, 1)])
                    v.drain().then_inc(icol_ready, 1)
                    for n in range(NFT):
                        v.wait_ge(silu_ready, NFT * e + (n + 1))
                        v.tensor_tensor(hid[:, n], sil[:, n % 2],
                                        ps[:, (n % 2) * 512 + SLOTS:(n % 2) * 512 + 2 * SLOTS],
                                        ALU.mult).then_inc(hid_ready, 1)
                    v.wait_ge(rows_free, e + 1)
                    v.tensor_copy(icol[:, 1, 0:1], isel[:, 0, ds(e, 1)])
                    v.tensor_copy(icol[0:CAP1, 1, 1:2], isel[0:CAP1, 1, ds(e, 1)])
                    v.wait_ge(down_psum, 4 * e + 4)
                    v.tensor_scalar(ye, ps[:, 1024:2048], gsel[:, 0, ds(e, 1)], None, ALU.mult)
                    for q in range(4):
                        v.tensor_copy(ys[0:CAP1, q * 256:(q + 1) * 256], ps[32 * q:32 * q + 32, 2048:2048 + 256])
                    v.drain()
                    v.tensor_scalar(ys[0:CAP1], ys[0:CAP1], gsel[0:CAP1, 1, ds(e, 1)], None, ALU.mult)
                    v.drain().then_inc(y_gated, 1)

        xf = at(D_, 4, D)
        gf = at(D_ + 4 * D, D)
        jf = at(D_ + 5 * D, D)
        gf_in = sem("gf_in")
        xf_in = [sem(f"xf_in{b}") for b in range(4)]
        rmsf = sem("rmsf")
        yf_ready = sem("yf_ready")
        out_stored = [sem(f"out_stored{b}") for b in range(4)]

        with nc.Block() as block:
            @block.sync
            def _(sp):
                sp.dma_start(gf, gains[2:3, :].partition_broadcast(P)).then_inc(gf_in, 16)
                for t in range(NTT):
                    if t >= 4:
                        sp.wait_ge(out_stored[t % 4], 16 * (t // 4))
                    sp.dma_start(xf[:, t % 4], resid[t * P:(t + 1) * P, :]).then_inc(xf_in[t % 4], 16)
                    if t >= 2:
                        sp.wait_ge(yf_ready, t - 1)
                        sp.dma_start(out[(t - 2) * P:(t - 1) * P, :], xf[:, (t - 2) % 4]
                                     ).then_inc(out_stored[(t - 2) % 4], 16)
                for t in range(NTT - 2, NTT):
                    sp.wait_ge(yf_ready, t + 1)
                    sp.dma_start(out[t * P:(t + 1) * P, :], xf[:, t % 4]).then_inc(out_stored[t % 4], 16)
                for b in range(4):
                    sp.wait_ge(out_stored[b], 16 * len(range(b, NTT, 4)))

            @block.scalar
            def _(act):
                for t in range(NTT):
                    act.wait_ge(xf_in[t % 4], 16 * (t // 4 + 1))
                    act.activation(jf, xf[:, t % 4], ACT.Square, accum_out=small[:, t:t + 1])
                    act.drain()
                    act.activation(small[:, 16 + t:17 + t], small[:, t:t + 1], ACT.Sqrt,
                                   bias=cst[:, 0:1], scale=1.0 / D).then_inc(rmsf, 1)

            @block.vector
            def _(v):
                v.wait_ge(gf_in, 16)
                for t in range(NTT):
                    v.wait_ge(rmsf, t + 1)
                    v.reciprocal(small[:, 32 + t:33 + t], small[:, 16 + t:17 + t])
                    v.drain()
                    v.scalar_tensor_tensor(xf[:, t % 4], xf[:, t % 4], small[:, 32 + t:33 + t], gf,
                                           ALU.mult, ALU.mult).then_inc(yf_ready, 1)


def masks():
    row, col = np.arange(P)[:, None], np.arange(P)[None, :]
    block = row // C == col // C
    cols = [row == col, block]
    for d in range(2):
        before = row < col if d == 0 else row > col
        cols += [block & before, block & (before | (row == col))]
    for d in range(2):
        for m in LEVELS:
            same = row // (2 * m) == col // (2 * m)
            first, second = (row, col) if d == 0 else (col, row)
            cols.append(same & (first % (2 * m) < m) & (second % (2 * m) >= m))
    return np.concatenate([c.astype(np.float32) for c in cols], axis=1)


def kernel(**inputs):
    import concourse.bacc as bacc
    from concourse.bass_utils import run_bass_kernel_spmd

    x = {k: np.asarray(v) for k, v in inputs.items()}

    def tiles(a, n):
        a = a.reshape(-1, a.shape[-1])
        full = np.zeros((a.shape[0], n * P), np.float32)
        full[:, :a.shape[1]] = a
        return full.reshape(-1, P).T

    par = np.concatenate([tiles(x["shift_mu"][0], ZT)] + [tiles(x[k][0], RT) for k in ("w0", "a0")]
                         + [tiles(x[k][0].reshape(1, RW), RT) for k in ("k_k", "k_a", "r_k", "lnx_w", "lnx_b")], axis=1)
    dist = np.abs(np.arange(P)[:, None] - (np.arange(BIAS_W)[None, :] - (T0 - P))).astype(np.float32)
    arrays = {
        "tokens": np.concatenate([x["x_prompt"][0], x["x_sample"][0]], axis=0),
        "gains": np.stack([x["norm1_g"][0], x["norm2_g"][0], x["final_g"]]),
        "sub_g": x["subln_g"].reshape(1, P),
        "w_in": x["w_in"][0],
        "lam_qk": x["lambda_qk"].reshape(1, 256),
        "par": par,
        "w2": x["w2"][0], "a2": x["a2"][0], "g2": x["g2"][0],
        "w_out": x["w_out"][0], "w_router": x["w_router"][0],
        "w_gate": x["w_gate"][0], "w_up": x["w_up"][0], "w_down": x["w_down"][0],
        "c_bias": -dist,
        "c_mask": masks(),
    }
    arrays = {k: np.ascontiguousarray(v) for k, v in arrays.items()}
    nc = bacc.Bacc("TRN2", target_bir_lowering=False, num_devices=1)
    aps = [nc.dram_tensor(k, v.shape, mybir.dt.from_np(v.dtype), kind="ExternalInput").ap()
           for k, v in arrays.items()]
    out = nc.dram_tensor("out", (NT, D), mybir.dt.float32, kind="ExternalOutput").ap()
    build(nc, *aps, out)
    r = run_bass_kernel_spmd(nc, [arrays], core_ids=[0])
    y = r.results[0]["out"]
    return y[:T0].reshape(1, T0, D), y[T0:].reshape(1, T1, D)
```

```python
import math
from contextlib import ExitStack

import concourse.bass as bass
from concourse import mybir
import numpy as np

P = 128
D = 1024
KD = D // P
T0, T1 = 1024, 256
NT = T0 + T1
NTT = NT // P
HEADS_A = 4
AW = 512
RW = 512
RT = RW // P
LORA = 128
GATE = 96
IN_COLS = 3 * AW + 3 * RW + LORA + GATE
ZT = 3 * RT + 2
C = 64
NE = 16
FF = 2048
CAP0, CAP1 = 2 * T0 // NE, 2 * T1 // NE
SLOTS = CAP0 + CAP1
LAMBDA_INIT = 0.8 - 0.6 * math.exp(-0.3 * 0)
NORM_EPS, GN_EPS = 1e-6, 64e-5
DECAY = -math.exp(-0.5)
LEVELS = (1, 2, 4, 8, 16, 32)

CHUNKS = ((0, 512), (512, 512), (1024, 256))

F_R, F_K, F_V, F_KK, F_SIG, F_IC, F_BONUS, F_GATE = 0, 4, 8, 12, 16, 24, 32, 36
N_FEAT = 40

P_MU = 0
P_W0 = P_MU + 2 * ZT
P_A0 = P_W0 + 2 * RT
P_KK = P_A0 + 2 * RT
P_KA = P_KK + RT
P_RK = P_KA + RT
P_LW = P_RK + RT
P_LB = P_LW + RT
N_PAR = P_LB + RT

BIAS_W = T0 + T0 - P


def build(nc, tokens, gains, sub_g, w_in, lam_qk, par, w2, a2, g2, w_out, w_router,
          w_gate, w_up, w_down, c_bias, c_mask, out):
    F32 = mybir.dt.float32
    U32 = mybir.dt.uint32
    ALU = mybir.AluOpType
    ACT = mybir.ActivationFunctionType
    AX = mybir.AxisListType.X
    ds = bass.ds

    feat = nc.dram_tensor("feat", (N_FEAT, P, NT), F32).ap()
    resid = nc.dram_tensor("resid", (NT, D), F32).ap()
    h2 = nc.dram_tensor("h2", (NT, D), F32).ap()

    with ExitStack() as ctx:
        def sb(name, shape, dt=F32):
            return ctx.enter_context(nc.sbuf_tensor(name, shape, dt))

        ident = sb("ident", [P, P])
        onesbd = sb("onesbd", [P, P])
        causal = sb("causal", [P, 2, 2 * P])
        lvl = sb("lvl", [P, 2, len(LEVELS), P])
        pars = sb("pars", [P, N_PAR])
        muc = sb("muc", [P, ZT])
        cst = sb("cst", [P, 4])
        small = sb("small", [P, 64])
        subg = sb("subg", [P, P])
        restart = sb("restart", [P, RT * C])
        g2s = sb("g2s", [GATE, RW])
        lamr = sb("lamr", [P, 384])
        arena = sb("arena", [P, 48140])

        def at(off, *dims):
            n = int(np.prod(dims))
            v = arena[:, off:off + n]
            if len(dims) == 1:
                return v
            if len(dims) == 2:
                return v.rearrange("p (a b) -> p a b", b=dims[1])
            if len(dims) == 3:
                return v.rearrange("p (a b c) -> p a b c", b=dims[1], c=dims[2])
            return v.rearrange("p (a b c d) -> p a b c d", b=dims[1], c=dims[2], d=dims[3])

        A_, B_, C_, D_ = 0, 10240, 20480, 25600
        E_ = D_ + ZT * NT
        hT = at(A_, KD, NT)
        qk = at(B_, KD, NT)
        vt = at(C_, NTT, AW)
        zt = at(D_, ZT, NT)
        wb = at(E_, 2, KD, P)
        zpad = at(E_ + 2 * KD * P, 2, NT + 3)
        loraw = at(E_, 4 * RW)
        xt = at(D_, 2, D)
        hb = at(D_ + 2 * D, 2, D)
        junk = at(D_ + 4 * D, D)
        g1 = at(D_ + 5 * D, D)
        wv = at(D_ + 8 * D, KD, AW)

        ps = ctx.enter_context(nc.psum_tensor("ps", [P, 8 * 512], F32))

        carry = sb("carry", [P, 4])

        def bank(b, n=512):
            return ps[:, b * 512:b * 512 + n]


        sems = {}

        def sem(name):
            sems[name] = ctx.enter_context(nc.semaphore(name))
            return sems[name]

        consts_in = sem("consts_in")
        tables_in = sem("tables_in")
        eps_ready = sem("eps_ready")
        x_in = [sem(f"x_in{b}") for b in range(2)]
        x_free = [sem(f"x_free{b}") for b in range(2)]
        rms_ready = sem("rms_ready")
        h_ready = sem("h_ready")
        hT_psum = sem("hT_psum")
        hT_ready = sem("hT_ready")
        wv_in = sem("wv_in")
        v_psum = sem("v_psum")
        v_ready = sem("v_ready")
        w_in_in = [sem(f"w_in_in{b}") for b in range(2)]
        proj_psum = sem("proj_psum")
        proj_out = sem("proj_out")
        mix_done = sem("mix_done")
        n_consts = 3 * 16

        with nc.Block() as block:
            @block.sync
            def _(sp):
                sp.dma_start(ident[:, :], c_mask[:, 0:P]).then_inc(consts_in, 16)
                sp.dma_start(g1, gains[0:1, :].partition_broadcast(P)).then_inc(consts_in, 16)
                for b in range(2):
                    sp.dma_start(xt[:, b], tokens[b * P:(b + 1) * P, :]).then_inc(x_in[b], 16)
                sp.dma_start(wv, w_in[:, 2 * AW:3 * AW].rearrange("(k p) n -> p k n", p=P)).then_inc(wv_in, 16)
                sp.dma_start(pars[:, :], par).then_inc(consts_in, 16)
                with sp.Fori(1, NTT // 2) as j:
                    for b in range(2):
                        sp.wait_ge(x_free[b], j)
                        sp.dma_start(xt[:, b], tokens[ds((2 * j + b) * P, P), :]).then_inc(x_in[b], 16)
                for b in range(2):
                    sp.dma_start(wb[:, b], w_in[:, 3 * AW + b * P:3 * AW + (b + 1) * P]
                                 .rearrange("(k p) n -> p k n", p=P)).then_inc(w_in_in[b], 16)
                sp.dma_start(onesbd[:, :], c_mask[:, P:2 * P]).then_inc(tables_in, 16)
                sp.dma_start(subg[:, :], sub_g.partition_broadcast(P)).then_inc(tables_in, 16)
                sp.dma_start(causal[:, :, :].rearrange("p a b -> p (a b)"),
                             c_mask[:, 2 * P:6 * P]).then_inc(tables_in, 16)
                sp.dma_start(lvl[:, :, :, :].rearrange("p a b c -> p (a b c)"),
                             c_mask[:, 6 * P:(6 + 2 * len(LEVELS)) * P]).then_inc(tables_in, 16)
                sp.dma_start(lamr[:, 0:256], lam_qk.partition_broadcast(P)).then_inc(tables_in, 16)
                with sp.Fori(1, (ZT - 2) // 2) as j:
                    for b in range(2):
                        sp.wait_ge(proj_psum, 2 * j + b - 1)
                        sp.dma_start(wb[:, b], w_in[:, ds((2 * j + b) * P + 3 * AW, P)]
                                     .rearrange("(k p) n -> p k n", p=P)).then_inc(w_in_in[b], 16)
                sp.wait_ge(proj_psum, ZT - 3)
                sp.dma_start(wb[:, 0], w_in[:, 3 * AW + 12 * P:3 * AW + 13 * P]
                             .rearrange("(k p) n -> p k n", p=P)).then_inc(w_in_in[0], 16)
                sp.wait_ge(proj_psum, ZT - 2)
                sp.dma_start(wb[:, 1, :, 0:GATE], w_in[:, 3 * AW + 13 * P:IN_COLS]
                             .rearrange("(k p) n -> p k n", p=P)).then_inc(w_in_in[1], 16)
                with sp.Fori(0, 4) as j:
                    for b in range(2):
                        sp.wait_ge(proj_psum, 2 * j + (ZT + b - 1))
                        sp.dma_start(wb[:, b], w_in[:, ds((2 * j + b) * P, P)]
                                     .rearrange("(k p) n -> p k n", p=P)).then_inc(w_in_in[b], 16)

            @block.scalar
            def _(act):
                act.drain().then_inc(hT_ready, 2)
                act.wait_ge(eps_ready, 1)
                with act.Fori(0, NTT // 2) as j:
                    for b in range(2):
                        act.wait_ge(x_in[b], 16 * j + 16)
                        act.activation(junk, xt[:, b], ACT.Square, accum_out=small[:, b:b + 1])
                        act.drain()
                        act.activation(small[:, 2 + b:3 + b], small[:, b:b + 1], ACT.Sqrt,
                                       bias=cst[:, 0:1], scale=1.0 / D).then_inc(rms_ready, 1)
                    for b in range(2):
                        act.wait_ge(hT_psum, 2 * j + b + 3)
                        for half in range(2):
                            ins = act.copy(hT[:, 4 * half:4 * half + 4, ds((2 * j + b) * P, P)],
                                           ps[:, (2 * b + half) * 512:(2 * b + half + 1) * 512]
                                           .rearrange("p (a b) -> p a b", b=P))
                        ins.then_inc(hT_ready, 1)
                with act.Fori(0, NTT // 2) as j:
                    for b in range(2):
                        act.wait_ge(v_psum, 2 * j + b + 1)
                        act.copy(vt[:, ds(2 * j + b, 1), :].rearrange("p a b -> p (a b)"),
                                 bank(4 + b)).then_inc(v_ready, 1)
                with act.Fori(0, ZT // 2) as j:
                    for b in range(2):
                        act.wait_ge(proj_psum, 2 * j + b + 1)
                        act.wait_ge(mix_done, 2 * j + b + 1)
                        act.copy(zpad[:, b, 1:1 + T0], ps[:, b * 2048:b * 2048 + T0])
                        act.copy(zpad[:, b, 2 + T0:2 + NT],
                                 ps[:, b * 2048 + T0:b * 2048 + NT]).then_inc(proj_out, 1)
                with act.Fori(0, 4) as j:
                    for b in range(2):
                        act.wait_ge(proj_psum, 2 * j + (ZT + b + 1))
                        act.copy(qk[:, ds(2 * j + b, 1), :].rearrange("p a b -> p (a b)"),
                                 ps[:, b * 2048:b * 2048 + NT]).then_inc(proj_out, 1)

            @block.vector
            def _(v):
                v.memset(cst[:, 0:1], NORM_EPS)
                v.memset(carry[:, :], 0.0)
                v.memset(cst[:, 1:2], GN_EPS).then_inc(eps_ready, 1)
                v.memset(restart[:, :], 1.0)
                v.memset(zpad.rearrange("p a b -> p (a b)"), 0.0)
                v.drain()
                v.memset(restart[:, :].rearrange("p (a b) -> p a b", b=C)[:, :, 0:1], 0.0)
                v.drain().then_inc(mix_done, 2)
                v.wait_ge(consts_in, n_consts)
                with v.Fori(0, NTT // 2) as j:
                    for b in range(2):
                        v.wait_ge(rms_ready, 2 * j + b + 1)
                        v.reciprocal(small[:, 4 + b:5 + b], small[:, 2 + b:3 + b])
                        v.drain()
                        v.wait_ge(hT_psum, 2 * j + b + 1)
                        v.scalar_tensor_tensor(hb[:, b], xt[:, b], small[:, 4 + b:5 + b], g1,
                                               ALU.mult, ALU.mult).then_inc(h_ready, 1)
                        v.drain().then_inc(x_free[b], 1)
                v.tensor_tensor(muc[:, :], pars[:, P_MU:P_MU + ZT], pars[:, P_MU + ZT:P_MU + 2 * ZT], ALU.add)
                v.drain()
                v.tensor_scalar(muc[:, :], muc[:, :], -1.0, 1.0, ALU.mult, ALU.add)
                v.drain()
                v.wait_ge(v_psum, NTT)
                with v.Fori(0, ZT // 2) as j:
                    for b in range(2):
                        v.wait_ge(proj_out, 2 * j + b + 1)
                        v.tensor_copy(small[:, 8:9], muc[:, ds(2 * j + b, 1)])
                        v.tensor_copy(small[:, 9:10], pars[:, ds(2 * j + b + P_MU, 1)])
                        v.tensor_copy(small[:, 10:11], pars[:, ds(2 * j + b + P_MU + ZT, 1)])
                        v.drain()
                        for step in range(3):
                            for o, c, n in ((1, 0, T0), (T0 + 2, T0, T1)):
                                dst = zt[:, ds(2 * j + b, 1), c:c + n].rearrange("p a b -> p (a b)")
                                if step == 0:
                                    v.tensor_scalar(dst, zpad[:, b, o:o + n], small[:, 8:9], None, ALU.mult)
                                else:
                                    src = zpad[:, b, o - 1:o - 1 + n] if step == 1 else zpad[:, b, o + 1:o + 1 + n]
                                    v.scalar_tensor_tensor(dst, src, small[:, 8 + step:9 + step], dst,
                                                           ALU.mult, ALU.add)
                            if step < 2:
                                v.drain()
                        v.drain().then_inc(mix_done, 1)

            @block.tensor
            def _(pe):
                pe.drain().then_inc(hT_psum, 2)
                pe.wait_ge(consts_in, n_consts)
                with pe.Fori(0, NTT // 2) as j:
                    for b in range(2):
                        pe.wait_ge(h_ready, 2 * j + b + 1)
                        pe.wait_ge(hT_ready, 2 * j + b + 1)
                        for k in range(KD):
                            o = 2 * b * 512 + k * P
                            ins = pe.transpose(ps[:, o:o + P], hb[:, b, k * P:(k + 1) * P], ident[:, :])
                        ins.then_inc(hT_psum, 1)
                pe.wait_ge(wv_in, 16)
                pe.wait_ge(hT_ready, NTT + 2)
                for t in range(NTT):
                    if t >= 2:
                        pe.wait_ge(v_ready, t - 1)
                    for k in range(KD):
                        ins = pe.matmul(bank(4 + t % 2), hT[:, k, t * P:(t + 1) * P], wv[:, k, :],
                                        start=(k == 0), stop=(k == KD - 1))
                    ins.then_inc(v_psum, 1)
                pe.wait_ge(v_ready, NTT)

                def project(b):
                    for o, n in CHUNKS:
                        for k in range(KD):
                            ins = pe.matmul(ps[:, b * 2048 + o:b * 2048 + o + n], wb[:, b, k, :],
                                            hT[:, k, o:o + n], start=(k == 0), stop=(k == KD - 1))
                    ins.then_inc(proj_psum, 1)

                for b in range(2):
                    pe.wait_ge(w_in_in[b], 16)
                    project(b)
                with pe.Fori(1, ZT // 2 + 4) as j:
                    for b in range(2):
                        pe.wait_ge(w_in_in[b], 16 * j + 16)
                        pe.wait_ge(proj_out, 2 * j + b - 1)
                        project(b)

        sq = at(A_, 2, NT)
        ob = at(A_ + 2 * NT, 4, NT)
        tmp = at(A_ + 6 * NT, NT)
        lora_in = sem("lora_in")
        loraw_zero = sem("loraw_zero")
        tanh_done = sem("tanh_done")
        sq_ready = sem("sq_ready")
        pre_psum = sem("pre_psum")
        root_ready = sem("root_ready")
        pset_free = [sem(f"pset_free{b}") for b in range(2)]
        ob_full = [sem(f"ob_full{b}") for b in range(4)]
        ob_stored = [sem(f"ob_stored{b}") for b in range(4)]
        z_stored = sem("z_stored")
        items = [("kk", f, 0, F_KK + f) for f in range(RT)]
        for f in range(RT):
            items.append(("bonus", f, 0, F_BONUS + f))
            for d in range(2):
                items.append(("sig", f, d, F_SIG + RT * d + f))
                items.append(("ic", f, d, F_IC + RT * d + f))
            items.append(("gate", f, 0, F_GATE + f))
        n_sums = [sum(1 for x in items[:n] if x[0] in ("kk", "bonus")) for n in range(len(items) + 1)]
        Z_LORA, Z_GATE = 3 * RT, 3 * RT + 1

        with nc.Block() as block:
            @block.sync
            def _(sp):
                sp.wait_ge(loraw_zero, 1)
                for n, w in enumerate((w2[0], w2[1], a2[0], a2[1])):
                    sp.dma_start(loraw[32 * n:32 * n + 32, RW * n:RW * (n + 1)], w).then_inc(lora_in, 16)
                sp.dma_start(g2s[:, :], g2).then_inc(lora_in, 16)
                sp.dma_start(feat[0:3 * RT].rearrange("t p n -> p t n"), zt[:, 0:3 * RT, :]).then_inc(z_stored, 16)
                for n, (_, _, _, where) in enumerate(items):
                    sp.wait_ge(ob_full[n % 4], n // 4 + 1)
                    sp.dma_start(feat[where], ob[:, n % 4]).then_inc(ob_stored[n % 4], 16)
                for b in range(4):
                    sp.wait_ge(ob_stored[b], 16 * len(items[b::4]))
                sp.wait_ge(z_stored, 16)

            @block.tensor
            def _(pe):
                pe.wait_ge(tables_in, 5 * 16)
                pe.wait_ge(lora_in, 5 * 16)
                for n, (what, f, d, _) in enumerate(items):
                    if what in ("kk", "bonus"):
                        pe.wait_ge(sq_ready, n_sums[n + 1])
                    if n >= 2:
                        pe.wait_ge(pset_free[n % 2], n // 2)
                    if what in ("sig", "ic", "gate"):
                        pe.wait_ge(tanh_done, 1)
                    for o, c in CHUNKS:
                        dst = ps[:, (n % 2) * 2048 + o:(n % 2) * 2048 + o + c]
                        if what in ("kk", "bonus"):
                            ins = pe.matmul(dst, onesbd[:, :], sq[:, n_sums[n] % 2, o:o + c], start=True, stop=True)
                        elif what == "gate":
                            ins = pe.matmul(dst, g2s[:, f * P:(f + 1) * P], zt[0:GATE, Z_GATE, o:o + c],
                                            start=True, stop=True)
                        else:
                            w = (d if what == "sig" else 2 + d) * RW + f * P
                            ins = pe.matmul(dst, loraw[:, w:w + P], zt[:, Z_LORA, o:o + c], start=True, stop=True)
                    ins.then_inc(pre_psum, 1)

            @block.scalar
            def _(act):
                act.activation(zt[0:64, Z_LORA, :], zt[0:64, Z_LORA, :], ACT.Tanh)
                act.activation(zt[0:GATE, Z_GATE, :], zt[0:GATE, Z_GATE, :], ACT.Sigmoid).then_inc(tanh_done, 1)
                for n, (what, f, d, _) in enumerate(items):
                    src = ps[:, (n % 2) * 2048:(n % 2) * 2048 + NT]
                    if what == "bonus":
                        continue
                    act.wait_ge(pre_psum, n + 1)
                    if what == "kk":
                        act.activation(src, src, ACT.Sqrt).then_inc(root_ready, 1)
                        continue
                    if n >= 4:
                        act.wait_ge(ob_stored[n % 4], 16 * (n // 4))
                    if what == "gate":
                        act.copy(ob[:, n % 4], src)
                    else:
                        first = P_W0 if what == "sig" else P_A0
                        act.activation(ob[:, n % 4], src, ACT.Sigmoid,
                                       bias=pars[:, first + RT * d + f:first + RT * d + f + 1])
                    act.drain().then_inc(ob_full[n % 4], 1)
                    act.drain().then_inc(pset_free[n % 2], 1)

            @block.vector
            def _(v):
                v.memset(loraw, 0.0).then_inc(loraw_zero, 1)

                def operand(n):
                    what, f, _, _ = items[n]
                    if n_sums[n] >= 2:
                        last = [m for m in range(n) if items[m][0] in ("kk", "bonus")][-2]
                        v.wait_ge(pre_psum, last + 1)
                    dst = sq[:, n_sums[n] % 2]
                    if what == "kk":
                        v.tensor_scalar(dst, zt[:, RT + f], pars[:, P_KK + f:P_KK + f + 1], None, ALU.mult)
                        v.drain()
                        v.tensor_tensor(dst, dst, dst, ALU.mult).then_inc(sq_ready, 1)
                    else:
                        v.scalar_tensor_tensor(dst, zt[:, f], pars[:, P_RK + f:P_RK + f + 1], zt[:, RT + f],
                                               ALU.mult, ALU.mult).then_inc(sq_ready, 1)

                sums = [n for n in range(len(items)) if items[n][0] in ("kk", "bonus")]
                operand(sums[0])
                for s, n in enumerate(sums):
                    if s + 1 < len(sums):
                        operand(sums[s + 1])
                    what, f, _, _ = items[n]
                    src = ps[:, (n % 2) * 2048:(n % 2) * 2048 + NT]
                    if n >= 4:
                        v.wait_ge(ob_stored[n % 4], 16 * (n // 4))
                    if what == "kk":
                        v.wait_ge(root_ready, s + 1)
                        v.tensor_scalar(tmp, src, 1e-12, None, ALU.max)
                        v.drain()
                        v.reciprocal(tmp, tmp)
                        v.drain()
                        v.scalar_tensor_tensor(ob[:, n % 4], zt[:, RT + f], pars[:, P_KK + f:P_KK + f + 1], tmp,
                                               ALU.mult, ALU.mult)
                    else:
                        v.wait_ge(pre_psum, n + 1)
                        v.tensor_tensor(ob[:, n % 4], src, zt[:, 2 * RT + f], ALU.mult)
                    v.drain().then_inc(ob_full[n % 4], 1)
                    v.drain().then_inc(pset_free[n % 2], 1)

        qz = at(D_, 2, NT)
        sc = at(D_ + 2 * NT, 2, 2, T0)
        pd = at(D_ + 2 * NT + 4 * T0, 2, T0)
        pdT = at(D_ + 2 * NT + 6 * T0, 2, KD, P)
        oraw = at(D_ + 2 * NT + 8 * T0, HEADS_A, NTT, P)
        bias = at(A_, BIAS_W)
        ojunk = at(A_ + 2048, P)
        ostat = at(A_ + 2048 + P, 3, HEADS_A * NTT)
        srow = at(A_ + 2048 + 4 * P, 2, 8)
        bias_in = sem("bias_in")
        lam_exp = sem("lam_exp")
        lam_dot = sem("lam_dot")
        q_ready = sem("q_ready")
        scores_psum = sem("scores_psum")
        scores_read = sem("scores_read")
        probs_ready = sem("probs_ready")
        pd_ready = sem("pd_ready")
        pdT_psum = sem("pdT_psum")
        pdT_ready = sem("pdT_ready")
        o_psum = sem("o_psum")
        o_read = sem("o_read")
        ostat_root = sem("ostat_root")
        on_ready = sem("on_ready")
        oT_psum = sem("oT_psum")
        oT_read = sem("oT_read")
        NU = NTT
        units = [(0, T0, i) for i in range(T0 // P)] + [(T0, T1, i) for i in range(T1 // P)]

        with nc.Block() as block:
            @block.sync
            def _(sp):
                sp.dma_start(bias, c_bias).then_inc(bias_in, 16)

            @block.tensor
            def _(pe):
                with pe.Fori(0, HEADS_A) as h:
                    pe.wait_ge(q_ready, h + 1)

                    def scores(u):
                        t0, n, i = units[u]
                        for m in range(2):
                            pe.wait_ge(scores_read, 2 * NU * h + (2 * u + m + 1))
                            for o in range(0, n, 512):
                                w = min(512, n)
                                ins = pe.matmul(ps[:, m * T0 + o:m * T0 + o + w],
                                                qz[:, m, t0 + i * P:t0 + (i + 1) * P],
                                                qk[:, ds(h + HEADS_A, 1), t0 + o:t0 + o + w]
                                                .rearrange("p a b -> p (a b)"), start=True, stop=True)
                            ins.then_inc(scores_psum, 1)

                    def turn(u):
                        n = units[u][1]
                        pe.wait_ge(pd_ready, NU * h + (u + 1))
                        pe.wait_ge(pdT_ready, NU * h + (u + 1))
                        for k in range(n // P):
                            ins = pe.transpose(ps[:, 4 * 512 + k * P:4 * 512 + (k + 1) * P],
                                               pd[:, u % 2, k * P:(k + 1) * P], ident[:, :])
                        ins.then_inc(pdT_psum, 1)

                    def weigh(u):
                        t0, n, i = units[u]
                        pe.wait_ge(pdT_ready, NU * h + (u + 2))
                        pe.wait_ge(o_read, NU * h + (u + 1))
                        for k in range(n // P):
                            ins = pe.matmul(bank(6 + u % 2, P), pdT[:, u % 2, k, :],
                                            vt[:, t0 // P + k, ds(h * P, P)],
                                            start=(k == 0), stop=(k == n // P - 1))
                        ins.then_inc(o_psum, 1)

                    for s in range(NU + 3):
                        if s < NU:
                            scores(s)
                        if 2 <= s < NU + 2:
                            turn(s - 2)
                        if s >= 3:
                            weigh(s - 3)
                for n in range(HEADS_A):
                    for u in range(NU):
                        m = n * NU + u
                        pe.wait_ge(on_ready, m + 1)
                        if m >= 2:
                            pe.wait_ge(oT_read, m - 1)
                        pe.transpose(bank(m % 2, P), oraw[:, n, u], ident[:, :]).then_inc(oT_psum, 1)

            @block.scalar
            def _(act):
                act.drain().then_inc(pdT_ready, 1)
                act.drain().then_inc(o_read, 2)
                act.wait_ge(lam_dot, 1)
                act.activation(small[:, 18:20], small[:, 16:18], ACT.Exp).then_inc(lam_exp, 1)
                with act.Fori(0, HEADS_A) as h:
                    def probs(u):
                        t0, n, i = units[u]
                        for m in range(2):
                            act.wait_ge(scores_read, 2 * NU * h + (2 * u + m + 3))
                            act.activation(sc[:, u % 2, m, 0:n], sc[:, u % 2, m, 0:n], ACT.Exp,
                                           bias=srow[:, u % 2, m:m + 1],
                                           accum_out=srow[:, u % 2, 2 + m:3 + m]).then_inc(probs_ready, 1)

                    def keep_turned(u):
                        n = units[u][1]
                        act.wait_ge(pdT_psum, NU * h + (u + 1))
                        act.copy(pdT[:, u % 2, 0:n // P, :].rearrange("p a b -> p (a b)"),
                                 ps[:, 4 * 512:4 * 512 + n]).then_inc(pdT_ready, 1)

                    def keep_output(u):
                        act.wait_ge(o_psum, NU * h + (u + 1))
                        act.copy(oraw[:, ds(h, 1), u].rearrange("p a b -> p (a b)"), bank(6 + u % 2, P))
                        act.activation(ojunk, bank(6 + u % 2, P), ACT.Square,
                                       accum_out=ostat[:, 0, ds(h * NU + u, 1)])
                        act.drain().then_inc(o_read, 1)

                    for s in range(NU + 3):
                        if s < NU:
                            probs(s)
                        if 2 <= s < NU + 2:
                            keep_turned(s - 2)
                        if s >= 3:
                            keep_output(s - 3)
                act.activation(ostat[:, 1], ostat[:, 0], ACT.Sqrt, bias=cst[:, 0:1],
                               scale=1.0 / P).then_inc(ostat_root, 1)
                for n in range(HEADS_A):
                    for u in range(NU):
                        m = n * NU + u
                        act.wait_ge(oT_psum, m + 1)
                        act.copy(qk[:, n, u * P:(u + 1) * P], bank(m % 2, P)).then_inc(oT_read, 1)

            @block.vector
            def _(v):
                v.wait_ge(tables_in, 5 * 16)
                for n in range(2):
                    v.tensor_tensor(lamr[:, 256 + 64 * n:320 + 64 * n], lamr[:, 128 * n:128 * n + 64],
                                    lamr[:, 128 * n + 64:128 * n + 128], ALU.mult)
                v.drain()
                v.tensor_reduce(small[:, 16:18], lamr[:, 256:384].rearrange("p (a b) -> p a b", b=64),
                                AX, ALU.add).then_inc(lam_dot, 1)
                v.memset(qz.rearrange("p a b -> p (a b)"), 0.0)
                v.wait_ge(lam_exp, 1)
                v.tensor_tensor(small[:, 20:21], small[:, 19:20], small[:, 18:19], ALU.subtract)
                v.drain()
                v.tensor_scalar(cst[:, 2:3], small[:, 20:21], -LAMBDA_INIT, None, ALU.add)
                v.drain().then_inc(scores_read, 2)
                v.wait_ge(bias_in, 16)
                with v.Fori(0, HEADS_A) as h:
                    v.tensor_scalar(bias, bias, 0.25, None, ALU.mult)
                    for m in range(2):
                        v.tensor_scalar(qz[64 * m:64 * m + 64, m, :],
                                        qk[64 * m:64 * m + 64, ds(h, 1), :].rearrange("p a b -> p (a b)"),
                                        0.125, None, ALU.mult)
                    v.drain().then_inc(q_ready, 1)

                    def biased(u):
                        t0, n, i = units[u]
                        for m in range(2):
                            v.wait_ge(scores_psum, 2 * NU * h + (2 * u + m + 1))
                            v.tensor_copy(carry[0:1, 0:1], carry[0:1, 1:2])
                            w = T0 - P - i * P
                            v.tensor_tensor_reduce(sc[:, u % 2, m, 0:n], ps[:, m * T0:m * T0 + n],
                                                   bias[:, w:w + n], 1.0, -3.0e38, ALU.add, ALU.max,
                                                   small[:, 24 + m:25 + m])
                            v.drain()
                            v.tensor_scalar(srow[:, u % 2, m:m + 1], small[:, 24 + m:25 + m], -1.0, None,
                                            ALU.mult).then_inc(scores_read, 1)

                    def difference(u):
                        n = units[u][1]
                        v.wait_ge(probs_ready, 2 * NU * h + (2 * u + 2))
                        r = srow[:, u % 2]
                        v.reciprocal(r[:, 4:6], r[:, 2:4])
                        v.drain()
                        v.tensor_scalar(r[:, 5:6], r[:, 5:6], cst[:, 2:3], None, ALU.mult)
                        if u >= 2:
                            v.wait_ge(pdT_psum, NU * h + (u - 1))
                        v.tensor_scalar(pd[:, u % 2, 0:n], sc[:, u % 2, 0, 0:n], r[:, 4:5], None, ALU.mult)
                        v.drain()
                        v.scalar_tensor_tensor(pd[:, u % 2, 0:n], sc[:, u % 2, 1, 0:n], r[:, 5:6],
                                               pd[:, u % 2, 0:n], ALU.mult, ALU.add).then_inc(pd_ready, 1)
                        v.drain()

                    for s in range(NU + 1):
                        if s < NU:
                            biased(s)
                        if s >= 1:
                            difference(s - 1)
                    v.wait_ge(pdT_psum, NU * h + NU)
                    v.tensor_copy(carry[0:1, 0:1], carry[0:1, 1:2])
                v.wait_ge(ostat_root, 1)
                v.reciprocal(ostat[:, 2], ostat[:, 1])
                v.drain()
                v.tensor_scalar(ostat[:, 2], ostat[:, 2], 1.0 - LAMBDA_INIT, None, ALU.mult)
                v.drain()
                for n in range(HEADS_A):
                    for u in range(NU):
                        m = n * NU + u
                        v.scalar_tensor_tensor(oraw[:, n, u], oraw[:, n, u], ostat[:, 2, m:m + 1], subg[:, :],
                                               ALU.mult, ALU.mult).then_inc(on_ready, 1)

        yacc = at(B_ + RT * NT, RT, NT)
        R1, R2 = A_, C_
        cin = [at(R2 + d * 6 * RT * C, 6, RT * C) for d in range(2)]
        o2 = R2 + 12 * RT * C
        ext = [at(o2 + d * 7 * RT * C, 7, RT * C) for d in range(2)]
        o3 = o2 + 14 * RT * C
        o4 = o3 + RT * 10 * P
        o5 = o4 + RT * 8 * P
        o7 = o5 + RT * 4 * P
        bd_at = [[o + d * RT * 5 * P for o in (o3, o7)] for d in range(2)]
        ar_bd = [[at(o, RT, 2, P) for o in bd_at[d]] for d in range(2)]
        b_bd = [[at(o + RT * 2 * P, RT, P) for o in bd_at[d]] for d in range(2)]
        k_bd = [[at(o + RT * 3 * P, RT, P) for o in bd_at[d]] for d in range(2)]
        v_bd = [[at(o + RT * 4 * P, RT, P) for o in bd_at[d]] for d in range(2)]
        bm = [at(o4 + d * RT * 4 * P, RT, 2, P) for d in range(2)]
        km = [at(o4 + d * RT * 4 * P + RT * 2 * P, RT, 2, P) for d in range(2)]
        inv = [at(o5 + d * RT * 2 * P, RT, P) for d in range(2)]
        invT = [at(o5 + d * RT * 2 * P + RT * P, RT, P) for d in range(2)]
        assert o7 + RT * 10 * P <= E_ + 2 * KD * P + 2 * (NT + 3)
        alv = [at(R1 + d * 6 * RT * P, len(LEVELS), RT, P) for d in range(2)]
        o6 = R1 + 12 * RT * P
        tokb = [at(o6 + d * 4 * RT * P, RT, P) for d in range(2)]
        tokk = [at(o6 + d * 4 * RT * P + RT * P, RT, P) for d in range(2)]
        tokv = [at(o6 + d * 4 * RT * P + 2 * RT * P, RT, P) for d in range(2)]
        prod = [at(o6 + d * 4 * RT * P + 3 * RT * P, RT, P) for d in range(2)]
        assert o6 + 8 * RT * P <= B_
        state = [sb(f"state{d}", [P, RT, P]) for d in range(2)]
        eb = sb("eb", [P, 2, 2, RT])

        cin_in = [sem(f"cin_in{d}") for d in range(2)]
        cin_free = [sem(f"cin_free{d}") for d in range(2)]
        cum_ready = [sem(f"cum_ready{d}") for d in range(2)]
        exp_ready = [sem(f"exp_ready{d}") for d in range(2)]
        vbd_ready = [sem(f"vbd_ready{d}") for d in range(2)]
        bd_ready = [sem(f"bd_ready{d}") for d in range(2)]
        pairs_psum = [sem(f"pairs_psum{d}") for d in range(2)]
        masks_ready = [sem(f"masks_ready{d}") for d in range(2)]
        first_psum = [sem(f"first_psum{d}") for d in range(2)]
        lvl_masked = [sem(f"lvl_masked{d}") for d in range(2)]
        tok_psum = [sem(f"tok_psum{d}") for d in range(2)]
        tok_read = [sem(f"tok_read{d}") for d in range(2)]
        inv_ready = [sem(f"inv_ready{d}") for d in range(2)]
        ax_psum = [sem(f"ax_psum{d}") for d in range(2)]
        prod_ready = [sem(f"prod_ready{d}") for d in range(2)]
        xax_psum = [sem(f"xax_psum{d}") for d in range(2)]
        state_ready = [sem(f"state_ready{d}") for d in range(2)]
        invT_final = [sem(f"invT_final{d}") for d in range(2)]
        g_psum = [sem(f"g_psum{d}") for d in range(2)]
        u_psum = [sem(f"u_psum{d}") for d in range(2)]
        y_psum = [sem(f"y_psum{d}") for d in range(2)]
        y_read = [sem(f"y_read{d}") for d in range(2)]
        NL = len(LEVELS) - 1
        NTOK = 3
        SEGS = ((0, T0 // C, 0, T0 // C // 2), (T0, T1 // C, T0 // C, T1 // C // 2 - 1))
        LAST = T1 // C - 2

        with nc.Block() as block:
            @block.sync
            def _(sp):
                for t0, nch, c0, _pairs in SEGS:
                    with sp.Fori(0, nch) as n:
                        for d in range(2):
                            first = n * C + t0 if d == 0 else (nch - 1) * C + t0 - n * C
                            sp.wait_ge(cin_free[d], 1)
                            sp.wait_ge(cin_free[d], n + (c0 + 1))
                            sp.wait_ge(vbd_ready[d], n + (c0 + 1))
                            for q, t in ((0, F_R), (1, F_K), (2, F_V), (3, F_KK),
                                         (4, F_SIG + RT * d), (5, F_IC + RT * d)):
                                sp.dma_start(cin[d][:, q].rearrange("p (a b) -> p a b", b=C),
                                             feat[t:t + RT, :, ds(first, C)].rearrange("t p n -> p t n")
                                             ).then_inc(cin_in[d], 16)

            @block.gpsimd
            def _(pool):
                def mask_levels(n, c0):
                    for levels in ((1,), range(2, NL + 1)):
                        for d in range(2):
                            pool.wait_ge(masks_ready[d], 3 * n + (3 * c0 + 1))
                            for l in levels:
                                pool.tensor_tensor(alv[d][:, l], bm[d][:, :, 0],
                                                   lvl[:, d, l:l + 1, :].broadcast_to([P, RT, P]),
                                                   ALU.mult).then_inc(lvl_masked[d], 1)

                for t0, nch, c0, pairs in SEGS:
                    with pool.Fori(0, pairs) as i:
                        for par in range(2):
                            mask_levels(i * 2 + par, c0)
                for par in range(2):
                    mask_levels(LAST + par, c0)

            @block.tensor
            def _(pe):
                def pb(d, b, p):
                    return ps[:, (4 * d + b) * 512 + p * P:(4 * d + b) * 512 + (p + 1) * P]

                def chunk(n, par, c0):
                    for d in range(2):
                        pe.wait_ge(bd_ready[d], n + (c0 + 1))
                        pe.wait_ge(y_read[d], n + (c0 + 1))
                        for p in range(RT):
                            o = (4 * d + p // 2) * 512 + (p % 2) * 2 * P
                            ins = pe.matmul(ps[:, o:o + 2 * P], b_bd[d][par][:, p],
                                            ar_bd[d][par][:, p].rearrange("p a b -> p (a b)"),
                                            start=True, stop=True)
                        ins.then_inc(pairs_psum[d], 1)
                    for d in range(2):
                        for p in range(RT):
                            o = (4 * d + 2 + p // 2) * 512 + (p % 2) * 2 * P
                            ins = pe.matmul(ps[:, o:o + 2 * P], k_bd[d][par][:, p],
                                            ar_bd[d][par][:, p].rearrange("p a b -> p (a b)"),
                                            start=True, stop=True)
                        ins.then_inc(pairs_psum[d], 1)
                    for d in range(2):
                        pe.wait_ge(masks_ready[d], 3 * n + (3 * c0 + 2))
                        for p in range(RT):
                            ins = pe.transpose(pb(d, 0, p), invT[d][:, p], ident[:, :])
                        ins.then_inc(first_psum[d], 1)
                    for l in range(1, NL + 1):
                        for d in range(2):
                            pe.wait_ge(inv_ready[d], NL * n + (NL * c0 + l))
                            pe.wait_ge(lvl_masked[d], NL * n + (NL * c0 + l))
                            for p in range(RT):
                                ins = pe.matmul(pb(d, 0, p), alv[d][:, l, p], inv[d][:, p],
                                                start=True, stop=True)
                            ins.then_inc(ax_psum[d], 1)
                        if l <= NTOK:
                            for d in range(2):
                                if l == 1:
                                    pe.wait_ge(vbd_ready[d], n + (c0 + 2))
                                    pe.wait_ge(masks_ready[d], 3 * n + (3 * c0 + 3))
                                else:
                                    pe.wait_ge(tok_read[d], NTOK * n + (NTOK * c0 + l - 1))
                                m = (v_bd, b_bd, k_bd)[l - 1]
                                for p in range(RT):
                                    ins = pe.transpose(pb(d, 3, p), m[d][par][:, p], ident[:, :])
                                ins.then_inc(tok_psum[d], 1)
                        for d in range(2):
                            pe.wait_ge(prod_ready[d], (NL + 2) * n + ((NL + 2) * c0 + l))
                            if l == 1:
                                pe.wait_ge(masks_ready[d], 3 * n + (3 * c0 + 3))
                            for p in range(RT):
                                if l < NL:
                                    pe.matmul(pb(d, 1, p), invT[d][:, p], prod[d][:, p],
                                              start=True, stop=True)
                                ins = pe.matmul(pb(d, 2, p), prod[d][:, p], invT[d][:, p],
                                                start=True, stop=True)
                            ins.then_inc(xax_psum[d], 1)
                    for d in range(2):
                        pe.wait_ge(state_ready[d], n + (c0 + 1))
                        pe.wait_ge(tok_read[d], NTOK * n + (NTOK * c0 + NTOK))
                        for p in range(RT):
                            pe.matmul(pb(d, 3, p), ar_bd[d][par][:, p, 0], state[d][:, p],
                                      start=True, stop=False)
                            ins = pe.matmul(pb(d, 3, p), km[d][:, p, 0], tokv[d][:, p], start=False, stop=True)
                        ins.then_inc(g_psum[d], 1)
                    for d in range(2):
                        pe.wait_ge(prod_ready[d], (NL + 2) * n + ((NL + 2) * c0 + NL + 1))
                        pe.wait_ge(invT_final[d], n + (c0 + 1))
                        for p in range(RT):
                            ins = pe.matmul(pb(d, 0, p), invT[d][:, p], prod[d][:, p], start=True, stop=True)
                        ins.then_inc(u_psum[d], 1)
                    for d in range(2):
                        for p in range(RT):
                            pe.matmul(pb(d, 1, p), state[d][:, p], ar_bd[d][par][:, p, 1],
                                      start=True, stop=False)
                            pe.matmul(pb(d, 1, p), tokv[d][:, p], km[d][:, p, 1], start=False, stop=False)
                            if p == 0:
                                pe.wait_ge(prod_ready[d], (NL + 2) * n + ((NL + 2) * c0 + NL + 2))
                            pe.matmul(pb(d, 1, p), prod[d][:, p], bm[d][:, p, 1], start=False, stop=True)
                            pe.matmul(pb(d, 2, p), tokb[d][:, p], prod[d][:, p], start=True, stop=False)
                            ins = pe.matmul(pb(d, 2, p), tokk[d][:, p], tokv[d][:, p], start=False, stop=True)
                        ins.then_inc(y_psum[d], 1)

                for t0, nch, c0, pairs in SEGS:
                    with pe.Fori(0, pairs) as i:
                        for par in range(2):
                            chunk(i * 2 + par, par, c0)
                for par in range(2):
                    chunk(LAST + par, par, c0)

            @block.scalar
            def _(act):
                def decays(n, par, c0, d):
                    s = -1.0 if d else 1.0
                    cum, exc = ext[d][:, 0], ext[d][:, 1]
                    act.wait_ge(cum_ready[d], n + (c0 + 1))
                    for slot, src, sign in (((2, exc, 1), (3, cum, 1), (4, cum, -1)) if d == 0 else
                                            ((2, cum, -1), (3, exc, -1), (4, exc, 1))):
                        act.activation(ext[d][:, slot], src, ACT.Exp, scale=sign * DECAY)
                    act.activation(eb[:, par, d, :].unsqueeze(2),
                                   cum.rearrange("p (a b) -> p a b", b=C)[:, :, C - 1:C],
                                   ACT.Exp, scale=DECAY).then_inc(exp_ready[d], 1)

                def v_blocks(par, d):
                    for hh in range(2):
                        r = slice(64 * hh, 64 * hh + 64)
                        ins = act.copy(v_bd[d][par][r, :, 64 * hh:64 * hh + 64],
                                       cin[d][r, 2].rearrange("p (a b) -> p a b", b=C))
                    ins.then_inc(vbd_ready[d], 1)

                def chunk(n, par, c0, more):
                    for d in range(2):
                        act.wait_ge(first_psum[d], n + (c0 + 1))
                        act.copy(inv[d].rearrange("p a b -> p (a b)"), bank(4 * d)).then_inc(inv_ready[d], 1)
                    for l in range(1, NL + 1):
                        for d in range(2):
                            act.wait_ge(ax_psum[d], NL * n + (NL * c0 + l))
                            act.copy(prod[d].rearrange("p a b -> p (a b)"),
                                     bank(4 * d)).then_inc(prod_ready[d], 1)
                        if l <= NTOK:
                            for d in range(2):
                                act.wait_ge(tok_psum[d], NTOK * n + (NTOK * c0 + l))
                                m = (tokv, tokb, tokk)[l - 1]
                                act.copy(m[d].rearrange("p a b -> p (a b)"),
                                         bank(4 * d + 3)).then_inc(tok_read[d], 1)
                        if more and l in (2, 3):
                            decays(n + 1, 1 - par, c0, l - 2)
                        if more and l == 4:
                            for d in range(2):
                                v_blocks(1 - par, d)
                    for d in range(2):
                        act.wait_ge(g_psum[d], n + (c0 + 1))
                        act.copy(prod[d].rearrange("p a b -> p (a b)"),
                                 bank(4 * d + 3)).then_inc(prod_ready[d], 1)
                    for d in range(2):
                        act.wait_ge(u_psum[d], n + (c0 + 1))
                        act.copy(prod[d].rearrange("p a b -> p (a b)"),
                                 bank(4 * d)).then_inc(prod_ready[d], 1)

                for d in range(2):
                    act.drain().then_inc(vbd_ready[d], 1)
                for d in range(2):
                    decays(0, 0, 0, d)
                    v_blocks(0, d)
                for t0, nch, c0, pairs in SEGS:
                    with act.Fori(0, pairs) as i:
                        for par in range(2):
                            chunk(i * 2 + par, par, c0, True)
                for par in range(2):
                    chunk(LAST + par, par, c0, par == 0)

            @block.vector
            def _(v):
                def tiles(x):
                    return x.rearrange("p (a b) -> p a b", b=C)

                def sums(n, c0, d):
                    r_, k_, v_, kk_, sig_, ic_ = (cin[d][:, q] for q in range(6))
                    cum, exc, ea, er, ebk, t1, t2 = (ext[d][:, q] for q in range(7))
                    v.wait_ge(cin_in[d], 96 * n + (96 * c0 + 96))
                    v.tensor_tensor_scan(cum, restart[:, :], sig_, 0.0, ALU.mult, ALU.add)
                    v.tensor_tensor(t1, kk_, ic_, ALU.mult)
                    v.scalar_tensor_tensor(
                        tiles(t2), tiles(ic_), -1.0,
                        pars[:, P_KA:P_KA + RT].unsqueeze(2).broadcast_to([P, RT, C]), ALU.add, ALU.mult)
                    v.drain()
                    v.tensor_tensor(exc, cum, sig_, ALU.subtract).then_inc(cum_ready[d], 1)
                    v.scalar_tensor_tensor(t2, t2, 1.0, k_, ALU.add, ALU.mult)
                    v.drain()

                def blocks(n, par, c0, d):
                    r_, k_, v_, kk_, sig_, ic_ = (cin[d][:, q] for q in range(6))
                    cum, exc, ea, er, ebk, t1, t2 = (ext[d][:, q] for q in range(7))
                    v.wait_ge(exp_ready[d], n + (c0 + 1))
                    for hh in range(2):
                        r = slice(64 * hh, 64 * hh + 64)
                        c = slice(64 * hh, 64 * hh + 64)
                        v.scalar_tensor_tensor(ar_bd[d][par][r, :, 0, c], tiles(kk_)[r], -1.0, tiles(ea)[r],
                                               ALU.mult, ALU.mult)
                        v.tensor_tensor(ar_bd[d][par][r, :, 1, c], tiles(r_)[r], tiles(er)[r], ALU.mult)
                        v.tensor_tensor(b_bd[d][par][r, :, c], tiles(t1)[r], tiles(ebk)[r], ALU.mult)
                        v.tensor_tensor(k_bd[d][par][r, :, c], tiles(t2)[r], tiles(ebk)[r], ALU.mult)
                    v.drain().then_inc(bd_ready[d], 1)
                    v.drain().then_inc(cin_free[d], 1)

                def mask_pairs(d, m, b):
                    for half in range(2):
                        v.tensor_tensor(m[d][:, 2 * half:2 * half + 2].rearrange("p a b c -> p a (b c)"),
                                        bank(4 * d + b + half).rearrange("p (a b) -> p a b", b=2 * P),
                                        causal[:, d:d + 1, :].broadcast_to([P, 2, 2 * P]), ALU.mult)

                def chunk(n, par, t0, nch, c0, more):
                    for d in range(2):
                        v.drain().then_inc(state_ready[d], 1)
                    for d in range(2):
                        v.wait_ge(pairs_psum[d], 2 * n + (2 * c0 + 1))
                        mask_pairs(d, bm, 0)
                        v.drain().then_inc(masks_ready[d], 1)
                        v.tensor_tensor(alv[d][:, 0], bm[d][:, :, 0],
                                        lvl[:, d, 0:1, :].broadcast_to([P, RT, P]), ALU.mult)
                        v.drain()
                        v.tensor_tensor(invT[d], alv[d][:, 0],
                                        ident[:, :].unsqueeze(1).broadcast_to([P, RT, P]),
                                        ALU.add).then_inc(masks_ready[d], 1)
                    for d in range(2):
                        v.wait_ge(pairs_psum[d], 2 * n + (2 * c0 + 2))
                        mask_pairs(d, km, 2)
                        v.drain().then_inc(masks_ready[d], 1)
                    for l in range(1, NL + 1):
                        for d in range(2):
                            v.wait_ge(xax_psum[d], NL * n + (NL * c0 + l))
                            if l < NL:
                                v.tensor_tensor(inv[d].rearrange("p a b -> p (a b)"),
                                                inv[d].rearrange("p a b -> p (a b)"), bank(4 * d + 1), ALU.add)
                            v.tensor_tensor(invT[d].rearrange("p a b -> p (a b)"),
                                            invT[d].rearrange("p a b -> p (a b)"), bank(4 * d + 2), ALU.add)
                            v.drain().then_inc(inv_ready[d] if l < NL else invT_final[d], 1)
                        if more and l in (1, 2):
                            sums(n + 1, c0, l - 1)
                        if more and l in (3, 4):
                            blocks(n + 1, 1 - par, c0, l - 3)
                    for d in range(2):
                        v.wait_ge(y_psum[d], n + (c0 + 1))
                        v.tensor_copy(carry[0:1, 0:1], carry[0:1, 1:2])
                        for hh in range(2):
                            r = slice(64 * hh, 64 * hh + 64)
                            first = n * C + t0 if d == 0 else (nch - 1) * C + t0 - n * C
                            y = yacc[r, :, ds(first, C)]
                            v.tensor_tensor(y, y, bank(4 * d + 1).rearrange("p (a b) -> p a b", b=P)
                                            [r, :, 64 * hh:64 * hh + 64], ALU.add)
                        v.tensor_tensor(state[d][:, :, :].rearrange("p a b -> p (a b)"),
                                        state[d][:, :, :].rearrange("p a b -> p (a b)"),
                                        bank(4 * d + 2), ALU.add)
                        v.drain().then_inc(y_read[d], 1)
                        if d == 0 or more:
                            v.tensor_tensor(state[d][:, :, :], state[d][:, :, :],
                                            eb[:, par if d == 0 else 1 - par, d, :].unsqueeze(2)
                                            .broadcast_to([P, RT, P]), ALU.mult)
                    v.drain()

                v.memset(at(o3, RT * 10 * P), 0.0)
                v.memset(at(o7, RT * 10 * P), 0.0)
                v.memset(yacc.rearrange("p a b -> p (a b)"), 0.0)
                v.drain()
                for d in range(2):
                    v.drain().then_inc(cin_free[d], 1)
                    v.drain().then_inc(y_read[d], 1)
                for d in range(2):
                    sums(0, 0, d)
                for d in range(2):
                    blocks(0, 0, 0, d)
                for t0, nch, c0, pairs in SEGS:
                    for d in range(2):
                        v.memset(state[d][:, :, :].rearrange("p a b -> p (a b)"), 0.0)
                    v.drain()
                    with v.Fori(0, pairs) as i:
                        for par in range(2):
                            chunk(i * 2 + par, par, t0, nch, c0, True)
                for par in range(2):
                    chunk(LAST + par, par, t0, nch, c0, par == 0)

        bonus = at(A_, RT, NT)
        gate = at(R2, RT, NT)
        cen = at(A_ + RT * NT, 2, NT)
        csq = at(A_ + (RT + 2) * NT, 2, NT)
        wo = at(D_, KD, D)
        o8 = D_ + KD * D
        x6 = at(o8, 2, D)
        ot = at(o8 + 2 * D, 2, KD, P)
        h6 = at(o8 + 4 * D, 2, D)
        hT6 = at(o8 + 6 * D, 2, KD, P)
        o9 = o8 + 8 * D
        wr = at(o9, KD, NE)
        g2n = at(o9 + KD * NE, D)
        junk6 = at(o9 + KD * NE + D, D)
        logit = at(o9 + KD * NE + 2 * D, NTT, NE)
        lstat = at(o9 + KD * NE + 2 * D + NTT * NE, 2, NTT)
        aff = at(o9 + KD * NE + 2 * D + NTT * NE + 2 * NTT, NT)[0:NE]
        assert o9 + KD * NE + 2 * D + NTT * NE + 2 * NTT + NT <= E_ + 2 * KD * P + 2 * (NT + 3)
        inv_s = at(o9 + KD * NE + D, 2, NT)
        assert o9 + KD * NE + D + 2 * NT <= E_ + 2 * KD * P + 2 * (NT + 3)
        post_in = sem("post_in")
        wo_in = sem("wo_in")
        x6_in = [sem(f"x6_in{b}") for b in range(2)]
        normed_ready = sem("normed_ready")
        sum_psum = sem("sum_psum")
        centred = sem("centred")
        var_psum = sem("var_psum")
        std_ready = sem("std_ready")
        post_done = sem("post_done")

        with nc.Block() as block:
            @block.sync
            def _(sp):
                sp.dma_start(bonus, feat[F_BONUS:F_BONUS + RT].rearrange("t p n -> p t n")).then_inc(post_in, 16)
                sp.dma_start(gate, feat[F_GATE:F_GATE + RT].rearrange("t p n -> p t n")).then_inc(post_in, 16)
                sp.dma_start(wo, w_out.rearrange("(k p) n -> p k n", p=P)).then_inc(wo_in, 16)
                sp.dma_start(wr, w_router.rearrange("(k p) n -> p k n", p=P)).then_inc(wo_in, 16)
                sp.dma_start(g2n, gains[1:2, :].partition_broadcast(P)).then_inc(wo_in, 16)
                for b in range(2):
                    sp.dma_start(x6[:, b], tokens[b * P:(b + 1) * P, :]).then_inc(x6_in[b], 16)

            @block.gpsimd
            def _(pool):
                pool.wait_ge(post_in, 32)
                for f in range(RT):
                    pool.wait_ge(normed_ready, f + 1)
                    pool.tensor_tensor(yacc[:, f], cen[:, f % 2], gate[:, f], ALU.mult).then_inc(post_done, 1)

            @block.tensor
            def _(pe):
                def head_sum(b, src):
                    for o, c in CHUNKS:
                        ins = pe.matmul(ps[:, b * 2048 + o:b * 2048 + o + c], onesbd[:, :], src[:, o:o + c],
                                        start=True, stop=True)
                    return ins

                for f in range(RT):
                    if f:
                        pe.wait_ge(centred, f)
                    head_sum(0, yacc[:, f]).then_inc(sum_psum, 1)
                    pe.wait_ge(std_ready, 2 * f + 1)
                    head_sum(1, csq[:, f % 2]).then_inc(var_psum, 1)

            @block.scalar
            def _(act):
                for f in range(RT):
                    act.wait_ge(centred, f + 1)
                    act.activation(csq[:, f % 2], cen[:, f % 2], ACT.Square).then_inc(std_ready, 1)
                    act.wait_ge(var_psum, f + 1)
                    if f >= 2:
                        act.wait_ge(normed_ready, f - 1)
                    act.activation(inv_s[:, f % 2], ps[:, 2048:2048 + NT], ACT.Sqrt, bias=cst[:, 1:2],
                                   scale=1.0 / 64).then_inc(std_ready, 1)

            @block.vector
            def _(v):
                def centre(f):
                    v.wait_ge(sum_psum, f + 1)
                    if f >= 2:
                        v.wait_ge(post_done, f - 1)
                    v.scalar_tensor_tensor(cen[:, f % 2], ps[:, 0:NT], -1.0 / 64, yacc[:, f],
                                           ALU.mult, ALU.add).then_inc(centred, 1)

                centre(0)
                v.wait_ge(post_in, 32)
                for f in range(RT):
                    if f + 1 < RT:
                        centre(f + 1)
                    v.wait_ge(std_ready, 2 * f + 2)
                    v.reciprocal(inv_s[:, f % 2], inv_s[:, f % 2])
                    v.drain()
                    v.scalar_tensor_tensor(cen[:, f % 2], cen[:, f % 2], pars[:, P_LW + f:P_LW + f + 1],
                                           inv_s[:, f % 2], ALU.mult, ALU.mult)
                    v.drain()
                    v.scalar_tensor_tensor(cen[:, f % 2], cen[:, f % 2], pars[:, P_LB + f:P_LB + f + 1],
                                           bonus[:, f], ALU.add, ALU.add).then_inc(normed_ready, 1)

        RING = 6
        AHEAD = 5
        WCH = 2048
        ring = [at(A_ + n * WCH, WCH) for n in range(RING)]
        ot_ready = sem("ot_ready")
        out_psum = sem("out_psum")
        x2_ready = sem("x2_ready")
        x2_stored = [sem(f"x2_stored{b}") for b in range(2)]
        h6_stored = [sem(f"h6_stored{b}") for b in range(2)]
        rms6_ready = sem("rms6_ready")
        h6_ready = sem("h6_ready")
        h6T_psum = sem("h6T_psum")
        h6T_ready = sem("h6T_ready")
        logit_psum = sem("logit_psum")
        logit_read = sem("logit_read")
        shift_ready = sem("shift_ready")
        exp_done = sem("exp_done")
        aff_ready = sem("aff_ready")
        affT_psum = sem("affT_psum")
        affT_read = sem("affT_read")
        w_in_ring = [sem(f"w_in_ring{n}") for n in range(RING)]

        def weight_chunk(k, e):
            if k < 16:
                w = (w_gate, w_up)[k % 2]
                return w[ds(e, 1), :, (k // 2) * 256:(k // 2 + 1) * 256].rearrange("o (k p) n -> p (o k) n", p=P)
            return w_down[ds(e, 1), (k - 16) * 256:(k - 15) * 256, :].rearrange("o (k p) n -> p (o k) n", p=P)

        def slot(k):
            return ring[k % RING].rearrange("p (a b) -> p a b", b=256 if k < 16 else D)

        with nc.Block() as block:
            @block.sync
            def _(sp):
                for k in range(AHEAD):
                    sp.dma_start(slot(k), weight_chunk(k, 0)).then_inc(w_in_ring[k], 16)

                def store(j, b):
                    rows = ds((2 * j + b) * P, P)
                    sp.wait_ge(x2_ready, 2 * j + b + 1)
                    sp.dma_start(resid[rows, :], x6[:, b]).then_inc(x2_stored[b], 16)
                    sp.wait_ge(h6_ready, 2 * j + b + 1)
                    sp.dma_start(h2[rows, :], h6[:, b]).then_inc(h6_stored[b], 16)

                with sp.Fori(0, NTT // 2 - 1) as j:
                    for b in range(2):
                        store(j, b)
                        sp.wait_ge(x2_stored[b], 16 * j + 16)
                        sp.dma_start(x6[:, b], tokens[ds((2 * j + b + 2) * P, P), :]).then_inc(x6_in[b], 16)
                for b in range(2):
                    store(NTT // 2 - 1, b)
                for b in range(2):
                    sp.wait_ge(x2_stored[b], 16 * (NTT // 2))
                    sp.wait_ge(h6_stored[b], 16 * (NTT // 2) + 16)

            @block.gpsimd
            def _(pool):
                with pool.Fori(0, NTT // 2) as j:
                    for b in range(2):
                        pool.wait_ge(out_psum, 2 * j + b + 1)
                        pool.tensor_copy(ot[:, b], qk[:, :, ds((2 * j + b) * P, P)]).then_inc(ot_ready, 1)

            @block.tensor
            def _(pe):
                pe.drain().then_inc(out_psum, 2)
                pe.wait_ge(wo_in, 48)

                def project(t, b, half):
                    for k in range(KD):
                        ins = pe.matmul(bank(2 * b + half), ot[:, b, k],
                                        wo[:, k, half * 512:(half + 1) * 512],
                                        start=(k == 0), stop=(k == KD - 1))
                    return ins

                def turn(t, b):
                    pe.wait_ge(h6_ready, t + 1)
                    for k in range(KD):
                        o = (4 + k // 4) * 512 + (k % 4) * P
                        ins = pe.transpose(ps[:, o:o + P], h6[:, b, k * P:(k + 1) * P], ident[:, :])
                    ins.then_inc(h6T_psum, 1)

                def route(t, b):
                    pe.wait_ge(h6T_ready, t + 1)
                    pe.wait_ge(logit_read, t + 1)
                    for k in range(KD):
                        ins = pe.matmul(bank(6, NE), hT6[:, b, k], wr[:, k], start=(k == 0), stop=(k == KD - 1))
                    ins.then_inc(logit_psum, 1)

                def tile(t, b, before):
                    pe.wait_ge(ot_ready, t + 1)
                    project(t, b, 0)
                    if before is not None:
                        turn(before, 1 - b)
                    project(t, b, 1).then_inc(out_psum, 1)
                    if before is not None:
                        route(before, 1 - b)

                tile(0, 0, None)
                tile(1, 1, 0)
                with pe.Fori(0, NTT // 2 - 1) as j:
                    for b in range(2):
                        tile(j * 2 + (2 + b), b, j * 2 + (1 + b))
                turn(NTT - 1, 1)
                route(NTT - 1, 1)
                pe.wait_ge(aff_ready, 1)
                for t in range(NTT):
                    if t >= 2:
                        pe.wait_ge(affT_read, t - 1)
                    pe.transpose(ps[0:NE, (t % 2) * 512:(t % 2) * 512 + P], logit[:, t], ident[:, :]).then_inc(affT_psum, 1)

            @block.scalar
            def _(act):
                act.drain().then_inc(logit_read, 1)
                def root(t, b):
                    act.wait_ge(x2_ready, t + 1)
                    act.activation(junk6, x6[:, b], ACT.Square, accum_out=small[:, b:b + 1])
                    act.drain()
                    act.activation(small[:, 2 + b:3 + b], small[:, b:b + 1], ACT.Sqrt,
                                   bias=cst[:, 0:1], scale=1.0 / D).then_inc(rms6_ready, 1)

                def keep(t, b):
                    act.wait_ge(h6T_psum, t + 1)
                    act.copy(hT6[:, b].rearrange("p a b -> p (a b)"),
                             ps[:, 2048:2048 + D]).then_inc(h6T_ready, 1)
                    act.wait_ge(logit_psum, t + 1)
                    act.copy(logit[:, ds(t, 1)].rearrange("p a b -> p (a b)"),
                             bank(6, NE)).then_inc(logit_read, 1)

                root(0, 0)
                with act.Fori(0, NTT // 2 - 1) as j:
                    for b in range(2):
                        keep(j * 2 + b, b)
                        root(j * 2 + (b + 1), 1 - b)
                keep(NTT - 2, 0)
                root(NTT - 1, 1)
                keep(NTT - 1, 1)
                act.wait_ge(shift_ready, 1)
                act.activation(logit.rearrange("p a b -> p (a b)"), logit.rearrange("p a b -> p (a b)"),
                               ACT.Exp).then_inc(exp_done, 1)
                for t in range(NTT):
                    act.wait_ge(affT_psum, t + 1)
                    act.copy(aff[:, t * P:(t + 1) * P],
                             ps[0:NE, (t % 2) * 512:(t % 2) * 512 + P]).then_inc(affT_read, 1)

            @block.vector
            def _(v):
                for b in range(2):
                    v.drain().then_inc(h6_stored[b], 16)
                v.wait_ge(wo_in, 48)
                with v.Fori(0, NTT // 2) as j:
                    for b in range(2):
                        v.wait_ge(out_psum, 2 * j + b + 3)
                        v.wait_ge(x6_in[b], 16 * j + 16)
                        v.tensor_tensor(x6[:, b], x6[:, b], ps[:, b * 1024:(b + 1) * 1024],
                                        ALU.add).then_inc(x2_ready, 1)
                        v.wait_ge(rms6_ready, 2 * j + b + 1)
                        v.reciprocal(small[:, 4 + b:5 + b], small[:, 2 + b:3 + b])
                        v.drain()
                        v.wait_ge(h6_stored[b], 16 * j + 16)
                        v.scalar_tensor_tensor(h6[:, b], x6[:, b], small[:, 4 + b:5 + b], g2n,
                                               ALU.mult, ALU.mult).then_inc(h6_ready, 1)
                        v.drain()
                v.wait_ge(logit_read, NTT + 1)
                v.tensor_reduce(lstat[:, 0], logit, AX, ALU.max)
                v.drain()
                v.tensor_tensor(logit, logit, lstat[:, 0].unsqueeze(2).broadcast_to([P, NTT, NE]), ALU.subtract)
                v.drain().then_inc(shift_ready, 1)
                v.wait_ge(exp_done, 1)
                v.tensor_reduce(lstat[:, 1], logit, AX, ALU.add)
                v.drain()
                v.reciprocal(lstat[:, 1], lstat[:, 1])
                v.drain()
                v.tensor_tensor(logit, logit, lstat[:, 1].unsqueeze(2).broadcast_to([P, NTT, NE]), ALU.mult)
                v.drain().then_inc(aff_ready, 1)

        F16 = mybir.dt.float16
        W_SCALE = 256.0
        SPLIT = 12
        split = [at(A_ + (RING + n) * WCH, WCH).bitcast(F16) for n in range(SPLIT)]

        def part(k, lo):
            return split[k % SPLIT][:, lo * WCH:(lo + 1) * WCH].rearrange("p (a b) -> p a b", b=256 if k < 16 else D)

        o10 = (RING + SPLIT) * WCH
        val = at(o10, SLOTS)[0:NE]
        idx = sb("idx", [NE, SLOTS], U32)
        idxf = at(o10 + SLOTS, SLOTS)[0:NE]
        gsel = sb("gsel", [P, 2, NE])
        isel = sb("isel", [P, 2, NE + 1])
        gate_e = sb("gate_e", [P, 2])
        icol = sb("icol", [P, 2, 2], U32)
        xe = at(o10 + 2 * SLOTS, D)
        xs = at(o10 + 2 * SLOTS + D, D)
        o11 = o10 + 2 * SLOTS + 2 * D
        xT2 = at(o11, KD * SLOTS).bitcast(F16).rearrange("p (w a b) -> p w a b", w=2, b=SLOTS)
        o12 = o11 + KD * SLOTS
        NFT = FF // P
        hid2 = at(o12, NFT * SLOTS).bitcast(F16).rearrange("p (w a b) -> p w a b", w=2, b=SLOTS)
        o13 = o12 + NFT * SLOTS
        sil = at(o13, 2, SLOTS)
        h32 = at(o13 + 2 * SLOTS, 2, SLOTS)
        ye = at(o13 + 4 * SLOTS, D)
        ys = at(o13 + 4 * SLOTS + D, D)
        assert o12 <= o9 and o13 + 4 * SLOTS + 2 * D <= E_ + 2 * KD * P + 2 * (NT + 3)
        NK = 24
        NP = 2
        PW = WCH // NP
        vi_ready = sem("vi_ready")
        vi_psum = sem("vi_psum")
        icol_ready = sem("icol_ready")
        rows_in = sem("rows_in")
        xT_psum = sem("xT_psum")
        xT_hi = sem("xT_hi")
        xT_ready = sem("xT_ready")
        w_hi = sem("w_hi")
        w_split = sem("w_split")
        gu_psum = sem("gu_psum")
        silu_ready = sem("silu_ready")
        hid_ready = sem("hid_ready")
        down_psum = sem("down_psum")
        y_gated = sem("y_gated")
        added = sem("added")
        gate_ready = sem("gate_ready")
        rows_free = sem("rows_free")
        PASSES = ((0, 0), (0, 1), (1, 0))

        with nc.Block() as block:
            @block.sync
            def _(sp):
                def load(k, e):
                    sp.dma_start(slot(k), weight_chunk(k, e)).then_inc(w_in_ring[k % RING], 16)

                for k in range(AHEAD, RING):
                    load(k, 0)
                for k in range(RING, NK):
                    sp.wait_ge(w_split, NP * (k - RING + 1))
                    load(k, 0)
                with sp.Fori(1, NE) as e:
                    for k in range(NK):
                        sp.wait_ge(w_split, NP * NK * e + NP * (k - RING + 1))
                        load(k, e)

            @block.gpsimd
            def _(pool):
                def gather(e):
                    pool.wait_ge(icol_ready, e + 1)
                    pool.wait_ge(xT_psum, e + 1)
                    pool.tensor_tensor(carry[0:1, 2:3], carry[0:1, 1:2], carry[0:1, 1:2], ALU.add)
                    pool.drain()
                    for g, (dst, n) in enumerate(((xe, CAP0), (xs, CAP1))):
                        pool.indirect_dma_start(dst[0:n], None, h2[:, :],
                                                bass.IndirectOffsetOnAxis(ap=icol[0:n, 0, g:g + 1], axis=0)
                                                ).then_inc(rows_in, 16)

                def add_rows(e):
                    pool.wait_ge(y_gated, e + 2)
                    pool.tensor_tensor(carry[0:1, 2:3], carry[0:1, 1:2], carry[0:1, 1:2], ALU.add)
                    pool.drain()
                    for g, (src, n) in enumerate(((ye, CAP0), (ys, CAP1))):
                        pool.indirect_dma_start(resid[:, :],
                                                bass.IndirectOffsetOnAxis(ap=icol[0:n, 1, g:g + 1], axis=0),
                                                src[0:n], None, compute_op=ALU.add).then_inc(added, 16)
                    pool.wait_ge(added, 32 * e + 32)
                    pool.tensor_tensor(carry[0:1, 2:3], carry[0:1, 1:2], carry[0:1, 1:2], ALU.add)
                    pool.drain()
                    pool.drain().then_inc(rows_free, 1)

                pool.drain().then_inc(rows_free, 1)
                gather(0)
                with pool.Fori(0, NE - 1) as e:
                    gather(e + 1)
                    add_rows(e)
                add_rows(NE - 1)

            @block.tensor
            def _(pe):
                pe.drain().then_inc(xT_psum, 1)
                pe.wait_ge(vi_ready, 1)
                for n, src in enumerate((val, idxf)):
                    pe.transpose(ps[:, n * 512:n * 512 + NE], src[:, 0:CAP0], ident[0:NE, 0:NE])
                    ins = pe.transpose(ps[0:CAP1, n * 512 + NE:n * 512 + 2 * NE], src[:, CAP0:SLOTS],
                                       ident[0:NE, 0:NE])
                ins.then_inc(vi_psum, 1)

                def turn(e):
                    pe.wait_ge(rows_in, 32 * e + 32)
                    for k in range(KD):
                        o = (5 + k // 3) * 512 + (k % 3) * SLOTS
                        pe.transpose(ps[:, o:o + CAP0], xe[:, k * P:(k + 1) * P], ident[:, :])
                        ins = pe.transpose(ps[:, o + CAP0:o + SLOTS], xs[0:CAP1, k * P:(k + 1) * P],
                                           ident[0:CAP1, 0:CAP1])
                    ins.then_inc(xT_psum, 1)

                def gate_up(e):
                    pe.wait_ge(xT_ready, e + 1)
                    for c in range(8):
                        pe.wait_ge(w_split, NP * NK * e + NP * (2 * c + 2))
                        for f in range(2):
                            n = 2 * c + f
                            pe.wait_ge(hid_ready, NFT * e + (n + 1))
                            for w in range(2):
                                o = (n % 2) * 512 + w * SLOTS
                                for k in range(KD):
                                    for i, (pw, px) in enumerate(PASSES):
                                        ins = pe.matmul(ps[:, o:o + SLOTS],
                                                        part(2 * c + w, pw)[:, k, f * P:(f + 1) * P], xT2[:, px, k],
                                                        start=(k == 0 and i == 0), stop=(k == KD - 1 and i == 2))
                            ins.then_inc(gu_psum, 1)

                def down(e):
                    pe.wait_ge(y_gated, e + 1)
                    for c in range(8):
                        k = 16 + c
                        pe.wait_ge(w_split, NP * NK * e + NP * (k + 1))
                        for f in range(2):
                            n = 2 * c + f
                            pe.wait_ge(hid_ready, NFT * e + (n + 3))
                            for i, (pw, px) in enumerate(PASSES):
                                first, last = n == 0 and i == 0, n == NFT - 1 and i == 2
                                for half in range(2):
                                    pe.matmul(bank(2 + half), hid2[:, px, n, 0:CAP0],
                                              part(k, pw)[:, f, half * 512:(half + 1) * 512],
                                              start=first, stop=last)
                            for i, (pw, px) in enumerate(PASSES):
                                first, last = n == 0 and i == 0, n == NFT - 1 and i == 2
                                for q in range(4):
                                    ins = pe.matmul(ps[32 * q:32 * q + 32, 4 * 512:4 * 512 + D // 4],
                                                    hid2[:, px, n, CAP0:SLOTS],
                                                    part(k, pw)[:, f, q * 256:(q + 1) * 256],
                                                    start=first, stop=last)
                        ins.then_inc(down_psum, 1)

                turn(0)
                with pe.Fori(0, NE - 1) as e:
                    gate_up(e)
                    turn(e + 1)
                    down(e)
                gate_up(NE - 1)
                down(NE - 1)

            @block.scalar
            def _(act):
                def hi(k, e, pieces):
                    for q in pieces:
                        if q == 0:
                            act.wait_ge(w_in_ring[k % RING], 16 * (NK // RING) * e + 16 * (k // RING + 1))
                        act.activation(split[k % SPLIT][:, q * PW:(q + 1) * PW], ring[k % RING][:, q * PW:(q + 1) * PW],
                                       ACT.Copy, scale=W_SCALE).then_inc(w_hi, 1)

                def rows_hi(e):
                    act.wait_ge(xT_psum, e + 2)
                    for k in range(0, KD, 3):
                        w = min(3, KD - k)
                        ins = act.copy(xT2[:, 0, k:k + w].rearrange("p a b -> p (a b)"),
                                       ps[:, (5 + k // 3) * 512:(5 + k // 3) * 512 + w * SLOTS])
                    ins.then_inc(xT_hi, 1)

                def ahead(k, e, last):
                    if k < NK:
                        hi(k, e, range(NP))
                    elif not last:
                        hi(k - NK, e + 1, range(NP))

                def expert(e, last):
                    for n in range(NFT):
                        act.wait_ge(gu_psum, NFT * e + (n + 1))
                        act.wait_ge(hid_ready, NFT * e + (n + 1))
                        act.activation(sil[:, n % 2], ps[:, (n % 2) * 512:(n % 2) * 512 + SLOTS],
                                       ACT.Silu, scale=1.0 / W_SCALE).then_inc(silu_ready, 1)
                        ahead(n + SPLIT - 2, e, last)
                    if not last:
                        rows_hi(e + 1)
                    for c in range(8):
                        if c and not last:
                            act.wait_ge(down_psum, 8 * e + c)
                        ahead(16 + c + SPLIT - 2, e, last)
                    act.wait_ge(gate_ready, e + 1)
                    act.wait_ge(down_psum, 8 * e + 8)
                    act.activation(ye, ps[:, 1024:2048], ACT.Copy, scale=gate_e[:, 0:1])
                    for q in range(4):
                        act.copy(ys[0:CAP1, q * 256:(q + 1) * 256], ps[32 * q:32 * q + 32, 2048:2048 + 256])
                    act.drain()
                    act.activation(ys[0:CAP1], ys[0:CAP1], ACT.Copy, scale=gate_e[0:CAP1, 1:2]).then_inc(y_gated, 1)

                act.drain().then_inc(y_gated, 1)
                for k in range(SPLIT - 2):
                    hi(k, 0, range(NP))
                rows_hi(0)
                with act.Fori(0, NE - 1) as e:
                    expert(e, False)
                expert(NE - 1, True)

            @block.vector
            def _(v):
                def lo(k, e, pieces):
                    for q in pieces:
                        v.wait_ge(w_hi, NP * NK * e + (NP * k + q + 1))
                        v.scalar_tensor_tensor(split[k % SPLIT][:, WCH + q * PW:WCH + (q + 1) * PW],
                                               ring[k % RING][:, q * PW:(q + 1) * PW], W_SCALE,
                                               split[k % SPLIT][:, q * PW:(q + 1) * PW],
                                               ALU.mult, ALU.subtract).then_inc(w_split, 1)

                def rows_lo(e):
                    v.wait_ge(xT_hi, e + 1)
                    for k in range(0, KD, 3):
                        w = min(3, KD - k)
                        ins = v.tensor_tensor(xT2[:, 1, k:k + w].rearrange("p a b -> p (a b)"),
                                              ps[:, (5 + k // 3) * 512:(5 + k // 3) * 512 + w * SLOTS],
                                              xT2[:, 0, k:k + w].rearrange("p a b -> p (a b)"), ALU.subtract)
                    ins.then_inc(xT_ready, 1)

                def ahead(k, e, last):
                    if k < NK:
                        lo(k, e, range(NP))
                    elif not last:
                        lo(k - NK, e + 1, range(NP))

                def expert(e, last):
                    v.wait_ge(rows_in, 32 * e + 32)
                    v.tensor_copy(icol[:, 0, 0:1], isel[:, 0, ds(e + 1, 1)])
                    v.tensor_copy(icol[0:CAP1, 0, 1:2], isel[0:CAP1, 1, ds(e + 1, 1)])
                    v.drain().then_inc(icol_ready, 1)
                    for n in range(NFT):
                        v.wait_ge(silu_ready, NFT * e + (n + 1))
                        v.scalar_tensor_tensor(h32[:, n % 2],
                                               ps[:, (n % 2) * 512 + SLOTS:(n % 2) * 512 + 2 * SLOTS],
                                               1.0 / W_SCALE, sil[:, n % 2], ALU.mult, ALU.mult)
                        v.scalar_tensor_tensor(hid2[:, 0, n],
                                               ps[:, (n % 2) * 512 + SLOTS:(n % 2) * 512 + 2 * SLOTS],
                                               1.0 / W_SCALE, sil[:, n % 2], ALU.mult, ALU.mult)
                        v.drain()
                        v.tensor_tensor(hid2[:, 1, n], h32[:, n % 2], hid2[:, 0, n], ALU.subtract).then_inc(hid_ready, 1)
                        ahead(n + SPLIT - 2, e, last)
                    if not last:
                        rows_lo(e + 1)
                    v.wait_ge(rows_free, e + 1)
                    v.tensor_copy(icol[:, 1, 0:1], isel[:, 0, ds(e, 1)])
                    v.tensor_copy(icol[0:CAP1, 1, 1:2], isel[0:CAP1, 1, ds(e, 1)])
                    for g in range(2):
                        v.tensor_scalar(gate_e[:, g:g + 1], gsel[:, g, ds(e, 1)], 1.0 / W_SCALE, None, ALU.mult)
                    v.drain().then_inc(gate_ready, 1)
                    for c in range(8):
                        ahead(16 + c + SPLIT - 2, e, last)

                v.memset(isel[:, :, :].rearrange("p a b -> p (a b)"), 0.0)
                v.memset(gsel[:, :, :].rearrange("p a b -> p (a b)"), 0.0)
                for first, n, o, cap in ((0, T0, 0, CAP0), (T0, T1, CAP0, CAP1)):
                    row = aff[:, first:first + n]
                    for r in range(cap // 8):
                        top = val[:, o + 8 * r:o + 8 * r + 8]
                        v.max(top, row)
                        v.drain()
                        v.max_index(idx[:, o + 8 * r:o + 8 * r + 8], top, row)
                        if r < cap // 8 - 1:
                            v.drain()
                            v.match_replace(row, top, row, -1.0)
                            v.drain()
                v.drain()
                v.tensor_copy(idxf, idx[:, :])
                v.drain()
                v.tensor_scalar(idxf[:, CAP0:SLOTS], idxf[:, CAP0:SLOTS], float(T0), None, ALU.add)
                v.drain().then_inc(vi_ready, 1)
                v.wait_ge(vi_psum, 1)
                for n, dst in enumerate((gsel, isel)):
                    v.tensor_copy(dst[:, 0, 0:NE], ps[:, n * 512:n * 512 + NE])
                    v.tensor_copy(dst[0:CAP1, 1, 0:NE], ps[0:CAP1, n * 512 + NE:n * 512 + 2 * NE])
                v.drain()
                v.tensor_copy(icol[:, 0, 0:1], isel[:, 0, 0:1])
                v.tensor_copy(icol[0:CAP1, 0, 1:2], isel[0:CAP1, 1, 0:1])
                v.drain().then_inc(icol_ready, 1)
                v.drain().then_inc(hid_ready, 2)
                for k in range(SPLIT - 2):
                    lo(k, 0, range(NP))
                rows_lo(0)
                with v.Fori(0, NE - 1) as e:
                    expert(e, False)
                expert(NE - 1, True)

        xf = at(A_, NTT, D)
        gf = at(D_ + 4 * D, D)
        jf = at(D_ + 5 * D, D)
        gf_in = sem("gf_in")
        xf_in = [sem(f"xf_in{b}") for b in range(NTT // 2)]
        rmsf = sem("rmsf")
        yf_ready = sem("yf_ready")
        out_stored = sem("out_stored")

        with nc.Block() as block:
            @block.sync
            def _(sp):
                for b in range(NTT // 2):
                    sp.dma_start(xf[:, 2 * b:2 * b + 2], resid[2 * b * P:(2 * b + 2) * P, :]
                                 .rearrange("(t p) n -> p t n", p=P)).then_inc(xf_in[b], 16)
                    if b == 0:
                        sp.dma_start(gf, gains[2:3, :].partition_broadcast(P)).then_inc(gf_in, 16)
                for t in range(NTT):
                    sp.wait_ge(yf_ready, t + 1)
                    sp.dma_start(out[t * P:(t + 1) * P, :], xf[:, t]).then_inc(out_stored, 16)
                sp.wait_ge(out_stored, 16 * NTT)

            @block.scalar
            def _(act):
                for t in range(NTT):
                    act.wait_ge(xf_in[t // 2], 16)
                    act.activation(jf, xf[:, t], ACT.Square, accum_out=small[:, t:t + 1])
                    act.drain()
                    act.activation(small[:, 16 + t:17 + t], small[:, t:t + 1], ACT.Sqrt,
                                   bias=cst[:, 0:1], scale=1.0 / D).then_inc(rmsf, 1)

            @block.vector
            def _(v):
                v.wait_ge(gf_in, 16)
                for t in range(NTT):
                    v.wait_ge(rmsf, t + 1)
                    v.reciprocal(small[:, 32 + t:33 + t], small[:, 16 + t:17 + t])
                    v.drain()
                    v.scalar_tensor_tensor(xf[:, t], xf[:, t], small[:, 32 + t:33 + t], gf,
                                           ALU.mult, ALU.mult).then_inc(yf_ready, 1)


def masks():
    row, col = np.arange(P)[:, None], np.arange(P)[None, :]
    block = row // C == col // C
    cols = [row == col, block]
    for d in range(2):
        before = row < col if d == 0 else row > col
        cols += [block & before, block & (before | (row == col))]
    for d in range(2):
        for m in LEVELS:
            same = row // (2 * m) == col // (2 * m)
            first, second = (row, col) if d == 0 else (col, row)
            cols.append(same & (first % (2 * m) < m) & (second % (2 * m) >= m))
    return np.concatenate([c.astype(np.float32) for c in cols], axis=1)


def kernel(**inputs):
    import concourse.bacc as bacc
    from concourse.bass_utils import run_bass_kernel_spmd

    x = {k: np.asarray(v) for k, v in inputs.items()}

    def tiles(a, n):
        a = a.reshape(-1, a.shape[-1])
        full = np.zeros((a.shape[0], n * P), np.float32)
        full[:, :a.shape[1]] = a
        return full.reshape(-1, P).T

    par = np.concatenate([tiles(x["shift_mu"][0], ZT)] + [tiles(x[k][0], RT) for k in ("w0", "a0")]
                         + [tiles(x[k][0].reshape(1, RW), RT) for k in ("k_k", "k_a", "r_k", "lnx_w", "lnx_b")], axis=1)
    dist = np.abs(np.arange(P)[:, None] - (np.arange(BIAS_W)[None, :] - (T0 - P))).astype(np.float32)
    arrays = {
        "tokens": np.concatenate([x["x_prompt"][0], x["x_sample"][0]], axis=0),
        "gains": np.stack([x["norm1_g"][0], x["norm2_g"][0], x["final_g"]]),
        "sub_g": x["subln_g"].reshape(1, P),
        "w_in": x["w_in"][0],
        "lam_qk": x["lambda_qk"].reshape(1, 256),
        "par": par,
        "w2": x["w2"][0], "a2": x["a2"][0], "g2": x["g2"][0],
        "w_out": x["w_out"][0], "w_router": x["w_router"][0],
        "w_gate": x["w_gate"][0], "w_up": x["w_up"][0], "w_down": x["w_down"][0],
        "c_bias": -dist,
        "c_mask": masks(),
    }
    arrays = {k: np.ascontiguousarray(v) for k, v in arrays.items()}
    nc = bacc.Bacc("TRN2", target_bir_lowering=False, num_devices=1)
    aps = [nc.dram_tensor(k, v.shape, mybir.dt.from_np(v.dtype), kind="ExternalInput").ap()
           for k, v in arrays.items()]
    out = nc.dram_tensor("out", (NT, D), mybir.dt.float32, kind="ExternalOutput").ap()
    build(nc, *aps, out)
    r = run_bass_kernel_spmd(nc, [arrays], core_ids=[0])
    y = r.results[0]["out"]
    return y[:T0].reshape(1, T0, D), y[T0:].reshape(1, T1, D)
```

```python
import math
from contextlib import ExitStack

import concourse.bass as bass
from concourse import mybir
import numpy as np

P = 128
D = 1024
KD = D // P
T0, T1 = 1024, 256
NT = T0 + T1
NTT = NT // P
HEADS_A = 4
AW = 512
RW = 512
RT = RW // P
LORA = 128
GATE = 96
IN_COLS = 3 * AW + 3 * RW + LORA + GATE
ZT = 3 * RT + 2
C = 64
NE = 16
FF = 2048
CAP0, CAP1 = 2 * T0 // NE, 2 * T1 // NE
SLOTS = CAP0 + CAP1
LAMBDA_INIT = 0.8 - 0.6 * math.exp(-0.3 * 0)
NORM_EPS, GN_EPS = 1e-6, 64e-5
DECAY = -math.exp(-0.5)
LEVELS = (1, 2, 4, 8, 16, 32)

CHUNKS = ((0, 512), (512, 512), (1024, 256))

F_R, F_K, F_V, F_KK, F_SIG, F_IC, F_BONUS, F_GATE = 0, 4, 8, 12, 16, 24, 32, 36
N_FEAT = 40

P_MU = 0
P_W0 = P_MU + 2 * ZT
P_A0 = P_W0 + 2 * RT
P_KK = P_A0 + 2 * RT
P_KA = P_KK + RT
P_RK = P_KA + RT
P_LW = P_RK + RT
P_LB = P_LW + RT
N_PAR = P_LB + RT

BIAS_W = T0 + T0 - P


def build(nc, tokens, gains, sub_g, w_in, lam_qk, par, w2, a2, g2, w_out, w_router,
          w_gate, w_up, w_down, c_bias, c_mask, out):
    F32 = mybir.dt.float32
    U32 = mybir.dt.uint32
    ALU = mybir.AluOpType
    ACT = mybir.ActivationFunctionType
    AX = mybir.AxisListType.X
    ds = bass.ds

    feat = nc.dram_tensor("feat", (N_FEAT, P, NT), F32).ap()
    resid = nc.dram_tensor("resid", (NT, D), F32).ap()
    h2 = nc.dram_tensor("h2", (NT, D), F32).ap()

    with ExitStack() as ctx:
        def sb(name, shape, dt=F32):
            return ctx.enter_context(nc.sbuf_tensor(name, shape, dt))

        ident = sb("ident", [P, P])
        onesbd = sb("onesbd", [P, P])
        causal = sb("causal", [P, 2, 2 * P])
        lvl = sb("lvl", [P, 2, len(LEVELS), P])
        pars = sb("pars", [P, N_PAR])
        muc = sb("muc", [P, ZT])
        cst = sb("cst", [P, 4])
        small = sb("small", [P, 64])
        subg = sb("subg", [P, P])
        restart = sb("restart", [P, RT * C])
        g2s = sb("g2s", [GATE, RW])
        lamr = sb("lamr", [P, 384])
        arena = sb("arena", [P, 48140])

        def at(off, *dims):
            n = int(np.prod(dims))
            v = arena[:, off:off + n]
            if len(dims) == 1:
                return v
            if len(dims) == 2:
                return v.rearrange("p (a b) -> p a b", b=dims[1])
            if len(dims) == 3:
                return v.rearrange("p (a b c) -> p a b c", b=dims[1], c=dims[2])
            return v.rearrange("p (a b c d) -> p a b c d", b=dims[1], c=dims[2], d=dims[3])

        F16 = mybir.dt.float16
        W_SCALE = 256.0
        PRODUCTS = ((0, 0), (0, 1), (1, 0))

        A_, B_, C_, D_ = 0, 10240, 20480, 25600
        E_ = D_ + ZT * NT
        hT2 = at(A_, KD * NT).bitcast(F16).rearrange("p (w k n) -> p w k n", w=2, k=KD)
        qk = at(B_, KD, NT)
        vt = at(C_, NTT, AW)
        zt = at(D_, ZT, NT)
        wraw = [at(B_ + (KD - 2 + b) * NT, KD * P) for b in range(2)]
        wraw3 = [w.rearrange("p (k n) -> p k n", n=P) for w in wraw]
        wb2 = at(E_, 2 * KD * P).bitcast(F16).rearrange("p (b w m) -> p b w m", b=2, w=2)
        zpad = at(E_ + 2 * KD * P, 2, NT + 3)
        loraw = at(E_, 4 * RW)
        xt = at(D_, 2, D)
        hb = at(D_ + 2 * D, 2, D)
        junk = at(D_ + 4 * D, D)
        g1 = at(D_ + 5 * D, D)
        wv = at(D_ + 8 * D, KD * AW)
        wv2 = at(D_ + 8 * D + KD * AW, KD * AW).bitcast(F16).rearrange("p (w m) -> p w m", w=2)
        assert D_ + 8 * D + 2 * KD * AW <= E_

        ps = ctx.enter_context(nc.psum_tensor("ps", [P, 8 * 512], F32))

        carry = sb("carry", [P, 4])

        def bank(b, n=512):
            return ps[:, b * 512:b * 512 + n]


        sems = {}

        def sem(name):
            sems[name] = ctx.enter_context(nc.semaphore(name))
            return sems[name]

        consts_in = sem("consts_in")
        tables_in = sem("tables_in")
        eps_ready = sem("eps_ready")
        x_in = [sem(f"x_in{b}") for b in range(2)]
        x_free = [sem(f"x_free{b}") for b in range(2)]
        rms_ready = sem("rms_ready")
        h_ready = sem("h_ready")
        hT_psum = sem("hT_psum")
        hT_hi = sem("hT_hi")
        hT_ready = sem("hT_ready")
        w_in_hi = sem("w_in_hi")
        w_in_split = sem("w_in_split")
        wv_in = sem("wv_in")
        v_psum = sem("v_psum")
        v_ready = sem("v_ready")
        w_in_in = [sem(f"w_in_in{b}") for b in range(2)]
        proj_psum = sem("proj_psum")
        proj_out = sem("proj_out")
        mix_done = sem("mix_done")
        z_stored = sem("z_stored")
        n_consts = 3 * 16

        with nc.Block() as block:
            @block.sync
            def _(sp):
                sp.dma_start(ident[:, :], c_mask[:, 0:P]).then_inc(consts_in, 16)
                sp.dma_start(g1, gains[0:1, :].partition_broadcast(P)).then_inc(consts_in, 16)
                for b in range(2):
                    sp.dma_start(xt[:, b], tokens[b * P:(b + 1) * P, :]).then_inc(x_in[b], 16)
                sp.dma_start(pars[:, :], par).then_inc(consts_in, 16)
                sp.dma_start(wv.rearrange("p (k n) -> p k n", n=AW), w_in[:, 2 * AW:3 * AW].rearrange("(k p) n -> p k n", p=P)).then_inc(wv_in, 16)
                with sp.Fori(1, NTT // 2) as j:
                    for b in range(2):
                        sp.wait_ge(x_free[b], j)
                        sp.dma_start(xt[:, b], tokens[ds((2 * j + b) * P, P), :]).then_inc(x_in[b], 16)
                for b in range(2):
                    sp.dma_start(wraw3[b], w_in[:, 3 * AW + b * P:3 * AW + (b + 1) * P]
                                 .rearrange("(k p) n -> p k n", p=P)).then_inc(w_in_in[b], 16)
                sp.dma_start(onesbd[:, :], c_mask[:, P:2 * P]).then_inc(tables_in, 16)
                sp.dma_start(subg[:, :], sub_g.partition_broadcast(P)).then_inc(tables_in, 16)
                sp.dma_start(causal[:, :, :].rearrange("p a b -> p (a b)"),
                             c_mask[:, 2 * P:6 * P]).then_inc(tables_in, 16)
                sp.dma_start(lvl[:, :, :, :].rearrange("p a b c -> p (a b c)"),
                             c_mask[:, 6 * P:(6 + 2 * len(LEVELS)) * P]).then_inc(tables_in, 16)
                sp.dma_start(lamr[:, 0:256], lam_qk.partition_broadcast(P)).then_inc(tables_in, 16)
                with sp.Fori(1, (ZT - 2) // 2) as j:
                    for b in range(2):
                        sp.wait_ge(w_in_split, 2 * j + b)
                        sp.dma_start(wraw3[b], w_in[:, ds((2 * j + b) * P + 3 * AW, P)]
                                     .rearrange("(k p) n -> p k n", p=P)).then_inc(w_in_in[b], 16)
                sp.wait_ge(w_in_split, ZT - 2)
                sp.dma_start(wraw3[0], w_in[:, 3 * AW + 12 * P:3 * AW + 13 * P]
                             .rearrange("(k p) n -> p k n", p=P)).then_inc(w_in_in[0], 16)
                sp.wait_ge(w_in_split, ZT - 1)
                sp.dma_start(wraw3[1][:, :, 0:GATE], w_in[:, 3 * AW + 13 * P:IN_COLS]
                             .rearrange("(k p) n -> p k n", p=P)).then_inc(w_in_in[1], 16)
                with sp.Fori(0, 4) as j:
                    for b in range(2):
                        sp.wait_ge(w_in_split, 2 * j + (ZT + b))
                        sp.dma_start(wraw3[b], w_in[:, ds((2 * j + b) * P, P)]
                                     .rearrange("(k p) n -> p k n", p=P)).then_inc(w_in_in[b], 16)

            @block.gpsimd
            def _(pool):
                pool.wait_ge(mix_done, 3 * RT + 2)
                pool.dma_start(feat[0:3 * RT].rearrange("t p n -> p t n"), zt[:, 0:3 * RT, :]).then_inc(z_stored, 16)

            @block.scalar
            def _(act):
                act.wait_ge(eps_ready, 1)

                def pair(j):
                    for b in range(2):
                        act.wait_ge(x_in[b], 16 * j + 16)
                        act.activation(junk, xt[:, b], ACT.Square, accum_out=small[:, b:b + 1])
                        act.drain()
                        act.activation(small[:, 2 + b:3 + b], small[:, b:b + 1], ACT.Sqrt,
                                       bias=cst[:, 0:1], scale=1.0 / D).then_inc(rms_ready, 1)
                    for b in range(2):
                        act.wait_ge(hT_psum, 2 * j + b + 3)
                        for half in range(2):
                            ins = act.copy(hT2[:, 0, 4 * half:4 * half + 4, ds((2 * j + b) * P, P)],
                                           ps[:, (2 * b + half) * 512:(2 * b + half + 1) * 512]
                                           .rearrange("p (a b) -> p a b", b=P))
                        ins.then_inc(hT_hi, 1)

                def keep_v(j):
                    for b in range(2):
                        act.wait_ge(v_psum, 2 * j + b + 1)
                        act.activation(vt[:, ds(2 * j + b, 1), :].rearrange("p a b -> p (a b)"),
                                       bank(4 + b), ACT.Copy, scale=1.0 / W_SCALE).then_inc(v_ready, 1)

                def weights_hi(n, b):
                    act.wait_ge(w_in_in[b], 16 * n + 16)
                    act.activation(wb2[:, b, 0], wraw[b], ACT.Copy, scale=W_SCALE).then_inc(w_in_hi, 1)

                pair(0)
                act.wait_ge(wv_in, 16)
                act.activation(wv2[:, 0], wv, ACT.Copy, scale=W_SCALE).then_inc(w_in_hi, 1)
                with act.Fori(0, NTT // 2 - 1) as j:
                    pair(j + 1)
                    keep_v(j)
                for b in range(2):
                    weights_hi(0, b)
                keep_v(NTT // 2 - 1)
                with act.Fori(0, ZT // 2) as j:
                    for b in range(2):
                        act.wait_ge(proj_psum, 2 * j + b + 1)
                        weights_hi(j + 1, b)
                        act.wait_ge(mix_done, 2 * j + b + 1)
                        act.activation(zpad[:, b, 1:1 + T0], ps[:, b * 2048:b * 2048 + T0],
                                       ACT.Copy, scale=1.0 / W_SCALE)
                        act.activation(zpad[:, b, 2 + T0:2 + NT], ps[:, b * 2048 + T0:b * 2048 + NT],
                                       ACT.Copy, scale=1.0 / W_SCALE).then_inc(proj_out, 1)

                def keep_qk(j, b, more):
                    act.wait_ge(proj_psum, 2 * j + (ZT + b + 1))
                    if more:
                        weights_hi(j + (ZT // 2 + 1), b)
                    act.activation(qk[:, ds(2 * j + b, 1), :].rearrange("p a b -> p (a b)"),
                                   ps[:, b * 2048:b * 2048 + NT],
                                   ACT.Copy, scale=1.0 / W_SCALE).then_inc(proj_out, 1)

                with act.Fori(0, 3) as j:
                    for b in range(2):
                        keep_qk(j, b, True)
                for b in range(2):
                    keep_qk(3, b, False)

            @block.vector
            def _(v):
                v.memset(cst[:, 0:1], NORM_EPS)
                v.memset(carry[:, :], 0.0)
                v.memset(cst[:, 1:2], GN_EPS).then_inc(eps_ready, 1)
                v.memset(restart[:, :], 1.0)
                v.memset(zpad.rearrange("p a b -> p (a b)"), 0.0)
                v.drain()
                v.memset(restart[:, :].rearrange("p (a b) -> p a b", b=C)[:, :, 0:1], 0.0)
                v.drain().then_inc(mix_done, 2)
                v.drain().then_inc(hT_ready, 2)
                v.wait_ge(consts_in, n_consts)

                def pair(j):
                    for b in range(2):
                        v.wait_ge(rms_ready, 2 * j + b + 1)
                        v.reciprocal(small[:, 4 + b:5 + b], small[:, 2 + b:3 + b])
                        v.drain()
                        v.wait_ge(hT_psum, 2 * j + b + 1)
                        v.scalar_tensor_tensor(hb[:, b], xt[:, b], small[:, 4 + b:5 + b], g1,
                                               ALU.mult, ALU.mult).then_inc(h_ready, 1)
                        v.drain().then_inc(x_free[b], 1)
                    for b in range(2):
                        v.wait_ge(hT_hi, 2 * j + b + 1)
                        for half in range(2):
                            hi, lo = (hT2[:, w, 4 * half:4 * half + 4, ds((2 * j + b) * P, P)] for w in range(2))
                            ins = v.tensor_tensor(lo, ps[:, (2 * b + half) * 512:(2 * b + half + 1) * 512]
                                                  .rearrange("p (a b) -> p a b", b=P), hi, ALU.subtract)
                        ins.then_inc(hT_ready, 1)

                def weights_lo(j, b):
                    v.wait_ge(w_in_hi, 2 * j + b + 2)
                    v.scalar_tensor_tensor(wb2[:, b, 1], wraw[b], W_SCALE, wb2[:, b, 0],
                                           ALU.mult, ALU.subtract).then_inc(w_in_split, 1)

                pair(0)
                v.wait_ge(w_in_hi, 1)
                v.scalar_tensor_tensor(wv2[:, 1], wv, W_SCALE, wv2[:, 0],
                                       ALU.mult, ALU.subtract).then_inc(w_in_split, 1)
                with v.Fori(1, NTT // 2) as j:
                    pair(j)
                v.tensor_tensor(muc[:, :], pars[:, P_MU:P_MU + ZT], pars[:, P_MU + ZT:P_MU + 2 * ZT], ALU.add)
                v.drain()
                v.tensor_scalar(muc[:, :], muc[:, :], -1.0, 1.0, ALU.mult, ALU.add)
                v.drain()
                for b in range(2):
                    weights_lo(0, b)
                v.wait_ge(v_psum, NTT)
                with v.Fori(0, ZT // 2) as j:
                    for b in range(2):
                        weights_lo(j + 1, b)
                        v.wait_ge(proj_out, 2 * j + b + 1)
                        v.tensor_copy(small[:, 8:9], muc[:, ds(2 * j + b, 1)])
                        v.tensor_copy(small[:, 9:10], pars[:, ds(2 * j + b + P_MU, 1)])
                        v.tensor_copy(small[:, 10:11], pars[:, ds(2 * j + b + P_MU + ZT, 1)])
                        v.drain()
                        for step in range(3):
                            for o, c, n in ((1, 0, T0), (T0 + 2, T0, T1)):
                                dst = zt[:, ds(2 * j + b, 1), c:c + n].rearrange("p a b -> p (a b)")
                                if step == 0:
                                    v.tensor_scalar(dst, zpad[:, b, o:o + n], small[:, 8:9], None, ALU.mult)
                                else:
                                    src = zpad[:, b, o - 1:o - 1 + n] if step == 1 else zpad[:, b, o + 1:o + 1 + n]
                                    v.scalar_tensor_tensor(dst, src, small[:, 8 + step:9 + step], dst,
                                                           ALU.mult, ALU.add)
                            if step < 2:
                                v.drain()
                        v.drain().then_inc(mix_done, 1)
                with v.Fori(ZT // 2 + 1, ZT // 2 + 4) as j:
                    for b in range(2):
                        weights_lo(j, b)

            @block.tensor
            def _(pe):
                pe.drain().then_inc(hT_psum, 2)
                pe.wait_ge(consts_in, n_consts)

                def turn(t):
                    pe.wait_ge(h_ready, t + 1)
                    pe.wait_ge(hT_ready, t + 1)
                    for k in range(KD):
                        o = 2 * (t % 2) * 512 + k * P
                        ins = pe.transpose(ps[:, o:o + P], hb[:, t % 2, k * P:(k + 1) * P], ident[:, :])
                    ins.then_inc(hT_psum, 1)

                def values(t):
                    pe.wait_ge(hT_ready, t + 3)
                    if t >= 2:
                        pe.wait_ge(v_ready, t - 1)
                    for k in range(KD):
                        for n, (x, w) in enumerate(PRODUCTS):
                            ins = pe.matmul(bank(4 + t % 2), hT2[:, x, k, t * P:(t + 1) * P],
                                            wv2[:, w, k * AW:(k + 1) * AW],
                                            start=(k == 0 and n == 0), stop=(k == KD - 1 and n == 2))
                    ins.then_inc(v_psum, 1)

                for j in range(NTT // 2):
                    for b in range(2):
                        turn(2 * j + b)
                    if j == 1:
                        pe.wait_ge(w_in_split, 1)
                    for b in range(2):
                        if j:
                            values(2 * j - 2 + b)
                for b in range(2):
                    values(NTT - 2 + b)
                pe.wait_ge(v_ready, NTT)

                def project(b):
                    for o, c in CHUNKS:
                        for k in range(KD):
                            for n, (w, x) in enumerate(PRODUCTS):
                                ins = pe.matmul(ps[:, b * 2048 + o:b * 2048 + o + c],
                                                wb2[:, b, w, k * P:(k + 1) * P], hT2[:, x, k, o:o + c],
                                                start=(k == 0 and n == 0), stop=(k == KD - 1 and n == 2))
                    ins.then_inc(proj_psum, 1)

                for b in range(2):
                    pe.wait_ge(w_in_split, b + 2)
                    project(b)
                with pe.Fori(1, ZT // 2 + 4) as j:
                    for b in range(2):
                        pe.wait_ge(w_in_split, 2 * j + b + 2)
                        pe.wait_ge(proj_out, 2 * j + b - 1)
                        project(b)

        sq = at(A_, 2, NT)
        oba = at(A_ + 2 * NT, 2, NT)
        obv = at(A_ + 4 * NT, 2, NT)
        tmp = at(A_ + 6 * NT, 2, NT)
        lora_in = sem("lora_in")
        loraw_zero = sem("loraw_zero")
        tanh_done = sem("tanh_done")
        sq_ready = sem("sq_ready")
        pre_psum = sem("pre_psum")
        root_ready = sem("root_ready")
        pset_read = sem("pset_read")
        oba_full = sem("oba_full")
        obv_full = sem("obv_full")
        oba_stored = [sem(f"oba_stored{b}") for b in range(2)]
        obv_stored = [sem(f"obv_stored{b}") for b in range(2)]
        bias = at(E_ + 2 * KD * P, BIAS_W)
        bias_in = sem("bias_in")
        act_small = sem("act_small")
        lam_dot = sem("lam_dot")
        items = []
        for f in range(RT):
            items.append(("kk", f, 0, F_KK + f))
            for d in range(2):
                items.append(("sig", f, d, F_SIG + RT * d + f))
                items.append(("ic", f, d, F_IC + RT * d + f))
                if d == 0:
                    items.append(("bonus", f, 0, F_BONUS + f))
            items.append(("gate", f, 0, F_GATE + f))
        sums = [n for n in range(len(items)) if items[n][0] in ("kk", "bonus")]
        acts = [n for n in range(len(items)) if n not in sums]
        n_sums = [sum(1 for x in items[:n] if x[0] in ("kk", "bonus")) for n in range(len(items) + 1)]
        Z_LORA, Z_GATE = 3 * RT, 3 * RT + 1

        with nc.Block() as block:
            @block.sync
            def _(sp):
                sp.dma_start(bias, c_bias).then_inc(bias_in, 16)
                sp.wait_ge(loraw_zero, 1)
                for n, w in enumerate((w2[0], w2[1], a2[0], a2[1])):
                    sp.dma_start(loraw[32 * n:32 * n + 32, RW * n:RW * (n + 1)], w).then_inc(lora_in, 16)
                sp.dma_start(g2s[:, :], g2).then_inc(lora_in, 16)
                for a, n in enumerate(acts):
                    sp.wait_ge(oba_full, a + 1)
                    sp.dma_start(feat[items[n][3]], oba[:, a % 2]).then_inc(oba_stored[a % 2], 16)
                for b in range(2):
                    sp.wait_ge(oba_stored[b], 16 * len(acts[b::2]))

            @block.gpsimd
            def _(pool):
                for s, n in enumerate(sums):
                    pool.wait_ge(obv_full, s + 1)
                    pool.dma_start(feat[items[n][3]], obv[:, s % 2]).then_inc(obv_stored[s % 2], 16)
                for b in range(2):
                    pool.wait_ge(obv_stored[b], 16 * len(sums[b::2]))
                pool.wait_ge(z_stored, 16)

            @block.tensor
            def _(pe):
                pe.wait_ge(tables_in, 5 * 16)
                for n, (what, f, d, _) in enumerate(items):
                    if what in ("kk", "bonus"):
                        pe.wait_ge(sq_ready, n_sums[n + 1])
                    if n >= 2:
                        pe.wait_ge(pset_read, n - 1)
                    if n == acts[0]:
                        pe.wait_ge(tanh_done, 1)
                        pe.wait_ge(lora_in, 5 * 16)
                    for o, c in CHUNKS:
                        dst = ps[:, (n % 2) * 2048 + o:(n % 2) * 2048 + o + c]
                        if what in ("kk", "bonus"):
                            ins = pe.matmul(dst, onesbd[:, :], sq[:, n_sums[n] % 2, o:o + c], start=True, stop=True)
                        elif what == "gate":
                            ins = pe.matmul(dst, g2s[:, f * P:(f + 1) * P], zt[0:GATE, Z_GATE, o:o + c],
                                            start=True, stop=True)
                        else:
                            w = (d if what == "sig" else 2 + d) * RW + f * P
                            ins = pe.matmul(dst, loraw[:, w:w + P], zt[:, Z_LORA, o:o + c], start=True, stop=True)
                    ins.then_inc(pre_psum, 1)

            @block.scalar
            def _(act):
                act.activation(zt[0:64, Z_LORA, :], zt[0:64, Z_LORA, :], ACT.Tanh)
                act.activation(zt[0:GATE, Z_GATE, :], zt[0:GATE, Z_GATE, :], ACT.Sigmoid).then_inc(tanh_done, 1)
                act.wait_ge(lam_dot, 1)
                act.activation(small[:, 18:20], small[:, 16:18], ACT.Exp).then_inc(act_small, 1)
                for n, (what, f, d, _) in enumerate(items):
                    src = ps[:, (n % 2) * 2048:(n % 2) * 2048 + NT]
                    act.wait_ge(pre_psum, n + 1)
                    if what in ("kk", "bonus"):
                        i = n_sums[n]
                        if i >= 2:
                            act.wait_ge(obv_full, i - 1)
                        act.activation(tmp[:, i % 2], src, ACT.Sqrt if what == "kk" else ACT.Copy)
                        act.drain().then_inc(root_ready, 1)
                    else:
                        a = n - n_sums[n]
                        if a >= 2:
                            act.wait_ge(oba_stored[a % 2], 16 * (a // 2))
                        if what == "gate":
                            act.copy(oba[:, a % 2], src)
                        else:
                            first = P_W0 if what == "sig" else P_A0
                            act.activation(oba[:, a % 2], src, ACT.Sigmoid,
                                           bias=pars[:, first + RT * d + f:first + RT * d + f + 1])
                        act.drain().then_inc(oba_full, 1)
                    act.drain().then_inc(pset_read, 1)

            @block.vector
            def _(v):
                v.memset(loraw, 0.0).then_inc(loraw_zero, 1)
                v.wait_ge(tables_in, 5 * 16)
                for n in range(2):
                    v.tensor_tensor(lamr[:, 256 + 64 * n:320 + 64 * n], lamr[:, 128 * n:128 * n + 64],
                                    lamr[:, 128 * n + 64:128 * n + 128], ALU.mult)
                v.drain()
                v.tensor_reduce(small[:, 16:18], lamr[:, 256:384].rearrange("p (a b) -> p a b", b=64),
                                AX, ALU.add).then_inc(lam_dot, 1)

                def operand(n):
                    what, f, _, _ = items[n]
                    if n_sums[n] >= 2:
                        last = [m for m in range(n) if items[m][0] in ("kk", "bonus")][-2]
                        v.wait_ge(pre_psum, last + 1)
                    dst = sq[:, n_sums[n] % 2]
                    if what == "kk":
                        v.tensor_scalar(dst, zt[:, RT + f], pars[:, P_KK + f:P_KK + f + 1], None, ALU.mult)
                        v.drain()
                        v.tensor_tensor(dst, dst, dst, ALU.mult).then_inc(sq_ready, 1)
                    else:
                        v.scalar_tensor_tensor(dst, zt[:, f], pars[:, P_RK + f:P_RK + f + 1], zt[:, RT + f],
                                               ALU.mult, ALU.mult).then_inc(sq_ready, 1)

                operand(sums[0])
                for s, n in enumerate(sums):
                    if s + 1 < len(sums):
                        operand(sums[s + 1])
                    what, f, _, _ = items[n]
                    v.wait_ge(root_ready, s + 1)
                    if what == "kk":
                        v.tensor_scalar(tmp[:, s % 2], tmp[:, s % 2], 1e-12, None, ALU.max)
                        v.drain()
                        v.reciprocal(tmp[:, s % 2], tmp[:, s % 2])
                        v.drain()
                    if s >= 2:
                        v.wait_ge(obv_stored[s % 2], 16 * (s // 2))
                    if what == "kk":
                        v.scalar_tensor_tensor(obv[:, s % 2], zt[:, RT + f], pars[:, P_KK + f:P_KK + f + 1],
                                               tmp[:, s % 2], ALU.mult, ALU.mult)
                    else:
                        v.tensor_tensor(obv[:, s % 2], tmp[:, s % 2], zt[:, 2 * RT + f], ALU.mult)
                    v.drain().then_inc(obv_full, 1)
                v.wait_ge(act_small, 1)
                v.tensor_tensor(small[:, 20:21], small[:, 19:20], small[:, 18:19], ALU.subtract)
                v.drain()
                v.tensor_scalar(cst[:, 2:3], small[:, 20:21], -LAMBDA_INIT, None, ALU.add)

        qz = at(D_, 2, NT)
        sc = at(D_ + 2 * NT, 2, 2, T0)
        pd = at(D_ + 2 * NT + 4 * T0, 2, T0)
        pdT = at(D_ + 2 * NT + 6 * T0, 2, KD, P)
        oraw = at(D_ + 2 * NT + 8 * T0, HEADS_A, NTT, P)
        ojunk = at(A_ + 2048, P)
        ostat = at(A_ + 2048 + P, 3, HEADS_A * NTT)
        NR = 5
        srow = at(A_ + 2048 + 4 * P, NR, 8)
        q_ready = sem("q_ready")
        scores_psum = sem("scores_psum")
        scores_read = sem("scores_read")
        probs_ready = sem("probs_ready")
        pd_ready = sem("pd_ready")
        pdT_psum = sem("pdT_psum")
        pdT_ready = sem("pdT_ready")
        o_psum = sem("o_psum")
        o_read = sem("o_read")
        on_ready = sem("on_ready")
        oT_psum = sem("oT_psum")
        oT_read = sem("oT_read")
        NU = NTT
        units = [(0, T0, i) for i in range(T0 // P)] + [(T0, T1, i) for i in range(T1 // P)]

        with nc.Block() as block:
            @block.tensor
            def _(pe):
                with pe.Fori(0, HEADS_A) as h:
                    pe.wait_ge(q_ready, h + 1)

                    def scores(u):
                        t0, n, i = units[u]
                        for m in range(2):
                            pe.wait_ge(scores_read, 2 * NU * h + (2 * u + m + 1))
                            for o in range(0, n, 512):
                                w = min(512, n)
                                ins = pe.matmul(ps[:, m * T0 + o:m * T0 + o + w],
                                                qz[:, m, t0 + i * P:t0 + (i + 1) * P],
                                                qk[:, ds(h + HEADS_A, 1), t0 + o:t0 + o + w]
                                                .rearrange("p a b -> p (a b)"), start=True, stop=True)
                            ins.then_inc(scores_psum, 1)

                    def turn(u):
                        n = units[u][1]
                        pe.wait_ge(pd_ready, NU * h + (u + 1))
                        pe.wait_ge(pdT_ready, NU * h + (u + 1))
                        for k in range(n // P):
                            ins = pe.transpose(ps[:, 4 * 512 + k * P:4 * 512 + (k + 1) * P],
                                               pd[:, u % 2, k * P:(k + 1) * P], ident[:, :])
                        ins.then_inc(pdT_psum, 1)

                    def weigh(u):
                        t0, n, i = units[u]
                        pe.wait_ge(pdT_ready, NU * h + (u + 2))
                        pe.wait_ge(o_read, NU * h + (u + 1))
                        for k in range(n // P):
                            ins = pe.matmul(bank(6 + u % 2, P), pdT[:, u % 2, k, :],
                                            vt[:, t0 // P + k, ds(h * P, P)],
                                            start=(k == 0), stop=(k == n // P - 1))
                        ins.then_inc(o_psum, 1)

                    for s in range(NU + 3):
                        if s < NU:
                            scores(s)
                        if 2 <= s < NU + 2:
                            turn(s - 2)
                        if s >= 3:
                            weigh(s - 3)
                for n in range(HEADS_A):
                    for u in range(NU):
                        m = n * NU + u
                        pe.wait_ge(on_ready, m + 1)
                        if m >= 8:
                            pe.wait_ge(oT_read, m - 7)
                        pe.transpose(bank(m % 8, P), oraw[:, n, u], ident[:, :]).then_inc(oT_psum, 1)

            @block.scalar
            def _(act):
                act.drain().then_inc(pdT_ready, 1)
                act.drain().then_inc(o_read, 2)
                with act.Fori(0, HEADS_A) as h:
                    def probs(u):
                        t0, n, i = units[u]
                        for m in range(2):
                            act.wait_ge(scores_read, 2 * NU * h + (2 * u + m + 3))
                            act.activation(sc[:, u % 2, m, 0:n], sc[:, u % 2, m, 0:n], ACT.Exp,
                                           bias=srow[:, u % NR, m:m + 1],
                                           accum_out=srow[:, u % NR, 2 + m:3 + m]).then_inc(probs_ready, 1)

                    def keep_turned(u):
                        n = units[u][1]
                        act.wait_ge(pdT_psum, NU * h + (u + 1))
                        act.copy(pdT[:, u % 2, 0:n // P, :].rearrange("p a b -> p (a b)"),
                                 ps[:, 4 * 512:4 * 512 + n]).then_inc(pdT_ready, 1)

                    def keep_output(u):
                        act.wait_ge(o_psum, NU * h + (u + 1))
                        o = oraw[:, ds(h, 1), u].rearrange("p a b -> p (a b)")
                        act.activation(o, bank(6 + u % 2, P), ACT.Copy, scale=srow[:, u % NR, 4:5])
                        act.drain().then_inc(o_read, 1)
                        act.activation(ojunk, o, ACT.Square, accum_out=ostat[:, 0, ds(h * NU + u, 1)])

                    for s in range(NU + 3):
                        if s < NU:
                            probs(s)
                        if 2 <= s < NU + 2:
                            keep_turned(s - 2)
                        if s >= 3:
                            keep_output(s - 3)
                act.drain()
                act.activation(ostat[:, 1], ostat[:, 0], ACT.Sqrt, bias=cst[:, 0:1],
                               scale=1.0 / P).then_inc(act_small, 1)
                for n in range(HEADS_A):
                    for u in range(NU):
                        m = n * NU + u
                        act.wait_ge(oT_psum, m + 1)
                        act.copy(qk[:, n, u * P:(u + 1) * P], bank(m % 8, P)).then_inc(oT_read, 1)

            @block.vector
            def _(v):
                v.memset(qz.rearrange("p a b -> p (a b)"), 0.0)
                v.drain().then_inc(scores_read, 2)
                v.wait_ge(bias_in, 16)
                with v.Fori(0, HEADS_A) as h:
                    for m in range(2):
                        v.tensor_scalar(qz[64 * m:64 * m + 64, m, :],
                                        qk[64 * m:64 * m + 64, ds(h, 1), :].rearrange("p a b -> p (a b)"),
                                        0.125, None, ALU.mult)
                    v.drain().then_inc(q_ready, 1)
                    v.tensor_scalar(bias, bias, 0.25, None, ALU.mult)
                    v.drain()

                    def biased(u):
                        t0, n, i = units[u]
                        for m in range(2):
                            v.wait_ge(scores_psum, 2 * NU * h + (2 * u + m + 1))
                            v.tensor_copy(carry[0:1, 0:1], carry[0:1, 1:2])
                            w = T0 - P - i * P
                            v.tensor_tensor_reduce(sc[:, u % 2, m, 0:n], ps[:, m * T0:m * T0 + n],
                                                   bias[:, w:w + n], 1.0, -3.0e38, ALU.add, ALU.max,
                                                   small[:, 24 + m:25 + m])
                            v.drain()
                            v.tensor_scalar(srow[:, u % NR, m:m + 1], small[:, 24 + m:25 + m], -1.0, None,
                                            ALU.mult).then_inc(scores_read, 1)

                    def difference(u):
                        n = units[u][1]
                        v.wait_ge(probs_ready, 2 * NU * h + (2 * u + 2))
                        r = srow[:, u % NR]
                        v.reciprocal(r[:, 4:6], r[:, 2:4])
                        v.drain()
                        v.scalar_tensor_tensor(r[:, 5:6], r[:, 5:6], cst[:, 2:3], r[:, 2:3], ALU.mult, ALU.mult)
                        v.drain()
                        if u >= 2:
                            v.wait_ge(pdT_psum, NU * h + (u - 1))
                        v.scalar_tensor_tensor(pd[:, u % 2, 0:n], sc[:, u % 2, 1, 0:n], r[:, 5:6],
                                               sc[:, u % 2, 0, 0:n], ALU.mult, ALU.add).then_inc(pd_ready, 1)
                        v.drain()

                    for s in range(NU + 1):
                        if s < NU:
                            biased(s)
                        if s >= 1:
                            difference(s - 1)
                    v.wait_ge(pdT_psum, NU * h + NU)
                    v.tensor_copy(carry[0:1, 0:1], carry[0:1, 1:2])
                v.wait_ge(act_small, 2)
                v.reciprocal(ostat[:, 2], ostat[:, 1])
                v.drain()
                v.tensor_scalar(ostat[:, 2], ostat[:, 2], 1.0 - LAMBDA_INIT, None, ALU.mult)
                v.drain()
                for n in range(HEADS_A):
                    for u in range(NU):
                        m = n * NU + u
                        v.scalar_tensor_tensor(oraw[:, n, u], oraw[:, n, u], ostat[:, 2, m:m + 1], subg[:, :],
                                               ALU.mult, ALU.mult).then_inc(on_ready, 1)

        yacc = at(B_ + RT * NT, RT, NT)
        R1, R2 = A_, C_
        cin = [at(R2 + d * 6 * RT * C, 6, RT * C) for d in range(2)]
        o2 = R2 + 12 * RT * C
        ext = [at(o2 + d * 7 * RT * C, 7, RT * C) for d in range(2)]
        o3 = o2 + 14 * RT * C
        o4 = o3 + RT * 10 * P
        o5 = o4 + RT * 8 * P
        o7 = o5 + RT * 4 * P
        bd_at = [[o + d * RT * 5 * P for o in (o3, o7)] for d in range(2)]
        ar_bd = [[at(o, RT, 2, P) for o in bd_at[d]] for d in range(2)]
        b_bd = [[at(o + RT * 2 * P, RT, P) for o in bd_at[d]] for d in range(2)]
        k_bd = [[at(o + RT * 3 * P, RT, P) for o in bd_at[d]] for d in range(2)]
        v_bd = [[at(o + RT * 4 * P, RT, P) for o in bd_at[d]] for d in range(2)]
        bm = [at(o4 + d * RT * 4 * P, RT, 2, P) for d in range(2)]
        km = [at(o4 + d * RT * 4 * P + RT * 2 * P, RT, 2, P) for d in range(2)]
        inv = [at(o5 + d * RT * 2 * P, RT, P) for d in range(2)]
        invT = [at(o5 + d * RT * 2 * P + RT * P, RT, P) for d in range(2)]
        assert o7 + RT * 10 * P <= E_ + 2 * KD * P + 2 * (NT + 3)
        alv = [at(R1 + d * 6 * RT * P, len(LEVELS), RT, P) for d in range(2)]
        o6 = R1 + 12 * RT * P
        tokb = [at(o6 + d * 4 * RT * P, RT, P) for d in range(2)]
        tokk = [at(o6 + d * 4 * RT * P + RT * P, RT, P) for d in range(2)]
        tokv = [at(o6 + d * 4 * RT * P + 2 * RT * P, RT, P) for d in range(2)]
        prod = [at(o6 + d * 4 * RT * P + 3 * RT * P, RT, P) for d in range(2)]
        assert o6 + 8 * RT * P <= B_
        state = [sb(f"state{d}", [P, RT, P]) for d in range(2)]
        eb = sb("eb", [P, 2, 2, RT])

        cin_in = [sem(f"cin_in{d}") for d in range(2)]
        cin_free = [sem(f"cin_free{d}") for d in range(2)]
        zeroed = sem("zeroed")
        cum_ready = [sem(f"cum_ready{d}") for d in range(2)]
        exp_ready = [sem(f"exp_ready{d}") for d in range(2)]
        vbd_ready = [sem(f"vbd_ready{d}") for d in range(2)]
        bd_ready = [sem(f"bd_ready{d}") for d in range(2)]
        pairs_psum = [sem(f"pairs_psum{d}") for d in range(2)]
        masks_ready = [sem(f"masks_ready{d}") for d in range(2)]
        first_psum = [sem(f"first_psum{d}") for d in range(2)]
        lvl_masked = [sem(f"lvl_masked{d}") for d in range(2)]
        tok_psum = [sem(f"tok_psum{d}") for d in range(2)]
        tok_read = [sem(f"tok_read{d}") for d in range(2)]
        inv_ready = [sem(f"inv_ready{d}") for d in range(2)]
        ax_psum = [sem(f"ax_psum{d}") for d in range(2)]
        prod_ready = [sem(f"prod_ready{d}") for d in range(2)]
        xax_psum = [sem(f"xax_psum{d}") for d in range(2)]
        state_ready = [sem(f"state_ready{d}") for d in range(2)]
        invT_final = [sem(f"invT_final{d}") for d in range(2)]
        g_psum = [sem(f"g_psum{d}") for d in range(2)]
        u_psum = [sem(f"u_psum{d}") for d in range(2)]
        y_psum = [sem(f"y_psum{d}") for d in range(2)]
        y_read = [sem(f"y_read{d}") for d in range(2)]
        NL = len(LEVELS) - 1
        NTOK = 3
        TOKENS = {2: ((0, 0), (1, 0)), 3: ((0, 1), (1, 1)), 4: ((0, 2),), 5: ((1, 2),)}
        assert NL == 5
        SEGS = ((0, T0 // C, 0, T0 // C // 2), (T0, T1 // C, T0 // C, T1 // C // 2 - 1))
        LAST = T1 // C - 2

        with nc.Block() as block:
            @block.sync
            def _(sp):
                for t0, nch, c0, _ in SEGS:
                    with sp.Fori(0, nch) as n:
                        for d in range(2):
                            first = n * C + t0 if d == 0 else (nch - 1) * C + t0 - n * C
                            sp.wait_ge(cin_free[d], 1)
                            sp.wait_ge(cin_free[d], n + (c0 + 1))
                            sp.wait_ge(vbd_ready[d], n + (c0 + 1))
                            for q, t in ((0, F_R), (1, F_K), (2, F_V), (3, F_KK),
                                         (4, F_SIG + RT * d), (5, F_IC + RT * d)):
                                sp.dma_start(cin[d][:, q].rearrange("p (a b) -> p a b", b=C),
                                             feat[t:t + RT, :, ds(first, C)].rearrange("t p n -> p t n")
                                             ).then_inc(cin_in[d], 16)

            @block.gpsimd
            def _(pool):
                def mask_levels(n, c0):
                    for levels in ((1,), range(2, NL + 1)):
                        for d in range(2):
                            pool.wait_ge(masks_ready[d], 3 * n + (3 * c0 + 1))
                            for l in levels:
                                pool.tensor_tensor(alv[d][:, l], bm[d][:, :, 0],
                                                   lvl[:, d, l:l + 1, :].broadcast_to([P, RT, P]),
                                                   ALU.mult).then_inc(lvl_masked[d], 1)

                pool.memset(yacc.rearrange("p a b -> p (a b)"), 0.0)
                pool.memset(at(o7, RT * 10 * P), 0.0)
                pool.drain().then_inc(zeroed, 1)
                for t0, nch, c0, pairs in SEGS:
                    with pool.Fori(0, pairs) as i:
                        for par in range(2):
                            mask_levels(i * 2 + par, c0)
                for par in range(2):
                    mask_levels(LAST + par, c0)

            @block.tensor
            def _(pe):
                def pb(d, b, p):
                    return ps[:, (4 * d + b) * 512 + p * P:(4 * d + b) * 512 + (p + 1) * P]

                def chunk(n, par, c0):
                    for d in range(2):
                        pe.wait_ge(bd_ready[d], n + (c0 + 1))
                        pe.wait_ge(y_read[d], n + (c0 + 1))
                        for p in range(RT):
                            o = (4 * d + p // 2) * 512 + (p % 2) * 2 * P
                            ins = pe.matmul(ps[:, o:o + 2 * P], b_bd[d][par][:, p],
                                            ar_bd[d][par][:, p].rearrange("p a b -> p (a b)"),
                                            start=True, stop=True)
                        ins.then_inc(pairs_psum[d], 1)
                    for d in range(2):
                        for p in range(RT):
                            o = (4 * d + 2 + p // 2) * 512 + (p % 2) * 2 * P
                            ins = pe.matmul(ps[:, o:o + 2 * P], k_bd[d][par][:, p],
                                            ar_bd[d][par][:, p].rearrange("p a b -> p (a b)"),
                                            start=True, stop=True)
                        ins.then_inc(pairs_psum[d], 1)
                    for d in range(2):
                        pe.wait_ge(masks_ready[d], 3 * n + (3 * c0 + 2))
                        for p in range(RT):
                            ins = pe.transpose(pb(d, 0, p), invT[d][:, p], ident[:, :])
                        ins.then_inc(first_psum[d], 1)
                    for l in range(1, NL + 1):
                        for d in range(2):
                            pe.wait_ge(inv_ready[d], NL * n + (NL * c0 + l))
                            pe.wait_ge(lvl_masked[d], NL * n + (NL * c0 + l))
                            for p in range(RT):
                                ins = pe.matmul(pb(d, 0, p), alv[d][:, l, p], inv[d][:, p],
                                                start=True, stop=True)
                            ins.then_inc(ax_psum[d], 1)
                            if d == 0:
                                for dt, i in TOKENS.get(l, ()):
                                    if i == 0:
                                        pe.wait_ge(vbd_ready[dt], n + (c0 + 2))
                                        pe.wait_ge(masks_ready[dt], 3 * n + (3 * c0 + 3))
                                    else:
                                        pe.wait_ge(tok_read[dt], NTOK * n + (NTOK * c0 + i))
                                    m = (v_bd, b_bd, k_bd)[i]
                                    for p in range(RT):
                                        ins = pe.transpose(pb(dt, 3, p), m[dt][par][:, p], ident[:, :])
                                    ins.then_inc(tok_psum[dt], 1)
                        for d in range(2):
                            pe.wait_ge(prod_ready[d], (NL + 2) * n + ((NL + 2) * c0 + l))
                            if l == 1:
                                pe.wait_ge(masks_ready[d], 3 * n + (3 * c0 + 3))
                            for p in range(RT):
                                if l < NL:
                                    pe.matmul(pb(d, 1, p), invT[d][:, p], prod[d][:, p],
                                              start=True, stop=True)
                                ins = pe.matmul(pb(d, 2, p), prod[d][:, p], invT[d][:, p],
                                                start=True, stop=True)
                            ins.then_inc(xax_psum[d], 1)
                    for d in range(2):
                        pe.wait_ge(state_ready[d], n + (c0 + 1))
                        pe.wait_ge(tok_read[d], NTOK * n + (NTOK * c0 + NTOK))
                        for p in range(RT):
                            pe.matmul(pb(d, 3, p), ar_bd[d][par][:, p, 0], state[d][:, p],
                                      start=True, stop=False)
                            ins = pe.matmul(pb(d, 3, p), km[d][:, p, 0], tokv[d][:, p], start=False, stop=True)
                        ins.then_inc(g_psum[d], 1)
                    for d in range(2):
                        pe.wait_ge(prod_ready[d], (NL + 2) * n + ((NL + 2) * c0 + NL + 1))
                        pe.wait_ge(invT_final[d], n + (c0 + 1))
                        for p in range(RT):
                            ins = pe.matmul(pb(d, 0, p), invT[d][:, p], prod[d][:, p], start=True, stop=True)
                        ins.then_inc(u_psum[d], 1)
                    for d in range(2):
                        for p in range(RT):
                            pe.matmul(pb(d, 1, p), state[d][:, p], ar_bd[d][par][:, p, 1],
                                      start=True, stop=False)
                            pe.matmul(pb(d, 1, p), tokv[d][:, p], km[d][:, p, 1], start=False, stop=False)
                            if p == 0:
                                pe.wait_ge(prod_ready[d], (NL + 2) * n + ((NL + 2) * c0 + NL + 2))
                            pe.matmul(pb(d, 1, p), prod[d][:, p], bm[d][:, p, 1], start=False, stop=True)
                            pe.matmul(pb(d, 2, p), tokb[d][:, p], prod[d][:, p], start=True, stop=False)
                            ins = pe.matmul(pb(d, 2, p), tokk[d][:, p], tokv[d][:, p], start=False, stop=True)
                        ins.then_inc(y_psum[d], 1)

                for t0, nch, c0, pairs in SEGS:
                    with pe.Fori(0, pairs) as i:
                        for par in range(2):
                            chunk(i * 2 + par, par, c0)
                for par in range(2):
                    chunk(LAST + par, par, c0)

            @block.scalar
            def _(act):
                def decays(n, par, c0, d):
                    s = -1.0 if d else 1.0
                    cum, exc = ext[d][:, 0], ext[d][:, 1]
                    act.wait_ge(cum_ready[d], n + (c0 + 1))
                    for slot, src, sign in (((2, exc, 1), (3, cum, 1), (4, cum, -1)) if d == 0 else
                                            ((2, cum, -1), (3, exc, -1), (4, exc, 1))):
                        act.activation(ext[d][:, slot], src, ACT.Exp, scale=sign * DECAY)
                    act.activation(eb[:, par, d, :].unsqueeze(2),
                                   cum.rearrange("p (a b) -> p a b", b=C)[:, :, C - 1:C],
                                   ACT.Exp, scale=DECAY).then_inc(exp_ready[d], 1)

                def v_blocks(par, d):
                    for hh in range(2):
                        r = slice(64 * hh, 64 * hh + 64)
                        ins = act.copy(v_bd[d][par][r, :, 64 * hh:64 * hh + 64],
                                       cin[d][r, 2].rearrange("p (a b) -> p a b", b=C))
                    ins.then_inc(vbd_ready[d], 1)

                def chunk(n, par, c0, more):
                    for d in range(2):
                        act.wait_ge(first_psum[d], n + (c0 + 1))
                        act.copy(inv[d].rearrange("p a b -> p (a b)"), bank(4 * d)).then_inc(inv_ready[d], 1)
                    for l in range(1, NL + 1):
                        for d in range(2):
                            act.wait_ge(ax_psum[d], NL * n + (NL * c0 + l))
                            act.copy(prod[d].rearrange("p a b -> p (a b)"),
                                     bank(4 * d)).then_inc(prod_ready[d], 1)
                            if d == 0:
                                for dt, i in TOKENS.get(l, ()):
                                    act.wait_ge(tok_psum[dt], NTOK * n + (NTOK * c0 + i + 1))
                                    act.copy((tokv, tokb, tokk)[i][dt].rearrange("p a b -> p (a b)"),
                                             bank(4 * dt + 3)).then_inc(tok_read[dt], 1)
                        if more and l in (2, 3):
                            decays(n + 1, 1 - par, c0, l - 2)
                        if more and l == 4:
                            for d in range(2):
                                v_blocks(1 - par, d)
                    for d in range(2):
                        act.wait_ge(g_psum[d], n + (c0 + 1))
                        act.copy(prod[d].rearrange("p a b -> p (a b)"),
                                 bank(4 * d + 3)).then_inc(prod_ready[d], 1)
                    for d in range(2):
                        act.wait_ge(u_psum[d], n + (c0 + 1))
                        act.copy(prod[d].rearrange("p a b -> p (a b)"),
                                 bank(4 * d)).then_inc(prod_ready[d], 1)

                for d in range(2):
                    act.drain().then_inc(vbd_ready[d], 1)
                for d in range(2):
                    decays(0, 0, 0, d)
                    v_blocks(0, d)
                for t0, nch, c0, pairs in SEGS:
                    with act.Fori(0, pairs) as i:
                        for par in range(2):
                            chunk(i * 2 + par, par, c0, True)
                for par in range(2):
                    chunk(LAST + par, par, c0, par == 0)

            @block.vector
            def _(v):
                def tiles(x):
                    return x.rearrange("p (a b) -> p a b", b=C)

                def sums(n, c0, d):
                    r_, k_, v_, kk_, sig_, ic_ = (cin[d][:, q] for q in range(6))
                    cum, exc, ea, er, ebk, t1, t2 = (ext[d][:, q] for q in range(7))
                    v.wait_ge(cin_in[d], 96 * n + (96 * c0 + 96))
                    v.tensor_tensor_scan(cum, restart[:, :], sig_, 0.0, ALU.mult, ALU.add)
                    v.tensor_tensor(t1, kk_, ic_, ALU.mult)
                    v.scalar_tensor_tensor(
                        tiles(t2), tiles(ic_), -1.0,
                        pars[:, P_KA:P_KA + RT].unsqueeze(2).broadcast_to([P, RT, C]), ALU.add, ALU.mult)
                    v.drain()
                    v.tensor_tensor(exc, cum, sig_, ALU.subtract).then_inc(cum_ready[d], 1)
                    v.scalar_tensor_tensor(t2, t2, 1.0, k_, ALU.add, ALU.mult)
                    v.drain()

                def blocks(n, par, c0, d):
                    r_, k_, v_, kk_, sig_, ic_ = (cin[d][:, q] for q in range(6))
                    cum, exc, ea, er, ebk, t1, t2 = (ext[d][:, q] for q in range(7))
                    v.wait_ge(exp_ready[d], n + (c0 + 1))
                    for hh in range(2):
                        r = slice(64 * hh, 64 * hh + 64)
                        c = slice(64 * hh, 64 * hh + 64)
                        v.scalar_tensor_tensor(ar_bd[d][par][r, :, 0, c], tiles(kk_)[r], -1.0, tiles(ea)[r],
                                               ALU.mult, ALU.mult)
                        v.tensor_tensor(ar_bd[d][par][r, :, 1, c], tiles(r_)[r], tiles(er)[r], ALU.mult)
                        v.tensor_tensor(b_bd[d][par][r, :, c], tiles(t1)[r], tiles(ebk)[r], ALU.mult)
                        v.tensor_tensor(k_bd[d][par][r, :, c], tiles(t2)[r], tiles(ebk)[r], ALU.mult)
                    v.drain().then_inc(bd_ready[d], 1)
                    v.drain().then_inc(cin_free[d], 1)

                def mask_pairs(d, m, b):
                    for half in range(2):
                        v.tensor_tensor(m[d][:, 2 * half:2 * half + 2].rearrange("p a b c -> p a (b c)"),
                                        bank(4 * d + b + half).rearrange("p (a b) -> p a b", b=2 * P),
                                        causal[:, d:d + 1, :].broadcast_to([P, 2, 2 * P]), ALU.mult)

                def chunk(n, par, t0, nch, c0, more):
                    for d in range(2):
                        v.drain().then_inc(state_ready[d], 1)
                    for d in range(2):
                        v.wait_ge(pairs_psum[d], 2 * n + (2 * c0 + 1))
                        mask_pairs(d, bm, 0)
                        v.drain().then_inc(masks_ready[d], 1)
                        v.tensor_tensor(alv[d][:, 0], bm[d][:, :, 0],
                                        lvl[:, d, 0:1, :].broadcast_to([P, RT, P]), ALU.mult)
                        v.drain()
                        v.tensor_tensor(invT[d], alv[d][:, 0],
                                        ident[:, :].unsqueeze(1).broadcast_to([P, RT, P]),
                                        ALU.add).then_inc(masks_ready[d], 1)
                    for d in range(2):
                        v.wait_ge(pairs_psum[d], 2 * n + (2 * c0 + 2))
                        mask_pairs(d, km, 2)
                        v.drain().then_inc(masks_ready[d], 1)
                    for l in range(1, NL + 1):
                        for d in range(2):
                            v.wait_ge(xax_psum[d], NL * n + (NL * c0 + l))
                            if l < NL:
                                v.tensor_tensor(inv[d].rearrange("p a b -> p (a b)"),
                                                inv[d].rearrange("p a b -> p (a b)"), bank(4 * d + 1), ALU.add)
                            v.tensor_tensor(invT[d].rearrange("p a b -> p (a b)"),
                                            invT[d].rearrange("p a b -> p (a b)"), bank(4 * d + 2), ALU.add)
                            v.drain().then_inc(inv_ready[d] if l < NL else invT_final[d], 1)
                        if more and l in (1, 2):
                            sums(n + 1, c0, l - 1)
                        if more and l in (3, 4):
                            blocks(n + 1, 1 - par, c0, l - 3)
                    for d in range(2):
                        v.wait_ge(y_psum[d], n + (c0 + 1))
                        v.tensor_copy(carry[0:1, 0:1], carry[0:1, 1:2])
                        for hh in range(2):
                            r = slice(64 * hh, 64 * hh + 64)
                            first = n * C + t0 if d == 0 else (nch - 1) * C + t0 - n * C
                            y = yacc[r, :, ds(first, C)]
                            v.tensor_tensor(y, y, bank(4 * d + 1).rearrange("p (a b) -> p a b", b=P)
                                            [r, :, 64 * hh:64 * hh + 64], ALU.add)
                        v.tensor_tensor(state[d][:, :, :].rearrange("p a b -> p (a b)"),
                                        state[d][:, :, :].rearrange("p a b -> p (a b)"),
                                        bank(4 * d + 2), ALU.add)
                        v.drain().then_inc(y_read[d], 1)
                        if d == 0 or more:
                            v.tensor_tensor(state[d][:, :, :], state[d][:, :, :],
                                            eb[:, par if d == 0 else 1 - par, d, :].unsqueeze(2)
                                            .broadcast_to([P, RT, P]), ALU.mult)
                    v.drain()

                for d in range(2):
                    v.drain().then_inc(cin_free[d], 1)
                    v.drain().then_inc(y_read[d], 1)
                v.memset(at(o3, RT * 10 * P), 0.0)
                v.drain()
                for d in range(2):
                    sums(0, 0, d)
                for d in range(2):
                    blocks(0, 0, 0, d)
                v.wait_ge(zeroed, 1)
                for t0, nch, c0, pairs in SEGS:
                    for d in range(2):
                        v.memset(state[d][:, :, :].rearrange("p a b -> p (a b)"), 0.0)
                    v.drain()
                    with v.Fori(0, pairs) as i:
                        for par in range(2):
                            chunk(i * 2 + par, par, t0, nch, c0, True)
                for par in range(2):
                    chunk(LAST + par, par, t0, nch, c0, par == 0)

        bonus = at(A_, RT, NT)
        gate = at(R2, RT, NT)
        cen = at(A_ + RT * NT, 2, NT)
        csq = at(A_ + (RT + 2) * NT, 2, NT)
        wo_raw = at(D_ + 2 * D, KD, D)
        assert KD == 2 * RT
        wo2 = at(D_, KD * D).bitcast(F16).rearrange("p (k w n) -> p k w n", k=KD, w=2)
        o8 = D_ + (KD + 2) * D
        x6 = at(o8, 2, D)
        ot2 = at(o8 + 2 * D, 2 * KD * P).bitcast(F16).rearrange("p (b x k n) -> p b x k n", b=2, x=2, k=KD)
        h6 = at(o8 + 4 * D, 2, D)
        hT6 = at(o8 + 6 * D, 2, KD, P)
        o9 = o8 + 8 * D
        wr = at(o9, KD, NE)
        g2n = at(o9 + KD * NE, D)
        junk6 = at(o9 + KD * NE + D, D)
        logit = at(o9 + KD * NE + 2 * D, NTT, NE)
        lstat = at(o9 + KD * NE + 2 * D + NTT * NE, 2, NTT)
        aff = at(o9 + KD * NE + 2 * D + NTT * NE + 2 * NTT, NT)[0:NE]
        assert o9 + KD * NE + 2 * D + NTT * NE + 2 * NTT + NT <= E_ + 2 * KD * P + 2 * (NT + 3)
        inv_s = at(o9 + KD * NE + D, 2, NT)
        assert o9 + KD * NE + D + 2 * NT <= E_ + 2 * KD * P + 2 * (NT + 3)
        post_in = sem("post_in")
        wo_in = sem("wo_in")
        wo_hi = sem("wo_hi")
        wo_lo = sem("wo_lo")
        x6_in = [sem(f"x6_in{b}") for b in range(2)]
        normed_ready = sem("normed_ready")
        sum_psum = sem("sum_psum")
        centred = sem("centred")
        var_psum = sem("var_psum")
        std_ready = sem("std_ready")
        post_done = sem("post_done")

        with nc.Block() as block:
            @block.sync
            def _(sp):
                sp.dma_start(bonus, feat[F_BONUS:F_BONUS + RT].rearrange("t p n -> p t n")).then_inc(post_in, 16)
                sp.dma_start(gate, feat[F_GATE:F_GATE + RT].rearrange("t p n -> p t n")).then_inc(post_in, 16)
                sp.dma_start(wo_raw, w_out.rearrange("(k p) n -> p k n", p=P)).then_inc(wo_in, 16)
                sp.dma_start(wr, w_router.rearrange("(k p) n -> p k n", p=P)).then_inc(wo_in, 16)
                sp.dma_start(g2n, gains[1:2, :].partition_broadcast(P)).then_inc(wo_in, 16)
                for b in range(2):
                    sp.dma_start(x6[:, b], tokens[b * P:(b + 1) * P, :]).then_inc(x6_in[b], 16)

            @block.gpsimd
            def _(pool):
                pool.wait_ge(post_in, 32)
                for f in range(RT):
                    for k in (2 * f, 2 * f + 1):
                        pool.wait_ge(wo_hi, k + 1)
                        pool.tensor_tensor(wo2[:, k, 1], wo_raw[:, k], wo2[:, k, 0], ALU.subtract).then_inc(wo_lo, 1)
                    pool.wait_ge(normed_ready, f + 1)
                    pool.tensor_tensor(yacc[:, f], cen[:, f % 2], gate[:, f], ALU.mult).then_inc(post_done, 1)

            @block.tensor
            def _(pe):
                def head_sum(b, src):
                    for o, c in CHUNKS:
                        ins = pe.matmul(ps[:, b * 2048 + o:b * 2048 + o + c], onesbd[:, :], src[:, o:o + c],
                                        start=True, stop=True)
                    return ins

                for f in range(RT):
                    if f:
                        pe.wait_ge(centred, f)
                    head_sum(0, yacc[:, f]).then_inc(sum_psum, 1)
                    pe.wait_ge(std_ready, 2 * f + 1)
                    head_sum(1, csq[:, f % 2]).then_inc(var_psum, 1)

            @block.scalar
            def _(act):
                for f in range(RT):
                    act.wait_ge(centred, f + 1)
                    act.activation(csq[:, f % 2], cen[:, f % 2], ACT.Square).then_inc(std_ready, 1)
                    act.wait_ge(var_psum, f + 1)
                    if f >= 2:
                        act.wait_ge(normed_ready, f - 1)
                    act.activation(inv_s[:, f % 2], ps[:, 2048:2048 + NT], ACT.Sqrt, bias=cst[:, 1:2],
                                   scale=1.0 / 64).then_inc(std_ready, 1)
                    if f == 0:
                        act.wait_ge(wo_in, 48)
                    for k in (2 * f, 2 * f + 1):
                        act.activation(wo_raw[:, k], wo_raw[:, k], ACT.Copy, scale=W_SCALE)
                        act.drain()
                        if k >= 2:
                            act.wait_ge(wo_lo, k - 1)
                        act.copy(wo2[:, k, 0], wo_raw[:, k]).then_inc(wo_hi, 1)

            @block.vector
            def _(v):
                def centre(f):
                    v.wait_ge(sum_psum, f + 1)
                    if f >= 2:
                        v.wait_ge(post_done, f - 1)
                    v.scalar_tensor_tensor(cen[:, f % 2], ps[:, 0:NT], -1.0 / 64, yacc[:, f],
                                           ALU.mult, ALU.add).then_inc(centred, 1)

                centre(0)
                v.wait_ge(post_in, 32)
                for f in range(RT):
                    if f + 1 < RT:
                        centre(f + 1)
                    v.wait_ge(std_ready, 2 * f + 2)
                    v.reciprocal(inv_s[:, f % 2], inv_s[:, f % 2])
                    v.drain()
                    v.scalar_tensor_tensor(cen[:, f % 2], cen[:, f % 2], pars[:, P_LW + f:P_LW + f + 1],
                                           inv_s[:, f % 2], ALU.mult, ALU.mult)
                    v.drain()
                    v.scalar_tensor_tensor(cen[:, f % 2], cen[:, f % 2], pars[:, P_LB + f:P_LB + f + 1],
                                           bonus[:, f], ALU.add, ALU.add).then_inc(normed_ready, 1)

        RING = 6
        AHEAD = 5
        WCH = 2048
        ring = [at(A_ + n * WCH, WCH) for n in range(RING)]
        ot_ready = sem("ot_ready")
        out_psum = sem("out_psum")
        x2_ready = sem("x2_ready")
        x2_stored = [sem(f"x2_stored{b}") for b in range(2)]
        h6_stored = [sem(f"h6_stored{b}") for b in range(2)]
        rms6_ready = sem("rms6_ready")
        h6_ready = sem("h6_ready")
        h6T_psum = sem("h6T_psum")
        h6T_ready = sem("h6T_ready")
        logit_psum = sem("logit_psum")
        logit_read = sem("logit_read")
        exp_done = sem("exp_done")
        aff_ready = sem("aff_ready")
        affT_psum = sem("affT_psum")
        affT_read = sem("affT_read")
        w_in_ring = [sem(f"w_in_ring{n}") for n in range(RING)]

        def weight_chunk(k, e):
            if k < 16:
                w, rows, cols = (w_gate, w_up)[k // 2 % 2], k % 2 * (D // 2), k // 4 * 512
                return w[ds(e, 1), rows:rows + D // 2, cols:cols + 512].rearrange("o (k p) n -> p (o k) n", p=P)
            return w_down[ds(e, 1), (k - 16) * 256:(k - 15) * 256, :].rearrange("o (k p) n -> p (o k) n", p=P)

        def slot(k):
            return ring[k % RING].rearrange("p (a b) -> p a b", b=512 if k < 16 else D)

        with nc.Block() as block:
            @block.sync
            def _(sp):
                for k in range(AHEAD):
                    sp.dma_start(slot(k), weight_chunk(k, 0)).then_inc(w_in_ring[k], 16)

                def store(j, b):
                    rows = ds((2 * j + b) * P, P)
                    sp.wait_ge(x2_ready, 2 * j + b + 1)
                    sp.dma_start(resid[rows, :], x6[:, b]).then_inc(x2_stored[b], 16)
                    sp.wait_ge(h6_ready, 2 * j + b + 1)
                    sp.dma_start(h2[rows, :], h6[:, b]).then_inc(h6_stored[b], 16)

                with sp.Fori(0, NTT // 2 - 1) as j:
                    for b in range(2):
                        store(j, b)
                        sp.wait_ge(x2_stored[b], 16 * j + 16)
                        sp.dma_start(x6[:, b], tokens[ds((2 * j + b + 2) * P, P), :]).then_inc(x6_in[b], 16)
                for b in range(2):
                    store(NTT // 2 - 1, b)
                for b in range(2):
                    sp.wait_ge(x2_stored[b], 16 * (NTT // 2))
                    sp.wait_ge(h6_stored[b], 16 * (NTT // 2) + 16)

            @block.gpsimd
            def _(pool):
                with pool.Fori(0, NTT // 2) as j:
                    for b in range(2):
                        pool.wait_ge(out_psum, 2 * j + b + 1)
                        src = qk[:, :, ds((2 * j + b) * P, P)]
                        pool.tensor_copy(ot2[:, b, 0], src)
                        pool.drain()
                        pool.tensor_tensor(ot2[:, b, 1], src, ot2[:, b, 0], ALU.subtract).then_inc(ot_ready, 1)

            @block.tensor
            def _(pe):
                pe.drain().then_inc(out_psum, 2)
                pe.wait_ge(wo_in, 48)

                def project(t, b, half):
                    for k in range(KD):
                        for n, (x, w) in enumerate(PRODUCTS):
                            ins = pe.matmul(bank(2 * b + half), ot2[:, b, x, k],
                                            wo2[:, k, w, half * 512:(half + 1) * 512],
                                            start=(k == 0 and n == 0), stop=(k == KD - 1 and n == 2))
                    return ins

                def turn(t, b):
                    pe.wait_ge(h6_ready, t + 1)
                    for k in range(KD):
                        o = (4 + k // 4) * 512 + (k % 4) * P
                        ins = pe.transpose(ps[:, o:o + P], h6[:, b, k * P:(k + 1) * P], ident[:, :])
                    ins.then_inc(h6T_psum, 1)

                def route(t, b):
                    pe.wait_ge(h6T_ready, t + 1)
                    pe.wait_ge(logit_read, t + 1)
                    for k in range(KD):
                        ins = pe.matmul(bank(6, NE), hT6[:, b, k], wr[:, k], start=(k == 0), stop=(k == KD - 1))
                    ins.then_inc(logit_psum, 1)

                def tile(t, b, before):
                    pe.wait_ge(ot_ready, t + 1)
                    project(t, b, 0)
                    if before is not None:
                        turn(before, 1 - b)
                    project(t, b, 1).then_inc(out_psum, 1)
                    if before is not None:
                        route(before, 1 - b)

                tile(0, 0, None)
                tile(1, 1, 0)
                with pe.Fori(0, NTT // 2 - 1) as j:
                    for b in range(2):
                        tile(j * 2 + (2 + b), b, j * 2 + (1 + b))
                turn(NTT - 1, 1)
                route(NTT - 1, 1)
                pe.wait_ge(aff_ready, 2)
                for t in range(NTT):
                    if t >= 2:
                        pe.wait_ge(affT_read, t - 1)
                    pe.transpose(ps[0:NE, (t % 2) * 512:(t % 2) * 512 + P], logit[:, t], ident[:, :]).then_inc(affT_psum, 1)

            @block.scalar
            def _(act):
                act.drain().then_inc(logit_read, 1)
                def root(t, b):
                    act.wait_ge(x2_ready, t + 1)
                    act.activation(junk6, x6[:, b], ACT.Square, accum_out=small[:, b:b + 1])
                    act.drain()
                    act.activation(small[:, 2 + b:3 + b], small[:, b:b + 1], ACT.Sqrt,
                                   bias=cst[:, 0:1], scale=1.0 / D).then_inc(rms6_ready, 1)

                def keep(t, b):
                    act.wait_ge(h6T_psum, t + 1)
                    act.copy(hT6[:, b].rearrange("p a b -> p (a b)"),
                             ps[:, 2048:2048 + D]).then_inc(h6T_ready, 1)
                    act.wait_ge(logit_psum, t + 1)
                    act.copy(logit[:, ds(t, 1)].rearrange("p a b -> p (a b)"),
                             bank(6, NE)).then_inc(logit_read, 1)

                root(0, 0)
                with act.Fori(0, NTT // 2 - 1) as j:
                    for b in range(2):
                        keep(j * 2 + b, b)
                        root(j * 2 + (b + 1), 1 - b)
                keep(NTT - 2, 0)
                root(NTT - 1, 1)
                keep(NTT - 1, 1)
                act.wait_ge(aff_ready, 1)
                act.activation(logit.rearrange("p a b -> p (a b)"), logit.rearrange("p a b -> p (a b)"),
                               ACT.Exp).then_inc(exp_done, 1)
                for t in range(NTT):
                    act.wait_ge(affT_psum, t + 1)
                    act.copy(aff[:, t * P:(t + 1) * P],
                             ps[0:NE, (t % 2) * 512:(t % 2) * 512 + P]).then_inc(affT_read, 1)

            @block.vector
            def _(v):
                for b in range(2):
                    v.drain().then_inc(h6_stored[b], 16)
                v.wait_ge(wo_in, 48)
                with v.Fori(0, NTT // 2) as j:
                    for b in range(2):
                        v.wait_ge(out_psum, 2 * j + b + 3)
                        v.wait_ge(x6_in[b], 16 * j + 16)
                        v.scalar_tensor_tensor(x6[:, b], ps[:, b * 1024:(b + 1) * 1024], 1.0 / W_SCALE,
                                               x6[:, b], ALU.mult, ALU.add).then_inc(x2_ready, 1)
                        v.wait_ge(rms6_ready, 2 * j + b + 1)
                        v.reciprocal(small[:, 4 + b:5 + b], small[:, 2 + b:3 + b])
                        v.drain()
                        v.wait_ge(h6_stored[b], 16 * j + 16)
                        v.scalar_tensor_tensor(h6[:, b], x6[:, b], small[:, 4 + b:5 + b], g2n,
                                               ALU.mult, ALU.mult).then_inc(h6_ready, 1)
                        v.drain()
                v.wait_ge(logit_read, NTT + 1)
                v.tensor_reduce(lstat[:, 0], logit, AX, ALU.max)
                v.drain()
                v.tensor_tensor(logit, logit, lstat[:, 0].unsqueeze(2).broadcast_to([P, NTT, NE]), ALU.subtract)
                v.drain().then_inc(aff_ready, 1)
                v.wait_ge(exp_done, 1)
                v.tensor_reduce(lstat[:, 1], logit, AX, ALU.add)
                v.drain()
                v.reciprocal(lstat[:, 1], lstat[:, 1])
                v.drain()
                v.tensor_tensor(logit, logit, lstat[:, 1].unsqueeze(2).broadcast_to([P, NTT, NE]), ALU.mult)
                v.drain().then_inc(aff_ready, 1)

        SPLIT = 12
        LAG = 4
        split = [at(A_ + (RING + n) * WCH, WCH).bitcast(F16) for n in range(SPLIT)]

        def part(k, lo):
            return split[k % SPLIT][:, lo * WCH:(lo + 1) * WCH].rearrange("p (a b) -> p a b", b=512 if k < 16 else D)

        o10 = (RING + SPLIT) * WCH
        val = at(o10, SLOTS)[0:NE]
        idx = sb("idx", [NE, SLOTS], U32)
        idxf = at(o10 + SLOTS, SLOTS)[0:NE]
        gsel = sb("gsel", [P, 2, NE])
        isel = sb("isel", [P, 2, NE + 1])
        gate_e = sb("gate_e", [P, 2])
        icol = sb("icol", [P, 2, 2], U32)
        xe = at(o10 + 2 * SLOTS, D)
        xs = at(o10 + 2 * SLOTS + D, D)
        o11 = o10 + 2 * SLOTS + 2 * D
        xT2 = at(o11, KD * SLOTS).bitcast(F16).rearrange("p (w a b) -> p w a b", w=2, b=SLOTS)
        o12 = o11 + KD * SLOTS
        NFT = FF // P
        hid2 = at(o12, NFT * SLOTS).bitcast(F16).rearrange("p (w a b) -> p w a b", w=2, b=SLOTS)
        o13 = o12 + NFT * SLOTS
        sil = at(o13, 2, SLOTS)
        h32 = at(o13 + 2 * SLOTS, 2, SLOTS)
        ye = at(o13 + 4 * SLOTS, D)
        ys = at(o13 + 4 * SLOTS + D, D)
        assert o12 <= o9 and o13 + 4 * SLOTS + 2 * D <= E_ + 2 * KD * P + 2 * (NT + 3)
        NK = 24
        NP = 2
        PW = WCH // NP
        vi_ready = sem("vi_ready")
        vi_psum = sem("vi_psum")
        icol_ready = sem("icol_ready")
        rows_in = sem("rows_in")
        xT_psum = sem("xT_psum")
        xT_hi = sem("xT_hi")
        xT_ready = sem("xT_ready")
        w_hi = sem("w_hi")
        w_split = sem("w_split")
        gu_psum = sem("gu_psum")
        silu_ready = sem("silu_ready")
        hid_ready = sem("hid_ready")
        down_psum = sem("down_psum")
        y_gated = sem("y_gated")
        added = sem("added")
        gate_ready = sem("gate_ready")
        rows_free = sem("rows_free")
        PASSES = ((0, 0), (0, 1), (1, 0))

        with nc.Block() as block:
            @block.sync
            def _(sp):
                def load(k, e):
                    sp.dma_start(slot(k), weight_chunk(k, e)).then_inc(w_in_ring[k % RING], 16)

                for k in range(AHEAD, RING):
                    load(k, 0)
                for k in range(RING, NK):
                    sp.wait_ge(w_split, NP * (k - RING + 1))
                    load(k, 0)
                with sp.Fori(1, NE) as e:
                    for k in range(NK):
                        sp.wait_ge(w_split, NP * NK * e + NP * (k - RING + 1))
                        load(k, e)

            @block.gpsimd
            def _(pool):
                def gather(e):
                    pool.wait_ge(icol_ready, e + 1)
                    pool.wait_ge(xT_psum, e + 1)
                    pool.tensor_tensor(carry[0:1, 2:3], carry[0:1, 1:2], carry[0:1, 1:2], ALU.add)
                    pool.drain()
                    for g, (dst, n) in enumerate(((xe, CAP0), (xs, CAP1))):
                        pool.indirect_dma_start(dst[0:n], None, h2[:, :],
                                                bass.IndirectOffsetOnAxis(ap=icol[0:n, 0, g:g + 1], axis=0)
                                                ).then_inc(rows_in, 16)

                def add_rows(e):
                    pool.wait_ge(y_gated, e + 2)
                    pool.tensor_tensor(carry[0:1, 2:3], carry[0:1, 1:2], carry[0:1, 1:2], ALU.add)
                    pool.drain()
                    for g, (src, n) in enumerate(((ye, CAP0), (ys, CAP1))):
                        pool.indirect_dma_start(resid[:, :],
                                                bass.IndirectOffsetOnAxis(ap=icol[0:n, 1, g:g + 1], axis=0),
                                                src[0:n], None, compute_op=ALU.add).then_inc(added, 16)
                    pool.wait_ge(added, 32 * e + 32)
                    pool.tensor_tensor(carry[0:1, 2:3], carry[0:1, 1:2], carry[0:1, 1:2], ALU.add)
                    pool.drain()
                    pool.drain().then_inc(rows_free, 1)

                pool.drain().then_inc(rows_free, 1)
                gather(0)
                with pool.Fori(0, NE - 1) as e:
                    gather(e + 1)
                    add_rows(e)
                add_rows(NE - 1)

            @block.tensor
            def _(pe):
                pe.drain().then_inc(xT_psum, 1)
                pe.wait_ge(vi_ready, 1)
                for n, src in enumerate((val, idxf)):
                    pe.transpose(ps[:, n * 512:n * 512 + NE], src[:, 0:CAP0], ident[0:NE, 0:NE])
                    ins = pe.transpose(ps[0:CAP1, n * 512 + NE:n * 512 + 2 * NE], src[:, CAP0:SLOTS],
                                       ident[0:NE, 0:NE])
                ins.then_inc(vi_psum, 1)

                def turn(e):
                    pe.wait_ge(rows_in, 32 * e + 32)
                    for k in range(KD):
                        o = (5 + k // 3) * 512 + (k % 3) * SLOTS
                        pe.transpose(ps[:, o:o + CAP0], xe[:, k * P:(k + 1) * P], ident[:, :])
                        ins = pe.transpose(ps[:, o + CAP0:o + SLOTS], xs[0:CAP1, k * P:(k + 1) * P],
                                           ident[0:CAP1, 0:CAP1])
                    ins.then_inc(xT_psum, 1)

                def gate_up(e):
                    pe.wait_ge(xT_ready, e + 1)
                    for c in range(4):
                        pe.wait_ge(w_split, NP * NK * e + NP * (4 * c + 4))
                        for f in range(4):
                            n = 4 * c + f
                            pe.wait_ge(hid_ready, NFT * e + (n + 1))
                            for w in range(2):
                                o = (n % 2) * 512 + w * SLOTS
                                for k in range(KD):
                                    for i, (pw, px) in enumerate(PASSES):
                                        ins = pe.matmul(ps[:, o:o + SLOTS],
                                                        part(4 * c + 2 * w + k // 4, pw)
                                                        [:, k % 4, f * P:(f + 1) * P], xT2[:, px, k],
                                                        start=(k == 0 and i == 0), stop=(k == KD - 1 and i == 2))
                            ins.then_inc(gu_psum, 1)

                def down(e):
                    pe.wait_ge(y_gated, e + 1)
                    for c in range(8):
                        k = 16 + c
                        pe.wait_ge(w_split, NP * NK * e + NP * (k + 1))
                        for f in range(2):
                            n = 2 * c + f
                            pe.wait_ge(hid_ready, NFT * e + (n + 3))
                            for i, (pw, px) in enumerate(PASSES):
                                first, last = n == 0 and i == 0, n == NFT - 1 and i == 2
                                for half in range(2):
                                    pe.matmul(bank(2 + half), hid2[:, px, n, 0:CAP0],
                                              part(k, pw)[:, f, half * 512:(half + 1) * 512],
                                              start=first, stop=last)
                            for i, (pw, px) in enumerate(PASSES):
                                first, last = n == 0 and i == 0, n == NFT - 1 and i == 2
                                for q in range(4):
                                    ins = pe.matmul(ps[32 * q:32 * q + 32, 4 * 512:4 * 512 + D // 4],
                                                    hid2[:, px, n, CAP0:SLOTS],
                                                    part(k, pw)[:, f, q * 256:(q + 1) * 256],
                                                    start=first, stop=last)
                        ins.then_inc(down_psum, 1)

                turn(0)
                with pe.Fori(0, NE - 1) as e:
                    gate_up(e)
                    turn(e + 1)
                    down(e)
                gate_up(NE - 1)
                down(NE - 1)

            @block.scalar
            def _(act):
                def hi(k, e, pieces):
                    for q in pieces:
                        if q == 0:
                            act.wait_ge(w_in_ring[k % RING], 16 * (NK // RING) * e + 16 * (k // RING + 1))
                        act.activation(split[k % SPLIT][:, q * PW:(q + 1) * PW], ring[k % RING][:, q * PW:(q + 1) * PW],
                                       ACT.Copy, scale=W_SCALE).then_inc(w_hi, 1)

                def rows_hi(e):
                    act.wait_ge(xT_psum, e + 2)
                    for k in range(0, KD, 3):
                        w = min(3, KD - k)
                        ins = act.copy(xT2[:, 0, k:k + w].rearrange("p a b -> p (a b)"),
                                       ps[:, (5 + k // 3) * 512:(5 + k // 3) * 512 + w * SLOTS])
                    ins.then_inc(xT_hi, 1)

                def ahead(k, e, last):
                    if k < NK:
                        hi(k, e, range(NP))
                    elif not last:
                        hi(k - NK, e + 1, range(NP))

                def expert(e, last):
                    for n in range(NFT):
                        act.wait_ge(gu_psum, NFT * e + (n + 1))
                        act.wait_ge(hid_ready, NFT * e + (n + 1))
                        act.activation(sil[:, n % 2], ps[:, (n % 2) * 512:(n % 2) * 512 + SLOTS],
                                       ACT.Silu, scale=1.0 / W_SCALE).then_inc(silu_ready, 1)
                        ahead(n + SPLIT - LAG, e, last)
                    if not last:
                        rows_hi(e + 1)
                    for c in range(8):
                        if c and not last:
                            act.wait_ge(down_psum, 8 * e + c)
                        ahead(16 + c + SPLIT - LAG, e, last)
                    act.wait_ge(gate_ready, e + 1)
                    act.wait_ge(down_psum, 8 * e + 8)
                    act.activation(ye, ps[:, 1024:2048], ACT.Copy, scale=gate_e[:, 0:1])
                    for q in range(4):
                        act.copy(ys[0:CAP1, q * 256:(q + 1) * 256], ps[32 * q:32 * q + 32, 2048:2048 + 256])
                    act.drain()
                    act.activation(ys[0:CAP1], ys[0:CAP1], ACT.Copy, scale=gate_e[0:CAP1, 1:2]).then_inc(y_gated, 1)

                act.drain().then_inc(y_gated, 1)
                for k in range(RING):
                    hi(k, 0, range(NP))
                rows_hi(0)
                for k in range(RING, SPLIT - LAG):
                    hi(k, 0, range(NP))
                with act.Fori(0, NE - 1) as e:
                    expert(e, False)
                expert(NE - 1, True)

            @block.vector
            def _(v):
                def lo(k, e, pieces):
                    for q in pieces:
                        v.wait_ge(w_hi, NP * NK * e + (NP * k + q + 1))
                        v.scalar_tensor_tensor(split[k % SPLIT][:, WCH + q * PW:WCH + (q + 1) * PW],
                                               ring[k % RING][:, q * PW:(q + 1) * PW], W_SCALE,
                                               split[k % SPLIT][:, q * PW:(q + 1) * PW],
                                               ALU.mult, ALU.subtract).then_inc(w_split, 1)

                def rows_lo(e):
                    v.wait_ge(xT_hi, e + 1)
                    for k in range(0, KD, 3):
                        w = min(3, KD - k)
                        ins = v.tensor_tensor(xT2[:, 1, k:k + w].rearrange("p a b -> p (a b)"),
                                              ps[:, (5 + k // 3) * 512:(5 + k // 3) * 512 + w * SLOTS],
                                              xT2[:, 0, k:k + w].rearrange("p a b -> p (a b)"), ALU.subtract)
                    ins.then_inc(xT_ready, 1)

                def ahead(k, e, last):
                    if k < NK:
                        lo(k, e, range(NP))
                    elif not last:
                        lo(k - NK, e + 1, range(NP))

                def expert(e, last):
                    v.wait_ge(rows_in, 32 * e + 32)
                    v.tensor_copy(icol[:, 0, 0:1], isel[:, 0, ds(e + 1, 1)])
                    v.tensor_copy(icol[0:CAP1, 0, 1:2], isel[0:CAP1, 1, ds(e + 1, 1)])
                    v.drain().then_inc(icol_ready, 1)
                    for n in range(NFT):
                        v.wait_ge(silu_ready, NFT * e + (n + 1))
                        v.scalar_tensor_tensor(h32[:, n % 2],
                                               ps[:, (n % 2) * 512 + SLOTS:(n % 2) * 512 + 2 * SLOTS],
                                               1.0 / W_SCALE, sil[:, n % 2], ALU.mult, ALU.mult)
                        v.scalar_tensor_tensor(hid2[:, 0, n],
                                               ps[:, (n % 2) * 512 + SLOTS:(n % 2) * 512 + 2 * SLOTS],
                                               1.0 / W_SCALE, sil[:, n % 2], ALU.mult, ALU.mult)
                        v.drain()
                        v.tensor_tensor(hid2[:, 1, n], h32[:, n % 2], hid2[:, 0, n], ALU.subtract).then_inc(hid_ready, 1)
                        ahead(n + SPLIT - LAG, e, last)
                    if not last:
                        rows_lo(e + 1)
                    v.wait_ge(rows_free, e + 1)
                    v.tensor_copy(icol[:, 1, 0:1], isel[:, 0, ds(e, 1)])
                    v.tensor_copy(icol[0:CAP1, 1, 1:2], isel[0:CAP1, 1, ds(e, 1)])
                    for g in range(2):
                        v.tensor_scalar(gate_e[:, g:g + 1], gsel[:, g, ds(e, 1)], 1.0 / W_SCALE, None, ALU.mult)
                    v.drain().then_inc(gate_ready, 1)
                    for c in range(8):
                        ahead(16 + c + SPLIT - LAG, e, last)

                v.memset(isel[:, :, :].rearrange("p a b -> p (a b)"), 0.0)
                v.memset(gsel[:, :, :].rearrange("p a b -> p (a b)"), 0.0)
                for first, n, o, cap in ((0, T0, 0, CAP0), (T0, T1, CAP0, CAP1)):
                    row = aff[:, first:first + n]
                    for r in range(cap // 8):
                        top = val[:, o + 8 * r:o + 8 * r + 8]
                        v.max(top, row)
                        v.drain()
                        v.max_index(idx[:, o + 8 * r:o + 8 * r + 8], top, row)
                        if r < cap // 8 - 1:
                            v.drain()
                            v.match_replace(row, top, row, -1.0)
                            v.drain()
                v.drain()
                v.tensor_copy(idxf, idx[:, :])
                v.drain()
                v.tensor_scalar(idxf[:, CAP0:SLOTS], idxf[:, CAP0:SLOTS], float(T0), None, ALU.add)
                v.drain().then_inc(vi_ready, 1)
                v.wait_ge(vi_psum, 1)
                for n, dst in enumerate((gsel, isel)):
                    v.tensor_copy(dst[:, 0, 0:NE], ps[:, n * 512:n * 512 + NE])
                    v.tensor_copy(dst[0:CAP1, 1, 0:NE], ps[0:CAP1, n * 512 + NE:n * 512 + 2 * NE])
                v.drain()
                v.tensor_copy(icol[:, 0, 0:1], isel[:, 0, 0:1])
                v.tensor_copy(icol[0:CAP1, 0, 1:2], isel[0:CAP1, 1, 0:1])
                v.drain().then_inc(icol_ready, 1)
                v.drain().then_inc(hid_ready, 2)
                for k in range(4):
                    lo(k, 0, range(NP))
                rows_lo(0)
                for k in range(4, SPLIT - LAG):
                    lo(k, 0, range(NP))
                with v.Fori(0, NE - 1) as e:
                    expert(e, False)
                expert(NE - 1, True)

        xf = at(A_, NTT, D)
        gf = at(D_ + 4 * D, D)
        jf = at(D_ + 5 * D, D)
        xf_in = [sem(f"xf_in{b}") for b in range(NTT // 2)]
        rmsf = sem("rmsf")
        yf_ready = sem("yf_ready")
        out_stored = sem("out_stored")

        with nc.Block() as block:
            @block.sync
            def _(sp):
                for b in range(NTT // 2):
                    sp.dma_start(xf[:, 2 * b:2 * b + 2], resid[2 * b * P:(2 * b + 2) * P, :]
                                 .rearrange("(t p) n -> p t n", p=P)).then_inc(xf_in[b], 16)
                    if b == 0:
                        sp.dma_start(gf, gains[2:3, :].partition_broadcast(P)).then_inc(xf_in[0], 16)
                for t in range(NTT):
                    sp.wait_ge(yf_ready, t + 1)
                    sp.dma_start(out[t * P:(t + 1) * P, :], xf[:, t]).then_inc(out_stored, 16)
                sp.wait_ge(out_stored, 16 * NTT)

            @block.scalar
            def _(act):
                for t in range(NTT):
                    act.wait_ge(xf_in[t // 2], 32 if t < 2 else 16)
                    act.activation(jf, xf[:, t], ACT.Square, accum_out=small[:, t:t + 1])
                    act.drain()
                    act.activation(small[:, 16 + t:17 + t], small[:, t:t + 1], ACT.Sqrt,
                                   bias=cst[:, 0:1], scale=1.0 / D).then_inc(rmsf, 1)

            @block.vector
            def _(v):
                v.wait_ge(xf_in[0], 32)
                for t in range(NTT):
                    v.wait_ge(rmsf, t + 1)
                    v.reciprocal(small[:, 32 + t:33 + t], small[:, 16 + t:17 + t])
                    v.drain()
                    v.scalar_tensor_tensor(xf[:, t], xf[:, t], small[:, 32 + t:33 + t], gf,
                                           ALU.mult, ALU.mult).then_inc(yf_ready, 1)


def masks():
    row, col = np.arange(P)[:, None], np.arange(P)[None, :]
    block = row // C == col // C
    cols = [row == col, block]
    for d in range(2):
        before = row < col if d == 0 else row > col
        cols += [block & before, block & (before | (row == col))]
    for d in range(2):
        for m in LEVELS:
            same = row // (2 * m) == col // (2 * m)
            first, second = (row, col) if d == 0 else (col, row)
            cols.append(same & (first % (2 * m) < m) & (second % (2 * m) >= m))
    return np.concatenate([c.astype(np.float32) for c in cols], axis=1)


def kernel(**inputs):
    import concourse.bacc as bacc
    from concourse.bass_utils import run_bass_kernel_spmd

    x = {k: np.asarray(v) for k, v in inputs.items()}

    def tiles(a, n):
        a = a.reshape(-1, a.shape[-1])
        full = np.zeros((a.shape[0], n * P), np.float32)
        full[:, :a.shape[1]] = a
        return full.reshape(-1, P).T

    par = np.concatenate([tiles(x["shift_mu"][0], ZT)] + [tiles(x[k][0], RT) for k in ("w0", "a0")]
                         + [tiles(x[k][0].reshape(1, RW), RT) for k in ("k_k", "k_a", "r_k", "lnx_w", "lnx_b")], axis=1)
    dist = np.abs(np.arange(P)[:, None] - (np.arange(BIAS_W)[None, :] - (T0 - P))).astype(np.float32)
    arrays = {
        "tokens": np.concatenate([x["x_prompt"][0], x["x_sample"][0]], axis=0),
        "gains": np.stack([x["norm1_g"][0], x["norm2_g"][0], x["final_g"]]),
        "sub_g": x["subln_g"].reshape(1, P),
        "w_in": x["w_in"][0],
        "lam_qk": x["lambda_qk"].reshape(1, 256),
        "par": par,
        "w2": x["w2"][0], "a2": x["a2"][0], "g2": x["g2"][0],
        "w_out": x["w_out"][0], "w_router": x["w_router"][0],
        "w_gate": x["w_gate"][0], "w_up": x["w_up"][0], "w_down": x["w_down"][0],
        "c_bias": -dist,
        "c_mask": masks(),
    }
    arrays = {k: np.ascontiguousarray(v) for k, v in arrays.items()}
    nc = bacc.Bacc("TRN2", target_bir_lowering=False, num_devices=1)
    aps = [nc.dram_tensor(k, v.shape, mybir.dt.from_np(v.dtype), kind="ExternalInput").ap()
           for k, v in arrays.items()]
    out = nc.dram_tensor("out", (NT, D), mybir.dt.float32, kind="ExternalOutput").ap()
    build(nc, *aps, out)
    r = run_bass_kernel_spmd(nc, [arrays], core_ids=[0])
    y = r.results[0]["out"]
    return y[:T0].reshape(1, T0, D), y[T0:].reshape(1, T1, D)
```
